# Optimizing a Trainium2 kernel written in Bass

```python
import jax, jax.numpy as jnp
from jax import lax
import numpy as np

D_MODEL = 2048
BATCH = 1
SEQ = 256
DEPTH = 2

MEM_LEN = 256
HEAD_DIM = 128
RET_HEADS = 4
RET_WIDTH = RET_HEADS * HEAD_DIM
RET_CHUNK = 128
MLA_HEADS = 4
MLA_NOPE = 128
MLA_ROPE = 64
MLA_V = 128
MLA_Q_RANK = 384
MLA_KV_RANK = 128
MLA_WIDTH = MLA_HEADS * MLA_V
ATTN_BLOCK = 128
MLSTM_HEADS = 4
MLSTM_WIDTH = MLSTM_HEADS * HEAD_DIM
MLSTM_CHUNK = 128
CONV_WIDTH = 4
MEM_HEADS = 4
MEM_WIDTH = MEM_HEADS * HEAD_DIM
MIX_WIDTH = RET_WIDTH + MLA_WIDTH + MLSTM_WIDTH + MEM_WIDTH

ROPE_THETA = 10000.0
LN_EPS = 1e-5
RMS_EPS = 1e-6
DEEPNORM_ALPHA = (2 * DEPTH) ** 0.25
DEEPNORM_BETA = (8 * DEPTH) ** -0.25

IN_SPLITS = (RET_WIDTH, RET_WIDTH, RET_WIDTH,
             MLA_Q_RANK, MLA_KV_RANK, MLA_ROPE,
             MLSTM_WIDTH, MLSTM_WIDTH, MLSTM_WIDTH,
             MLSTM_HEADS, MLSTM_HEADS,
             MEM_WIDTH,
             MIX_WIDTH)
IN_WIDTH = sum(IN_SPLITS)

kernel_name = "hymba_ret_mla_mlstm_deepnorm"

def _split_cols(h, sizes):
    idx = np.cumsum(sizes)[:-1].tolist()
    return jnp.split(h, idx, axis=-1)

def _heads(t, n):
    b, s, _ = t.shape
    return t.reshape(b, s, n, -1).transpose(0, 2, 1, 3)

def _merge(t):
    b, n, s, d = t.shape
    return t.transpose(0, 2, 1, 3).reshape(b, s, n * d)

def _to_chunks(t, size):
    b, h, s = t.shape[:3]
    t = t.reshape(b, h, s // size, size, *t.shape[3:])
    return jnp.moveaxis(t, 2, 0)

def _from_chunks(t):
    n, b, h, size = t.shape[:4]
    return jnp.moveaxis(t, 0, 2).reshape(b, h, n * size, *t.shape[4:])

def _layernorm(x, g, b):
    xf = x.astype(jnp.float32)
    mu = xf.mean(-1, keepdims=True)
    var = jnp.mean(jnp.square(xf - mu), -1, keepdims=True)
    y = (xf - mu) * lax.rsqrt(var + LN_EPS) * g.astype(jnp.float32) + b.astype(jnp.float32)
    return y.astype(x.dtype)

def _rmsnorm(x, g):
    xf = x.astype(jnp.float32)
    y = xf * lax.rsqrt(jnp.mean(jnp.square(xf), -1, keepdims=True) + RMS_EPS) * g.astype(jnp.float32)
    return y.astype(x.dtype)

def _head_norm(h, g):
    n, d = h.shape[1], h.shape[3]
    mu = h.mean(-1, keepdims=True)
    var = jnp.mean(jnp.square(h - mu), -1, keepdims=True)
    return (h - mu) * lax.rsqrt(var + LN_EPS) * g.astype(jnp.float32).reshape(n, 1, d)

def _rope(t, positions):
    half = t.shape[-1] // 2
    freqs = ROPE_THETA ** (-jnp.arange(half, dtype=jnp.float32) / half)
    ang = positions.astype(jnp.float32)[:, None, :, None] * freqs
    cos, sin = jnp.cos(ang), jnp.sin(ang)
    tf = t.astype(jnp.float32)
    t1, t2 = tf[..., :half], tf[..., half:]
    return jnp.concatenate([t1 * cos - t2 * sin, t2 * cos + t1 * sin], -1).astype(t.dtype)

def _retention(q, k, v, positions):
    b, n, s, d = q.shape
    q = _rope(q, positions)
    k = _rope(k, positions) * d ** -0.5
    log_g = jnp.log1p(-jnp.exp2(-5.0 - jnp.arange(n, dtype=jnp.float32)))
    size = RET_CHUNK
    idx = jnp.arange(size, dtype=jnp.float32)
    rel = idx[:, None] - idx[None, :]
    decay_in = jnp.where(rel >= 0, jnp.exp(log_g[:, None, None] * jnp.maximum(rel, 0.0)), 0.0)
    decay_q = jnp.exp(log_g[:, None] * (idx + 1.0))[..., None]
    decay_k = jnp.exp(log_g[:, None] * (size - 1.0 - idx))[..., None]
    decay_chunk = jnp.exp(log_g * size)[:, None, None]

    def step(state, inp):
        qc, kc, vc = inp
        sc = jnp.einsum('bhqd,bhkd->bhqk', qc, kc) * decay_in
        out = jnp.einsum('bhqk,bhkd->bhqd', sc, vc) + jnp.einsum('bhqd,bhde->bhqe', qc, state) * decay_q
        state = decay_chunk * state + jnp.einsum('bhkd,bhke->bhde', kc * decay_k, vc)
        return state, out

    state0 = jnp.zeros((b, n, d, v.shape[-1]), jnp.float32)
    _, out = lax.scan(step, state0, (_to_chunks(q, size), _to_chunks(k, size), _to_chunks(v, size)))
    return _from_chunks(out)

def _causal_attention(q, k, v):
    b, n, s, d = q.shape
    nb = s // ATTN_BLOCK
    qb = jnp.moveaxis(q.reshape(b, n, nb, ATTN_BLOCK, d), 2, 0)
    kpos = jnp.arange(s)

    def one_block(args):
        qblk, bi = args
        sc = jnp.einsum('bhqd,bhkd->bhqk', qblk, k).astype(jnp.float32)
        qpos = bi * ATTN_BLOCK + jnp.arange(ATTN_BLOCK)
        sc = jnp.where(kpos[None, :] <= qpos[:, None], sc, -jnp.inf)
        p = jax.nn.softmax(sc, axis=-1).astype(v.dtype)
        return jnp.einsum('bhqk,bhkd->bhqd', p, v)

    out = lax.map(one_block, (qb, jnp.arange(nb)))
    return _from_chunks(out)

def _mla(c_q, c_kv, k_pe, q_norm_g, w_uq, kv_norm_g, w_ukv, positions):
    b, s, _ = c_q.shape
    q = (_rmsnorm(c_q, q_norm_g) @ w_uq).reshape(b, s, MLA_HEADS, MLA_NOPE + MLA_ROPE).transpose(0, 2, 1, 3)
    q = jnp.concatenate([q[..., :MLA_NOPE], _rope(q[..., MLA_NOPE:], positions)], -1)
    kv = (_rmsnorm(c_kv, kv_norm_g) @ w_ukv).reshape(b, s, MLA_HEADS, MLA_NOPE + MLA_V).transpose(0, 2, 1, 3)
    k_rot = _rope(k_pe[:, None], positions)
    k = jnp.concatenate([kv[..., :MLA_NOPE], jnp.broadcast_to(k_rot, (b, MLA_HEADS, s, MLA_ROPE))], -1)
    v = kv[..., MLA_NOPE:]
    return _causal_attention(q * (MLA_NOPE + MLA_ROPE) ** -0.5, k, v)

def _causal_conv(t, w, bias):
    kw, c = w.shape
    tp = jnp.pad(t, ((0, 0), (kw - 1, 0), (0, 0)))
    y = lax.conv_general_dilated(tp, w[:, None, :], window_strides=(1,), padding='VALID',
                                 dimension_numbers=('NWC', 'WIO', 'NWC'), feature_group_count=c)
    return y + bias

def _mlstm(q, k, v, i_pre, f_pre):
    b, n, s, d = q.shape
    size = MLSTM_CHUNK
    k = k * d ** -0.5
    log_f = jax.nn.log_sigmoid(f_pre)
    causal = jnp.tril(jnp.ones((size, size), bool))

    def step(carry, inp):
        c_st, n_st, m_st = carry
        qc, kc, vc, ic, fc = inp
        cum = jnp.cumsum(fc, -1)
        log_d = jnp.where(causal, cum[..., :, None] - cum[..., None, :] + ic[..., None, :], -jnp.inf)
        inter = cum + m_st[..., None]
        m_t = jnp.maximum(inter, log_d.max(-1))
        sc = jnp.einsum('bhqd,bhkd->bhqk', qc, kc) * jnp.exp(log_d - m_t[..., None])
        w_inter = jnp.exp(inter - m_t)
        num = jnp.einsum('bhqk,bhkd->bhqd', sc, vc) + w_inter[..., None] * jnp.einsum('bhqd,bhde->bhqe', qc, c_st)
        den = sc.sum(-1) + w_inter * jnp.einsum('bhqd,bhd->bhq', qc, n_st)
        h = num / jnp.maximum(jnp.abs(den), jnp.exp(-m_t))[..., None]
        cum_last = cum[..., -1]
        log_wk = cum_last[..., None] - cum + ic
        m_new = jnp.maximum(cum_last + m_st, log_wk.max(-1))
        wk = jnp.exp(log_wk - m_new[..., None])
        decay = jnp.exp(cum_last + m_st - m_new)
        c_st = decay[..., None, None] * c_st + jnp.einsum('bhkd,bhke->bhde', kc * wk[..., None], vc)
        n_st = decay[..., None] * n_st + jnp.einsum('bhkd,bhk->bhd', kc, wk)
        return (c_st, n_st, m_new), h

    carry0 = (jnp.zeros((b, n, d, v.shape[-1]), jnp.float32), jnp.zeros((b, n, d), jnp.float32),
              jnp.zeros((b, n), jnp.float32))
    _, h = lax.scan(step, carry0, (_to_chunks(q, size), _to_chunks(k, size), _to_chunks(v, size),
                                   _to_chunks(i_pre, size), _to_chunks(log_f, size)))
    return _from_chunks(h)

def _mem_attention(q, mem, w_mem_kv):
    k, v = jnp.split(mem @ w_mem_kv, 2, axis=-1)
    qh = _heads(q, MEM_HEADS) * HEAD_DIM ** -0.5
    kh, vh = _heads(k, MEM_HEADS), _heads(v, MEM_HEADS)
    sc = jnp.einsum('bhqd,bhkd->bhqk', qh, kh).astype(jnp.float32)
    p = jax.nn.softmax(sc, axis=-1).astype(vh.dtype)
    return jnp.einsum('bhqk,bhkd->bhqd', p, vh)

def _layer(x, mem, positions, w_in, ret_norm_g, mla_q_norm_g, mla_w_uq, mla_kv_norm_g, mla_w_ukv,
           ml_conv_w, ml_conv_b, ml_w_q, ml_w_k, ml_i_bias, ml_f_bias, ml_skip, ml_norm_g,
           w_mem_kv, w_out, ln_g, ln_b):
    f32 = jnp.float32
    b, s, _ = x.shape
    (r_q, r_k, r_v, a_cq, a_ckv, a_kpe, l_x, l_v, l_o, l_i, l_f, c_q, z) = _split_cols(x @ w_in, IN_SPLITS)

    ret = _retention(_heads(r_q, RET_HEADS).astype(f32), _heads(r_k, RET_HEADS).astype(f32),
                     _heads(r_v, RET_HEADS).astype(f32), positions)
    ret = _merge(_head_norm(ret, ret_norm_g))

    mla = _merge(_mla(a_cq, a_ckv, a_kpe, mla_q_norm_g, mla_w_uq, mla_kv_norm_g, mla_w_ukv,
                      positions)).astype(f32)

    xc = jax.nn.silu(_causal_conv(l_x, ml_conv_w, ml_conv_b))
    xc_h = xc.reshape(b, s, MLSTM_HEADS, HEAD_DIM)
    lq = jnp.einsum('bshd,hde->bhse', xc_h, ml_w_q).astype(f32)
    lk = jnp.einsum('bshd,hde->bhse', xc_h, ml_w_k).astype(f32)
    lv = _heads(l_v, MLSTM_HEADS).astype(f32)
    i_pre = jnp.swapaxes(l_i + ml_i_bias, 1, 2).astype(f32)
    f_pre = jnp.swapaxes(l_f + ml_f_bias, 1, 2).astype(f32)
    cell = _mlstm(lq, lk, lv, i_pre, f_pre) * jax.nn.sigmoid(_heads(l_o, MLSTM_HEADS).astype(f32))
    mls = _merge(_head_norm(cell, ml_norm_g)) + ml_skip.astype(f32) * xc.astype(f32)

    memo = _merge(_mem_attention(c_q, mem, w_mem_kv)).astype(f32)

    y = jnp.concatenate([ret, mla, mls, memo], axis=-1) * jax.nn.silu(z.astype(f32))
    y = y.astype(x.dtype) @ w_out
    return _layernorm(DEEPNORM_ALPHA * x + y, ln_g, ln_b)

def setup_inputs(seed: int = 0) -> dict:
    key = jax.random.key(seed)
    ks = jax.random.split(key, 24)
    f32 = jnp.float32

    def nrm(k, shape, std):
        return jax.random.normal(k, shape, f32) * std

    def gain(k, shape):
        return 1.0 + 0.02 * jax.random.normal(k, shape, f32)

    L = DEPTH
    return {
        "x": nrm(ks[0], (BATCH, SEQ, D_MODEL), 1.0),
        "mem": nrm(ks[1], (BATCH, MEM_LEN, D_MODEL), 1.0),
        "positions": jnp.tile(jnp.arange(SEQ, dtype=jnp.int32)[None, :], (BATCH, 1)),
        "w_in": nrm(ks[2], (L, D_MODEL, IN_WIDTH), D_MODEL ** -0.5),
        "ret_norm_g": gain(ks[3], (L, RET_WIDTH)),
        "mla_q_norm_g": gain(ks[4], (L, MLA_Q_RANK)),
        "mla_w_uq": nrm(ks[5], (L, MLA_Q_RANK, MLA_HEADS * (MLA_NOPE + MLA_ROPE)), MLA_Q_RANK ** -0.5),
        "mla_kv_norm_g": gain(ks[6], (L, MLA_KV_RANK)),
        "mla_w_ukv": nrm(ks[7], (L, MLA_KV_RANK, MLA_HEADS * (MLA_NOPE + MLA_V)), MLA_KV_RANK ** -0.5),
        "ml_conv_w": nrm(ks[8], (L, CONV_WIDTH, MLSTM_WIDTH), CONV_WIDTH ** -0.5),
        "ml_conv_b": nrm(ks[9], (L, MLSTM_WIDTH), 0.02),
        "ml_w_q": nrm(ks[10], (L, MLSTM_HEADS, HEAD_DIM, HEAD_DIM), HEAD_DIM ** -0.5),
        "ml_w_k": nrm(ks[11], (L, MLSTM_HEADS, HEAD_DIM, HEAD_DIM), HEAD_DIM ** -0.5),
        "ml_i_bias": nrm(ks[12], (L, MLSTM_HEADS), 0.1),
        "ml_f_bias": jnp.linspace(3.0, 6.0, MLSTM_HEADS, dtype=f32)[None, :] + nrm(ks[13], (L, MLSTM_HEADS), 0.1),
        "ml_skip": gain(ks[14], (L, MLSTM_WIDTH)),
        "ml_norm_g": gain(ks[15], (L, MLSTM_WIDTH)),
        "w_mem_kv": nrm(ks[16], (L, D_MODEL, 2 * MEM_WIDTH), D_MODEL ** -0.5),
        "w_out": nrm(ks[17], (L, MIX_WIDTH, D_MODEL), DEEPNORM_BETA * MIX_WIDTH ** -0.5),
        "ln_g": gain(ks[18], (L, D_MODEL)),
        "ln_b": nrm(ks[19], (L, D_MODEL), 0.02),
    }

def reference(x, mem, positions, w_in, ret_norm_g, mla_q_norm_g, mla_w_uq, mla_kv_norm_g, mla_w_ukv,
              ml_conv_w, ml_conv_b, ml_w_q, ml_w_k, ml_i_bias, ml_f_bias, ml_skip, ml_norm_g,
              w_mem_kv, w_out, ln_g, ln_b):
    for l in range(DEPTH):
        x = _layer(x, mem, positions, w_in[l], ret_norm_g[l], mla_q_norm_g[l], mla_w_uq[l],
                   mla_kv_norm_g[l], mla_w_ukv[l], ml_conv_w[l], ml_conv_b[l], ml_w_q[l], ml_w_k[l],
                   ml_i_bias[l], ml_f_bias[l], ml_skip[l], ml_norm_g[l], w_mem_kv[l], w_out[l],
                   ln_g[l], ln_b[l])
    return x


_drawn_inputs = setup_inputs


def setup_inputs(seed=0):
    import zlib

    import numpy as np

    out = dict(_drawn_inputs(seed))
    spreads = {}
    factors = {'mem': 3.695,
     'ret_norm_g': 8.0,
     'mla_q_norm_g': 8.0,
     'mla_kv_norm_g': 8.0,
     'ml_conv_b': 8.0,
     'ml_i_bias': 64.0,
     'ml_skip': 23.343,
     'ml_norm_g': 8.0,
     'w_mem_kv': 3.553}
    for name, (base, spread) in spreads.items():
        noise = np.random.default_rng([zlib.crc32(name.encode()), seed]).standard_normal(out[name].shape)
        drawn = base * np.exp(spread * noise) if base else spread * noise
        out[name] = __import__('jax').numpy.asarray(drawn.astype(out[name].dtype))
    for name, factor in factors.items():
        out[name] = (out[name] * factor).astype(out[name].dtype)
    return out
```

```python
from contextlib import ExitStack

import numpy as np

import concourse.bass as bass
from concourse import mybir

F32 = mybir.dt.float32
F32R = mybir.dt.float32r
I32 = mybir.dt.int32
ALU = mybir.AluOpType
ACT = mybir.ActivationFunctionType
AX = mybir.AxisListType

P = 128
DEPTH = 2
D_MODEL = 2048
SEQ = 256
MEM_LEN = 256
HEADS = 4
HD = 128
NOPE, ROT = 128, 64
QRANK, KVRANK = 384, 128
TAPS = 4
NT = SEQ // P
KT = D_MODEL // P
GROUPS = 4
W = HEADS * HD
THETA = 10000.0
LN_EPS, RMS_EPS = 1e-5, 1e-6
ALPHA = (2 * DEPTH) ** 0.25
MLA_SCALE = float(NOPE + ROT) ** -0.5
HEAD_SCALE = float(HD) ** -0.5
PAD = TAPS - 1
TRI = 3 * P
MASKED = 1e30

_sizes = (W, W, W, QRANK, KVRANK, ROT, W, W, W, HEADS, HEADS, W, GROUPS * W)
_names = ("rq", "rk", "rv", "aq", "akv", "ape", "lx", "lv", "lo", "li", "lf", "cq", "z")
COL = dict(zip(_names, np.concatenate([[0], np.cumsum(_sizes)[:-1]]).tolist()))

AKV_W = KVRANK + ROT + 2 * HEADS
CHUNKS = [("memk", W, "feat"), ("memv", W, "tok"), ("cq", W, "feat"), ("lx", W, "feat"),
          ("akv", AKV_W, "tok"), ("aq", QRANK, "tok"), ("lv", W, "tok"), ("lo", W, "tok"),
          ("rq", W, "tok"), ("rk", W, "tok"), ("rv", W, "tok"),
          ("z3", W, "feat"), ("z2", W, "feat"), ("z1", W, "feat"), ("z0", W, "feat"),
          ("out0", 512, "tok"), ("out1", 512, "tok"), ("out2", 512, "tok"),
          ("out3", 256, "tok"), ("out4", 256, "tok")]
NCH = len(CHUNKS)
CI = {c[0]: i for i, c in enumerate(CHUNKS)}
OUT0 = CI["out0"]
OUTCOL = [0, 512, 1024, 1536, 1792]
NOUT = len(OUTCOL)
OUT_ORDER = [12, 13, 14, 15, 8, 9, 10, 11, 4, 5, 6, 7, 0, 1, 2, 3]
SLOTS = NCH * KT
PAIRS = SLOTS // 2
RAW = 5
RING = 5
LAYER_WORDS = sum(KT * P * w for _, w, _ in CHUNKS)
CHUNK_AT = np.concatenate([[0], np.cumsum([KT * P * w for _, w, _ in CHUNKS])]).tolist()

C_RETG, C_CG, C_CONVW, C_CONVB, C_SKIP, C_MLG, C_IB, C_FB = 0, 4, 8, 24, 28, 32, 36, 37
NCOLS = 38
K_ID, K_DECAY = 0, P
K_TRI = K_DECAY + HEADS * TRI
K_BIG = K_TRI + TRI
K_FREQ = K_BIG + TRI
FR, FM = HD // 2, ROT // 2
NCONST = K_FREQ + FR + FM

PE_AT = {}


def _put(table, slot, *step):
    table.setdefault(slot, []).append(step)


for _j in range(8):
    _put(PE_AT, 16 + 2 * _j, "xT", _j)
for _h in range(HEADS):
    _put(PE_AT, 56 + 6 * _h, "mem_scores", _h)
    _put(PE_AT, 65 + 6 * _h, "mem_pT", _h)
    _put(PE_AT, 153 + 6 * _h, "mla_scores", _h)
    _put(PE_AT, 162 + 6 * _h, "mla_pT", _h)
for _s, *_step in [
        (77, "mem_out", 0), (89, "mem_out", 1),
        (83, "ml_q", 0), (85, "ml_q", 1), (87, "ml_k", 0), (89, "ml_k", 1),
        (90, "gateT", 0), (104, "gate_cols", 0), (106, "m_rows", 0), (114, "m_rows", 1),
        (105, "cT", 0), (107, "cT", 1), (108, "kpeT", 0),
        (110, "ml_scores", 0), (112, "ml_scores", 1), (119, "ml_scores", 2), (121, "ml_scores", 3),
        (119, "ml_out", 0), (121, "ml_out", 1), (127, "ml_out", 2), (129, "ml_out", 3),
        (131, "mla_qr", 0), (132, "mla_qr", 1), (133, "mla_kn", 0), (135, "mla_kn", 1),
        (136, "mla_qn", 0), (138, "mla_qn", 1), (140, "mla_v", 0), (142, "mla_v", 1), (143, "qrT", 0),
        (150, "cellT", 0), (151, "cellT", 1),
        (154, "rqT", 0), (155, "rqT", 1), (170, "rkT", 0), (172, "rkT", 1),
        (174, "mla_out", 0), (186, "mla_out", 1),
        (188, "ret_scores", 0), (190, "ret_scores", 1), (198, "ret_scores", 2), (200, "ret_scores", 3),
        (197, "ret_out", 0), (207, "ret_out", 1), (209, "retT", 0), (219, "retT", 1)]:
    _put(PE_AT, _s, *_step)
JOBS = [step for slot in sorted(PE_AT) for step in PE_AT[slot]]
NJOBS = len(JOBS)
NBANK = 4
JOB = {step: j for j, step in enumerate(JOBS)}

ACT_AT = {}
for _j in range(8):
    _put(ACT_AT, 1 + 2 * _j, "normalise", _j)
    _put(ACT_AT, 21 + 2 * _j, "x_hi", _j)
for _h in range(HEADS):
    _put(ACT_AT, 61 + 6 * _h, "mem_exp", _h)
    _put(ACT_AT, 70 + 6 * _h, "mem_pT", _h)
    _put(ACT_AT, 158 + 6 * _h, "mla_exp", _h)
    _put(ACT_AT, 167 + 6 * _h, "mla_pT", _h)
for _s, *_step in [
        (20, "memk", 0), (22, "memk", 1), (52, "cq", 0), (53, "cq", 1), (68, "lx", 0), (69, "lx", 1),
        (81, "silu_conv", 0), (82, "silu_conv", 1), (84, "akv", 0), (85, "akv", 1),
        (88, "ml_q", 0), (90, "ml_q", 1), (92, "ml_k", 0), (94, "ml_k", 1),
        (96, "softplus", 0), (99, "gate_floor", 0), (100, "aq", 0), (101, "aq", 1),
        (111, "ml_decay", 0), (112, "ml_decay", 1), (113, "kpeT", 0), (119, "ml_decay", 2), (120, "ml_decay", 3),
        (116, "lv", 0), (117, "lv", 1), (132, "lo", 0), (133, "lo", 1),
        (138, "mla_kn", 0), (140, "mla_kn", 1), (141, "mla_qn", 0), (143, "mla_qn", 1),
        (145, "mla_v", 0), (147, "mla_v", 1), (149, "qrT", 0),
        (160, "rqT", 0), (161, "rqT", 1), (176, "rkT", 0), (178, "rkT", 1),
        (180, "rv", 0), (181, "rv", 1),
        (196, "silu", 3, 0), (197, "silu", 3, 1), (212, "silu", 2, 0), (213, "silu", 2, 1),
        (228, "silu", 1, 0), (229, "silu", 1, 1), (245, "silu", 0, 0), (245, "silu", 0, 1),
        (244, "y_hi", 0), (244, "y_hi", 1), (246, "y_hi", 2), (247, "y_hi", 3),
        (249, "y_hi", 4), (250, "y_hi", 5), (254, "y_hi", 6), (255, "y_hi", 7)]:
    _put(ACT_AT, _s, *_step)

DVE_AT = {}
for _j in range(8):
    _put(DVE_AT, 21 + 2 * _j, "x_lo", _j)
    _put(DVE_AT, 70 + _j, "conv", _j)
for _h in range(HEADS):
    _put(DVE_AT, 61 + 6 * _h, "mem_max", _h)
    _put(DVE_AT, 63 + 6 * _h, "mem_norm", _h)
    _put(DVE_AT, 158 + 6 * _h, "mla_max", _h)
    _put(DVE_AT, 160 + 6 * _h, "mla_norm", _h)
for _s, *_step in [
        (36, "memv", 0), (38, "memv", 1), (83, "mem_out", 0), (94, "mem_out", 1),
        (86, "rms", 0), (88, "ckv", 0), (89, "kpe_rope", 0),
        (95, "gates", 0), (97, "gate_scan", 0), (98, "skip", 0), (100, "ones", 0),
        (102, "rms", 1), (103, "cqn", 0), (104, "cqn", 1), (110, "cT", 0), (113, "cT", 1), (109, "gate_cols", 0),
        (111, "ml_gap", 0), (112, "ml_gap", 1), (119, "ml_gap", 2), (120, "ml_gap", 3),
        (115, "ml_weigh", 0), (117, "ml_weigh", 1), (124, "ml_weigh", 2), (126, "ml_weigh", 3),
        (127, "ml_out", 0), (128, "ml_out", 1), (132, "ml_out", 2), (134, "ml_out", 3),
        (136, "cell_gate", 0), (137, "cell_gate", 1), (139, "cell_stats", 0), (140, "cell_stats", 1),
        (142, "cell_norm", 0), (144, "cell_norm", 1),
        (137, "q_rope", 0), (138, "q_rope", 1),
        (156, "cellT", 0), (157, "cellT", 1),
        (148, "rope_rq", 0), (150, "rope_rq", 1), (165, "rope_rk", 0), (167, "rope_rk", 1),
        (179, "mla_out", 0), (191, "mla_out", 1),
        (193, "ret_weigh", 0), (195, "ret_weigh", 1), (203, "ret_weigh", 2), (205, "ret_weigh", 3),
        (202, "ret_stats", 0), (204, "ret_norm", 0), (212, "ret_stats", 1), (214, "ret_norm", 1),
        (216, "retT", 0), (224, "retT", 1),
        (198, "gate", 3, 0), (199, "gate", 3, 1), (215, "gate", 2, 0), (216, "gate", 2, 1),
        (230, "gate", 1, 0), (231, "gate", 1, 1), (247, "gate", 0, 0), (248, "gate", 0, 1),
        (244, "y_lo", 0), (244, "y_lo", 1), (246, "y_lo", 2), (247, "y_lo", 3),
        (249, "y_lo", 4), (250, "y_lo", 5), (254, "y_lo", 6), (255, "y_lo", 7)]:
    _put(DVE_AT, _s, *_step)
for _c in range(NOUT - 1):
    _put(DVE_AT, (OUT0 + _c + 1) * KT + 4, "residual", _c)

DVE_LINKS, ACT_LINKS = 64, 3
DVE_LINKS_BEFORE = 18


def pair_at(m):
    c, j = divmod(m, KT // 2)
    w = CHUNKS[c][1]
    return CHUNK_AT[c] + j * 2 * P * w, w


def two_pi_parts():
    first = 6.28125
    second = 253.0 / 2 ** 17
    return first, second, 2.0 * np.pi - first - second


PI_IN = 3.1415925


class Signal:

    def __init__(self, sem, per_layer, before=0, step=1):
        self.sem, self.per_layer, self.before, self.step = sem, per_layer, before, step

    def at(self, layer, i):
        return layer * (self.per_layer * self.step) + (self.before + i + 1) * self.step


def build_trunk(nc, a, out):
    ctx = ExitStack()
    with ctx:
        def sb(name, shape, dt=F32):
            return ctx.enter_context(nc.sbuf_tensor(name, shape, dt))

        def signal(name, per_layer, before=0, step=1):
            return Signal(ctx.enter_context(nc.semaphore(name)), per_layer, before, step)

        X = sb("X", [P, NT, D_MODEL])
        xh, xl = sb("xh", [P, KT, SEQ], F32R), sb("xl", [P, KT, SEQ], F32R)
        mh, ml = sb("mh", [P, KT, MEM_LEN], F32R), sb("ml", [P, KT, MEM_LEN], F32R)
        Y = sb("Y", [P, KT * SEQ])
        raw = sb("raw", [P, RAW, 2 * 512])
        hi, lo = sb("hi", [P, RING, 512], F32R), sb("lo", [P, RING, 512], F32R)
        const = sb("const", [P, NCONST])
        cols = sb("cols", [P, NCOLS])
        B = [sb(f"B{i}", [P, 4 * (SEQ + PAD) + 4]) for i in range(10)]
        qr = sb("qr", [P, NT, HEADS * ROT])
        qrT = sb("qrT", [P, 2, SEQ])
        krr = sb("krr", [P, NT, P])
        krT = sb("krT", [P, SEQ])
        prob = sb("prob", [P, 2, 512])
        probT = sb("probT", [P, 2, 512])
        tmp = sb("tmp", [P, 512])
        cosr, sinr = sb("cosr", [P, NT, FR]), sb("sinr", [P, NT, 2, FR])
        cosm, sinm = sb("cosm", [P, NT, FM]), sb("sinm", [P, NT, 2, FM])
        small = sb("small", [P, NT, AKV_W - KVRANK])
        gcol = sb("gcol", [P, 4, HEADS])
        nmax, rsum, rinv = sb("nmax", [P, 2, 2]), sb("rsum", [P, 2, 2]), sb("rinv", [P, 2, 2])
        sumsq, rms = sb("sumsq", [P, 2, NT]), sb("rms", [P, 2, NT])
        den = sb("den", [P, 2, NT])
        stats, mv, rstd = sb("stats", [P, 8, 6]), sb("mv", [P, 8, 2]), sb("rstd", [P, 8])
        ln_stats, ln_mv = sb("ln_stats", [P, NT, NOUT, 6]), sb("ln_mv", [P, NT, 2])
        ln_rstd, ln_shift = sb("ln_rstd", [P, NT]), sb("ln_shift", [P, NT])
        half = sb("half", [P, 8])
        pos = sb("pos", [P, NT], I32)

        memT = [B[i][:, 0:4 * SEQ] for i in range(4)]
        mKT, lv1, rqT = (B[0][:, 0:1024].rearrange("p (h t) -> p h t", h=HEADS),
                         B[0][:, 0:NT * HEADS * (HD + 1)].rearrange("p (i h e) -> p i h e", i=NT, h=HEADS),
                         B[0][:, 0:1024].rearrange("p (h t) -> p h t", h=HEADS))
        mV = mlaV = B[1][:, 0:1024].rearrange("p (i w) -> p i w", i=NT)
        cQT = memo = B[2][:, 0:1024].rearrange("p (h t) -> p h t", h=HEADS)
        LX = B[3][:, 0:4 * (SEQ + PAD)].rearrange("p (j t) -> p j t", j=4)
        lkT = rkT = B[3][:, 0:1024].rearrange("p (h t) -> p h t", h=HEADS)
        xcT = mls = B[4][:, 0:1024].rearrange("p (h t) -> p h t", h=HEADS)
        lqT = retT = B[5][:, 0:1024].rearrange("p (h t) -> p h t", h=HEADS)
        cell = B[5][:, 0:1024].rearrange("p (i w) -> p i w", i=NT)
        lw = B[6][:, 0:1024].rearrange("p (q h e) -> p q h e", q=2, h=HEADS)
        row = [B[6][0:HEADS, r * SEQ:(r + 1) * SEQ] for r in range(4)]
        sigo = rv = B[6][:, 0:1024].rearrange("p (i w) -> p i w", i=NT)
        cqn = B[7][:, 0:NT * 512].rearrange("p (i w) -> p i w", i=NT)
        knT = B[7][:, 0:1024].rearrange("p (h t) -> p h t", h=HEADS)
        cT = B[8][:, 0:1024].rearrange("p (j t) -> p j t", j=4)
        qnT = mlao = B[9][:, 0:1024].rearrange("p (h t) -> p h t", h=HEADS)
        gb = Y[:, :].rearrange("p (a n) -> p a n", a=2)
        wukv = Y[:, 0:1024].rearrange("p (h v e) -> p h v e", h=HEADS, v=2)
        wuq = Y[:, 1024:1024 + 3 * HEADS * (NOPE + ROT)].rearrange("p (k h e) -> p k h e", k=3, h=HEADS)
        gap = Y[:, 4096 - 2 * TRI:4096].rearrange("p (b c) -> p b c", b=2)
        rqt = Y[:, 1024:2048].rearrange("p (i w) -> p i w", i=NT)
        rkt = Y[:, 2048:3072].rearrange("p (i w) -> p i w", i=NT)
        retn = Y[:, 0:1024].rearrange("p (i w) -> p i w", i=NT)
        yT = Y[:, :].rearrange("p (k t) -> p k t", k=KT)
        junk = tmp

        ident = const[:, K_ID:K_ID + P]
        decay = const[:, K_DECAY:K_DECAY + HEADS * TRI].rearrange("p (h c) -> p h c", h=HEADS)
        tri, big = const[:, K_TRI:K_TRI + TRI], const[:, K_BIG:K_BIG + TRI]
        freq = const[:, K_FREQ:K_FREQ + FR + FM]

        acc = ctx.enter_context(nc.psum_tensor("acc", [P, 2, 2, 512], F32))
        work = ctx.enter_context(nc.psum_tensor("work", [P, NBANK, 512], F32))

        raw_full = [signal(f"raw_full{s}", PAIRS // RAW, step=16) for s in range(RAW)]
        hi_done = signal("hi_done", SLOTS)
        lo_done = signal("lo_done", SLOTS, before=2 * RAW)
        tile_used = signal("tile_used", SLOTS, before=RING)
        acc_read = [signal(f"acc_read{p}", NCH, before=2) for p in range(2)]
        job_done = signal("job_done", NJOBS)
        in_bank = [[j for j in range(NJOBS) if j % NBANK == b] for b in range(NBANK)]
        bank_read = [signal(f"bank_read{b}", len(in_bank[b]), before=1) for b in range(NBANK)]
        memb_in = [signal(f"mem_in{q}", 0, step=16) for q in range(4)]
        const_in = signal("const_in", 0, step=16)
        x_in = signal("x_in", 0, step=16)
        mem_hi, mem_lo = signal("mem_hi", 0), signal("mem_lo", 0)
        angles, tables = signal("angles", 0), signal("tables", 0)
        ready = signal("ready", 0)
        cols_in = signal("cols_in", 1, step=16)
        lw_in = signal("lw_in", 1, step=16)
        mlaw_in = signal("mlaw_in", 2, step=16)
        gb_in = signal("gb_in", 1, before=1, step=16)
        normed = signal("normed", 8)
        x_done = signal("x_done", 8, before=0)
        x_hi = signal("x_hi", 8)
        y_hi, y_lo = signal("y_hi", 8), signal("y_lo", 8)
        conv_done, xc_done = signal("conv_done", 1), signal("xc_done", 2)
        lx_pad = signal("lx_pad", 1)
        sq_done, var_done, rms_done = signal("sq_done", 2), signal("var_done", 2), signal("rms_done", 2)
        c_normed = signal("c_normed", 2)
        kpe_done = signal("kpe_done", 1)
        gate_abs, softplus_done = signal("gate_abs", 1), signal("softplus_done", 1)
        scan_done, floor_done = signal("scan_done", 1), signal("floor_done", 1)
        skip_done, ones_done = signal("skip_done", 1), signal("ones_done", 1)
        gap_done, decay_done = signal("gap_done", 4), signal("decay_done", 4)
        max_done, exp_done, prob_done = signal("max_done", 8), signal("exp_done", 4), signal("prob_done", 8)
        qr_done = signal("qr_done", 2)
        cell_var, cell_pow, cell_done = signal("cell_var", 1), signal("cell_pow", 1), signal("cell_done", 1)
        ret_var, ret_pow = signal("ret_var", 2), signal("ret_pow", 2)
        ln_var, ln_pow, ln_done = signal("ln_var", 1), signal("ln_pow", 1), signal("ln_done", 1, before=1)
        gated = signal("gated", 8)
        roped = signal("roped", 4)
        pool_mul = signal("pool_mul", 8)
        alone = signal("alone", 0)
        final_scaled, final_done, stored = signal("final_scaled", 0), signal("final_done", 0), signal("stored", 0, step=16)
        final_normed = signal("final_normed", 0)
        dve_own = signal("dve_own", DVE_LINKS, before=DVE_LINKS_BEFORE)
        act_own = signal("act_own", ACT_LINKS)

        def angle_views():
            n = NT * (FR + FM)
            v = [B[4][:, i * n:(i + 1) * n].rearrange("p (i f) -> p i f", i=NT) for i in range(4)]
            return dict(zip(("raw", "sin", "cos", "turns"), v))

        def stand_alone(eng):
            eng.sem_inc(alone.sem, 1)

        def bank_of(job):
            j = JOB[job]
            return j % NBANK, j // NBANK

        def bank(job):
            return work[:, bank_of(job)[0], :]

        def wait_job(eng, l, *jobs):
            eng.wait_ge(job_done.sem, job_done.at(l, max(JOB[job] for job in jobs)))

        def wait_read(eng, l, *jobs):
            last = {}
            for job in jobs:
                b, u = bank_of(job)
                last[b] = max(u, last.get(b, 0))
            for b, u in last.items():
                eng.wait_ge(bank_read[b].sem, bank_read[b].at(l, u))

        def free_bank(*job):
            return bank_read[bank_of(job)[0]].sem

        def wait_chunk(eng, l, c):
            eng.wait_ge(tile_used.sem, tile_used.at(l, (c + 1) * KT - 1))

        def wait_acc_read(eng, l, c, halves=2):
            eng.wait_ge(acc_read[c % 2].sem, acc_read[c % 2].at(l, (c // 2) * 2 + halves - 1))

        def acc_sem(name):
            return acc_read[CI[name] % 2].sem

        def A(name, i):
            return acc[:, CI[name] % 2, i, :]

        block = ctx.enter_context(nc.Block())

        @block.sync
        def _(sp):
            for q in range(4):
                sp.dma_start(memT[q], a["mem_t"][:, q * 1024:(q + 1) * 1024]).then_inc(memb_in[q].sem, 16)
            with sp.Fori(0, DEPTH) as l:
                for m in range(PAIRS):
                    sp.wait_ge(lo_done.sem, lo_done.at(l, 2 * m + 1 - 2 * RAW))
                    at, w = pair_at(m)
                    sp.dma_start(raw[:, m % RAW, 0:2 * w],
                                 a["w"][bass.ts(l, 1), at:at + 2 * P * w].rearrange("o (p n) -> p (o n)", p=P))\
                      .then_inc(raw_full[m % RAW].sem, 16)
                    if m == 4:
                        sp.dma_start(cols[:, :], a["cols"][bass.ts(l, 1), :].rearrange("o (p n) -> p (o n)", p=P))\
                          .then_inc(cols_in.sem, 16)
                        sp.dma_start(B[6][:, 0:1024], a["lw"][bass.ts(l, 1), :].rearrange("o (p n) -> p (o n)", p=P))\
                          .then_inc(lw_in.sem, 16)
                    if m == 24:
                        sp.wait_ge(x_done.sem, x_done.at(l, 7))
                        sp.dma_start(Y[:, 0:1024], a["wukv"][bass.ts(l, 1), :].rearrange("o (p n) -> p (o n)", p=P))\
                          .then_inc(mlaw_in.sem, 16)
                        sp.dma_start(Y[:, 1024:3328], a["wuq"][bass.ts(l, 1), :].rearrange("o (p n) -> p (o n)", p=P))\
                          .then_inc(mlaw_in.sem, 16)
                    if m == 136:
                        sp.wait_ge(y_lo.sem, y_lo.at(l, 7))
                        sp.dma_start(Y[:, :], a["gb"][bass.ds(l + 1, 1), :].partition_broadcast(P)
                                     .rearrange("p o n -> p (o n)")).then_inc(gb_in.sem, 16)
            for b in range(8):
                cb, i = divmod(b, 2)
                sp.wait_ge(final_done.sem, b + 1)
                sp.dma_start(out[i * P:(i + 1) * P, cb * 512:(cb + 1) * 512],
                             X[:, i, cb * 512:(cb + 1) * 512]).then_inc(stored.sem, 16)
            sp.wait_ge(stored.sem, 8 * 16)

        @block.gpsimd
        def _(pool):
            pool.dma_start(const[:, :], a["const"]).then_inc(const_in.sem, 16)
            pool.dma_start(pos[:, :], a["pos"]).then_inc(const_in.sem, 16)
            pool.wait_ge(ready.sem, 1)

            def root(dst, src, n):
                return pool.tensor_tensor(dst, src, half[:, 0:n], ALU.pow)

            with pool.Fori(0, DEPTH) as l:
                pool.wait_ge(gb_in.sem, gb_in.at(l, -1))
                for b in range(8):
                    cb, i = divmod(b, 2)
                    blk = X[:, i, cb * 512:(cb + 1) * 512]
                    pool.wait_ge(normed.sem, normed.at(l, b))
                    pool.tensor_tensor(blk, blk, gb[:, 0, cb * 512:(cb + 1) * 512], ALU.mult)\
                        .then_inc(pool_mul.sem, 1)
                    pool.wait_ge(pool_mul.sem, pool_mul.at(l, b))
                    pool.tensor_tensor(blk, blk, gb[:, 1, cb * 512:(cb + 1) * 512], ALU.add)\
                        .then_inc(x_done.sem, 1)
                for r in range(2):
                    pool.wait_ge(var_done.sem, var_done.at(l, r))
                    root(rms[:, r, :], sumsq[:, r, :], NT).then_inc(rms_done.sem, 1)
                pool.wait_ge(cell_var.sem, cell_var.at(l, 0))
                root(rstd[:, :], stats[:, :, 0], 8).then_inc(cell_pow.sem, 1)
                for r in range(2):
                    pool.wait_ge(ret_var.sem, ret_var.at(l, r))
                    root(rstd[:, 0:4], stats[:, 0:4, 0], 4).then_inc(ret_pow.sem, 1)
                pool.wait_ge(ln_var.sem, ln_var.at(l, 0))
                root(ln_rstd[:, :], ln_stats[:, :, 0, 0], NT).then_inc(ln_pow.sem, 1)

            for b in range(8):
                cb, i = divmod(b, 2)
                blk = X[:, i, cb * 512:(cb + 1) * 512]
                pool.wait_ge(final_scaled.sem, b + 1)
                pool.tensor_tensor(blk, blk, gb[:, 1, cb * 512:(cb + 1) * 512], ALU.add)\
                    .then_inc(final_done.sem, 1)

        @block.scalar
        def _(act):
            for q in range(4):
                act.wait_ge(memb_in[q].sem, 16)
                act.activation(mh[:, 4 * q:4 * q + 4, :], memT[q].rearrange("p (k t) -> p k t", k=4), ACT.Copy)\
                   .then_inc(mem_hi.sem, 1)
            for i in range(NT):
                act.dma_start(X[:, i, :], a["x"][i * P:(i + 1) * P, :]).then_inc(x_in.sem, 16)
            act.dma_start(Y[:, :], a["gb"][0:1, :].partition_broadcast(P).rearrange("p o n -> p (o n)"))\
               .then_inc(gb_in.sem, 16)
            act.wait_ge(angles.sem, 1)
            ang = angle_views()
            act.activation(ang["sin"], ang["sin"], ACT.Sin).then_inc(tables.sem, 1)
            act.activation(ang["cos"], ang["cos"], ACT.Sin).then_inc(tables.sem, 1)

            with act.Fori(0, DEPTH) as l:
                links = [0]

                def link(ins):
                    ins.then_inc(act_own.sem, 1)
                    links[0] += 1
                    act.wait_ge(act_own.sem, act_own.at(l, links[0] - 1))

                def normalise(b):
                    cb, i = divmod(b, 2)
                    blk = X[:, i, cb * 512:(cb + 1) * 512]
                    if b == 0:
                        act.wait_ge(x_in.sem, 2 * 16)
                        act.wait_ge(ln_done.sem, ln_done.at(l, -1))
                    act.activation(blk, blk, ACT.Identity, scale=ln_rstd[:, i:i + 1], bias=ln_shift[:, i:i + 1])\
                       .then_inc(normed.sem, 1)

                def x_hi_(j):
                    wait_job(act, l, ("xT", j))
                    act.activation(xh[:, 2 * j:2 * j + 2, :], bank(("xT", j)).rearrange("p (k t) -> p k t", k=2),
                                   ACT.Copy).then_inc(x_hi.sem, 1)

                def y_hi_(j):
                    k = OUT_ORDER[2 * j]
                    if j == 0:
                        wait_chunk(act, l, OUT0 - 1)
                    act.wait_ge(gated.sem, gated.at(l, j))
                    act.activation(xh[:, k:k + 2, :], yT[:, k:k + 2, :], ACT.Copy).then_inc(y_hi.sem, 1)

                def feat(name, dst):
                    def evacuate(i):
                        wait_chunk(act, l, CI[name])
                        act.activation(dst[:, 2 * i:2 * i + 2, :], A(name, i).rearrange("p (j t) -> p j t", j=2),
                                       ACT.Copy).then_inc(acc_sem(name), 1)
                    return evacuate

                def lx(i):
                    wait_chunk(act, l, CI["lx"])
                    act.activation(LX[:, 2 * i:2 * i + 2, PAD:PAD + SEQ],
                                   A("lx", i).rearrange("p (j t) -> p j t", j=2), ACT.Copy)\
                       .then_inc(acc_sem("lx"), 1)

                def mem_exp(h):
                    act.wait_ge(max_done.sem, max_done.at(l, h))
                    if h >= 2:
                        wait_job(act, l, ("mem_pT", h - 2))
                    for i in range(NT):
                        e = act.activation(prob[:, h % 2, i * 256:(i + 1) * 256], bank(("mem_scores", h))[:, i * 256:(i + 1) * 256],
                                           ACT.Exp, scale=HEAD_SCALE, bias=nmax[:, h % 2, i:i + 1],
                                           accum_out=rsum[:, h % 2, i:i + 1])
                    e.then_inc(free_bank("mem_scores", h), 1)

                def mem_pT(h):
                    wait_job(act, l, ("mem_pT", h), *([("mem_out", 0)] if h >= 2 else []))
                    act.activation(probT[:, h % 2, :], bank(("mem_pT", h)), ACT.Copy)\
                       .then_inc(free_bank("mem_pT", h), 1)

                def mla_exp(h):
                    act.wait_ge(max_done.sem, max_done.at(l, HEADS + h))
                    for i, (c0, c1) in enumerate(((0, P), (P, TRI))):
                        e = act.activation(prob[:, h % 2, c0:c1], prob[:, h % 2, c0:c1], ACT.Exp, scale=MLA_SCALE,
                                           bias=nmax[:, h % 2, i:i + 1], accum_out=rsum[:, h % 2, i:i + 1])
                    e.then_inc(exp_done.sem, 1)

                def mla_pT(h):
                    wait_job(act, l, ("mla_pT", h), *([("mla_out", 0)] if h >= 2 else []))
                    act.activation(probT[:, h % 2, 0:TRI], bank(("mla_pT", h))[:, 0:TRI], ACT.Copy)\
                       .then_inc(free_bank("mla_pT", h), 1)

                def silu_conv(q):
                    act.wait_ge(conv_done.sem, conv_done.at(l, 0))
                    for j in range(2 * q, 2 * q + 2):
                        s = act.activation(xcT[:, j, :], xcT[:, j, :], ACT.Silu, bias=cols[:, C_CONVB + j:C_CONVB + j + 1])
                    s.then_inc(xc_done.sem, 1)

                def akv(i):
                    wait_chunk(act, l, CI["akv"])
                    if i:
                        act.activation(small[:, i, :], A("akv", i)[:, KVRANK:AKV_W], ACT.Copy)
                        act.activation(junk[:, 0:KVRANK], A("akv", i)[:, 0:KVRANK], ACT.Square,
                                       accum_out=sumsq[:, 0, i:i + 1]).then_inc(sq_done.sem, 1)
                    else:
                        act.activation(small[:, i, :], A("akv", i)[:, KVRANK:AKV_W], ACT.Copy)
                        link(act.activation(junk[:, 0:KVRANK], A("akv", i)[:, 0:KVRANK], ACT.Square,
                                            accum_out=sumsq[:, 0, i:i + 1]))

                def aq(i):
                    wait_chunk(act, l, CI["aq"])
                    s = act.activation(junk[:, 0:QRANK], A("aq", i)[:, 0:QRANK], ACT.Square,
                                       accum_out=sumsq[:, 1, i:i + 1])
                    if i:
                        s.then_inc(sq_done.sem, 1)
                    else:
                        link(s)

                def pair(name, dst):
                    def evacuate(i):
                        wait_job(act, l, (name, i))
                        act.activation(dst[:, 2 * i:2 * i + 2, :], bank((name, i)).rearrange("p (j t) -> p j t", j=2),
                                       ACT.Copy).then_inc(free_bank(name, i), 1)
                    return evacuate

                def softplus(_):
                    act.wait_ge(gate_abs.sem, gate_abs.at(l, 0))
                    link(act.activation(row[2], row[2], ACT.Exp, scale=-1.0))
                    act.activation(row[2], row[2], ACT.Ln, bias=1.0).then_inc(softplus_done.sem, 1)

                def gate_floor(_):
                    act.wait_ge(scan_done.sem, scan_done.at(l, 0))
                    act.activation(row[3], row[3], ACT.Exp, scale=-1.0).then_inc(floor_done.sem, 1)

                def ml_decay(h):
                    act.wait_ge(gap_done.sem, gap_done.at(l, h))
                    act.activation(gap[:, h % 2, :], gap[:, h % 2, :], ACT.Exp, scale=-1.0).then_inc(decay_done.sem, 1)

                def lv(i):
                    wait_chunk(act, l, CI["lv"])
                    act.wait_ge(ones_done.sem, ones_done.at(l, 0))
                    act.activation(lv1[:, i, :, 0:HD], A("lv", i).rearrange("p (h e) -> p h e", h=HEADS), ACT.Copy)\
                       .then_inc(acc_sem("lv"), 1)

                def lo_(i):
                    wait_chunk(act, l, CI["lo"])
                    act.activation(sigo[:, i, :], A("lo", i), ACT.Sigmoid).then_inc(acc_sem("lo"), 1)

                def rv_(i):
                    wait_chunk(act, l, CI["rv"])
                    act.activation(rv[:, i, :], A("rv", i), ACT.Copy).then_inc(acc_sem("rv"), 1)

                def kpeT(_):
                    wait_job(act, l, ("kpeT", 0))
                    act.activation(krT[:, :], bank(("kpeT", 0))[:, 0:SEQ], ACT.Copy).then_inc(free_bank("kpeT", 0), 1)

                def mla_v(i):
                    wait_job(act, l, ("mla_v", i))
                    act.activation(mlaV[:, i, :], bank(("mla_v", i)), ACT.Copy).then_inc(free_bank("mla_v", i), 1)

                def qrT_(_):
                    wait_job(act, l, ("qrT", 0))
                    act.activation(qrT[:, :, :], bank(("qrT", 0)).rearrange("p (j t) -> p j t", j=2), ACT.Copy)\
                       .then_inc(free_bank("qrT", 0), 1)

                def turned(name, dst):
                    def evacuate(i):
                        wait_job(act, l, (name, i))
                        act.activation(dst[:, :, i * P:(i + 1) * P], bank((name, i)).rearrange("p (h t) -> p h t", h=HEADS),
                                       ACT.Copy).then_inc(free_bank(name, i), 1)
                    return evacuate

                def silu(g, i):
                    name = f"z{g}"
                    wait_chunk(act, l, CI[name])
                    if (g, i) == (3, 0):
                        wait_read(act, l, ("ml_scores", 3))
                    if (g, i) == (2, 0):
                        wait_job(act, l, ("rkT", 1))
                    if (g, i) == (0, 0):
                        wait_job(act, l, ("retT", 1))
                    act.activation(yT[:, 4 * g + 2 * i:4 * g + 2 * i + 2, :], A(name, i).rearrange("p (j t) -> p j t", j=2),
                                   ACT.Silu).then_inc(acc_sem(name), 1)

                steps = {"normalise": normalise, "x_hi": x_hi_, "y_hi": y_hi_, "memk": feat("memk", mKT),
                         "cq": feat("cq", cQT), "lx": lx, "mem_exp": mem_exp, "mem_pT": mem_pT,
                         "mla_exp": mla_exp, "mla_pT": mla_pT, "silu_conv": silu_conv, "akv": akv, "aq": aq,
                         "ml_q": pair("ml_q", lqT), "ml_k": pair("ml_k", lkT), "softplus": softplus,
                         "gate_floor": gate_floor, "ml_decay": ml_decay, "lv": lv, "lo": lo_, "rv": rv_,
                         "kpeT": kpeT, "mla_kn": pair("mla_kn", knT), "mla_qn": pair("mla_qn", qnT),
                         "mla_v": mla_v, "qrT": qrT_, "rqT": turned("rqT", rqT), "rkT": turned("rkT", rkT),
                         "silu": silu}
                for t in range(SLOTS):
                    c, k = divmod(t, KT)
                    w, s = CHUNKS[c][1], (t // 2) % RAW
                    if t % 2 == 0:
                        act.wait_ge(raw_full[s].sem, raw_full[s].at(l, t // 2 // RAW))
                    act.wait_ge(tile_used.sem, tile_used.at(l, t - RING))
                    act.activation(hi[:, t % RING, 0:w], raw[:, s, (t % 2) * w:(t % 2 + 1) * w], ACT.Copy)\
                       .then_inc(hi_done.sem, 1)
                    for name, *args in ACT_AT.get(t, ()):
                        steps[name](*args)
                assert links[0] == ACT_LINKS, links

            act.wait_ge(ln_done.sem, ln_done.at(DEPTH - 1, 0))
            for b in range(8):
                cb, i = divmod(b, 2)
                blk = X[:, i, cb * 512:(cb + 1) * 512]
                act.activation(blk, blk, ACT.Identity, scale=ln_rstd[:, i:i + 1], bias=ln_shift[:, i:i + 1])\
                   .then_inc(final_normed.sem, 1)

        @block.tensor
        def _(pe):
            pe.sem_inc(tile_used.sem, RING)
            pe.wait_ge(const_in.sem, 2 * 16)
            pe.wait_ge(mem_lo.sem, 4)

            with pe.Fori(0, DEPTH) as l:
                def take(*job):
                    b, u = bank_of(job)
                    stand_alone(pe)
                    pe.wait_ge(bank_read[b].sem, bank_read[b].at(l, u - 1))
                    return work[:, b, :]

                def turn(dst, src):
                    return pe.transpose(dst, src, ident[0:src.shape[0], 0:src.shape[0]])

                def xT(j):
                    pe.wait_ge(x_done.sem, x_done.at(l, 2 * (j // 2) + 1))
                    o = take("xT", j)
                    for kk in range(2):
                        for i in range(NT):
                            m = turn(o[:, kk * 256 + i * P:kk * 256 + (i + 1) * P],
                                     X[:, i, (2 * j + kk) * P:(2 * j + kk + 1) * P])
                    m.then_inc(job_done.sem, 1)

                def mem_scores(h):
                    if h == 0:
                        wait_acc_read(pe, l, CI["memk"])
                        wait_acc_read(pe, l, CI["cq"])
                    o = take("mem_scores", h)
                    for i in range(NT):
                        m = pe.matmul(o[:, i * 256:(i + 1) * 256], cQT[:, h, i * P:(i + 1) * P], mKT[:, h, :],
                                      start=True, stop=True)
                    m.then_inc(job_done.sem, 1)

                def mem_pT(h):
                    pe.wait_ge(prob_done.sem, prob_done.at(l, h))
                    o = take("mem_pT", h)
                    for kt in range(2):
                        for i in range(NT):
                            m = turn(o[:, kt * 256 + i * P:kt * 256 + (i + 1) * P],
                                     prob[:, h % 2, i * 256 + kt * P:i * 256 + (kt + 1) * P])
                    m.then_inc(job_done.sem, 1)

                def mem_out(q):
                    wait_acc_read(pe, l, CI["memv"])
                    wait_read(pe, l, ("mem_pT", 2 * q), ("mem_pT", 2 * q + 1))
                    o = take("mem_out", q)
                    for h in (2 * q, 2 * q + 1):
                        for kt in range(2):
                            m = pe.matmul(o[:, (h % 2) * 256:(h % 2 + 1) * 256], mV[:, kt, h * HD:(h + 1) * HD],
                                          probT[:, h % 2, kt * 256:(kt + 1) * 256], start=kt == 0, stop=kt == 1)
                    m.then_inc(job_done.sem, 1)

                def ml_proj(name, which):
                    def project(q):
                        if q == 0:
                            pe.wait_ge(lw_in.sem, lw_in.at(l, 0))
                        pe.wait_ge(xc_done.sem, xc_done.at(l, q))
                        o = take(name, q)
                        for h in (2 * q, 2 * q + 1):
                            m = pe.matmul(o[:, (h % 2) * 256:(h % 2 + 1) * 256], lw[:, which, h, :], xcT[:, h, :],
                                          start=True, stop=True)
                        m.then_inc(job_done.sem, 1)
                    return project

                def gateT(_):
                    wait_acc_read(pe, l, CI["akv"])
                    o = take("gateT", 0)
                    for g in range(2):
                        for i in range(NT):
                            m = turn(o[0:HEADS, g * 256 + i * P:g * 256 + (i + 1) * P],
                                     small[:, i, ROT + g * HEADS:ROT + (g + 1) * HEADS])
                    m.then_inc(job_done.sem, 1)

                def gate_cols(_):
                    pe.wait_ge(scan_done.sem, scan_done.at(l, 0))
                    pe.wait_ge(floor_done.sem, floor_done.at(l, 0))
                    o = take("gate_cols", 0)
                    stand_alone(pe)
                    for g in range(2):
                        for i in range(NT):
                            m = turn(o[:, (2 * g + i) * HEADS:(2 * g + i + 1) * HEADS],
                                     row[3 * g][:, i * P:(i + 1) * P])
                    m.then_inc(job_done.sem, 1)

                def m_rows(q):
                    o = take("m_rows", q)
                    for h in (2 * q, 2 * q + 1):
                        m = pe.matmul(o[:, (h % 2) * 256:(h % 2 + 1) * 256],
                                      ident[0:HEADS, h:h + 1].to_broadcast([HEADS, P]), row[1], start=True, stop=True)
                    m.then_inc(job_done.sem, 1)

                def cT_(i):
                    pe.wait_ge(c_normed.sem, c_normed.at(l, 1))
                    o = take("cT", i)
                    for j in range(4):
                        m = turn(o[:, j * P:(j + 1) * P], cqn[:, i, j * P:(j + 1) * P])
                    m.then_inc(job_done.sem, 1)

                def kpeT(_):
                    pe.wait_ge(kpe_done.sem, kpe_done.at(l, 0))
                    o = take("kpeT", 0)
                    for i in range(NT):
                        m = turn(o[:, i * P:(i + 1) * P], krr[:, i, :])
                    m.then_inc(job_done.sem, 1)

                def causal_scores(o, kT_, qT_, h):
                    pe.matmul(o[:, 0:256], kT_[:, h, 0:P], qT_[:, h, :], start=True, stop=True)
                    return pe.matmul(o[:, 256:TRI], kT_[:, h, P:2 * P], qT_[:, h, P:2 * P], start=True, stop=True)

                def ml_scores(h):
                    if h == 0:
                        wait_read(pe, l, ("ml_q", 0), ("ml_q", 1), ("ml_k", 0), ("ml_k", 1))
                    causal_scores(take("ml_scores", h), lkT, lqT, h).then_inc(job_done.sem, 1)

                def ml_out(h):
                    if h == 0:
                        wait_acc_read(pe, l, CI["lv"])
                    wait_read(pe, l, ("ml_scores", h))
                    o = take("ml_out", h)
                    pt, e = probT[:, h % 2, :], HD + 1
                    pe.matmul(o[:, 0:e], pt[:, 0:P], lv1[:, 0, h, :], start=True, stop=True)
                    pe.matmul(o[:, e:2 * e], pt[:, P:2 * P], lv1[:, 0, h, :], start=True, stop=False)
                    pe.matmul(o[:, e:2 * e], pt[:, 2 * P:3 * P], lv1[:, 1, h, :], start=False, stop=True)\
                      .then_inc(job_done.sem, 1)

                def mla_qr(i):
                    pe.wait_ge(mlaw_in.sem, mlaw_in.at(l, 1))
                    wait_read(pe, l, ("cT", i))
                    o = take("mla_qr", i)
                    for k in range(3):
                        m = pe.matmul(o[:, 0:HEADS * ROT].rearrange("p (h e) -> p h e", h=HEADS),
                                      cT[:, k, i * P:(i + 1) * P], wuq[:, k, :, NOPE:], start=k == 0, stop=k == 2)
                    m.then_inc(job_done.sem, 1)

                def mla_kn(q):
                    o = take("mla_kn", q)
                    for h in (2 * q, 2 * q + 1):
                        m = pe.matmul(o[:, (h % 2) * 256:(h % 2 + 1) * 256], wukv[:, h, 0, :], cT[:, 3, :],
                                      start=True, stop=True)
                    m.then_inc(job_done.sem, 1)

                def mla_qn(q):
                    o = take("mla_qn", q)
                    for h in (2 * q, 2 * q + 1):
                        for k in range(3):
                            m = pe.matmul(o[:, (h % 2) * 256:(h % 2 + 1) * 256], wuq[:, k, h, 0:NOPE], cT[:, k, :],
                                          start=k == 0, stop=k == 2)
                    m.then_inc(job_done.sem, 1)

                def mla_v(i):
                    o = take("mla_v", i)
                    pe.matmul(o.rearrange("p (h e) -> p h e", h=HEADS), cT[:, 3, i * P:(i + 1) * P], wukv[:, :, 1, :],
                              start=True, stop=True).then_inc(job_done.sem, 1)

                def qrT_(_):
                    pe.wait_ge(qr_done.sem, qr_done.at(l, 1))
                    o = take("qrT", 0)
                    for g in range(2):
                        for i in range(NT):
                            m = turn(o[:, g * 256 + i * P:g * 256 + (i + 1) * P], qr[:, i, g * P:(g + 1) * P])
                    m.then_inc(job_done.sem, 1)

                def cellT(q):
                    pe.wait_ge(cell_done.sem, cell_done.at(l, 0))
                    o = take("cellT", q)
                    for h in (2 * q, 2 * q + 1):
                        for i in range(NT):
                            m = turn(o[:, (h % 2) * 256 + i * P:(h % 2) * 256 + (i + 1) * P],
                                     cell[:, i, h * HD:(h + 1) * HD])
                    m.then_inc(job_done.sem, 1)

                def mla_scores(h):
                    if h == 0:
                        wait_read(pe, l, ("mla_kn", 0), ("mla_kn", 1), ("mla_qn", 0), ("mla_qn", 1),
                                  ("kpeT", 0), ("qrT", 0))
                        stand_alone(pe)
                    o = take("mla_scores", h)
                    r = slice((h % 2) * ROT, (h % 2 + 1) * ROT)
                    for i, (c0, c1) in enumerate(((0, P), (P, TRI))):
                        q = slice(i * P, (i + 1) * P)
                        pe.matmul(o[:, c0:c1], qnT[:, h, q], knT[:, h, 0:c1 - c0], start=True, stop=False)
                        m = pe.matmul(o[:, c0:c1], qrT[r, h // 2, q], krT[r, 0:c1 - c0], start=False, stop=True)
                    m.then_inc(job_done.sem, 1)

                def mla_pT(h):
                    pe.wait_ge(prob_done.sem, prob_done.at(l, HEADS + h))
                    o = take("mla_pT", h)
                    for j in range(3):
                        m = turn(o[:, j * P:(j + 1) * P], prob[:, h % 2, j * P:(j + 1) * P])
                    m.then_inc(job_done.sem, 1)

                def mla_out(q):
                    wait_read(pe, l, ("mla_v", 0), ("mla_v", 1), ("mla_pT", 2 * q), ("mla_pT", 2 * q + 1))
                    stand_alone(pe)
                    o = take("mla_out", q)
                    for h in (2 * q, 2 * q + 1):
                        c = (h % 2) * 256
                        pe.matmul(o[:, c:c + 256], mlaV[:, 0, h * HD:(h + 1) * HD], probT[:, h % 2, 0:256],
                                  start=True, stop=False, skip_group_check=True)
                        m = pe.matmul(o[:, c + P:c + 256], mlaV[:, 1, h * HD:(h + 1) * HD], probT[:, h % 2, 256:TRI],
                                      start=False, stop=True, skip_group_check=True)
                    m.then_inc(job_done.sem, 1)

                def turn_heads(name, src):
                    def turned(i):
                        pe.wait_ge(roped.sem, roped.at(l, i + (2 if name == "rkT" else 0)))
                        o = take(name, i)
                        for h in range(HEADS):
                            m = turn(o[:, h * P:(h + 1) * P], src[:, i, h * HD:(h + 1) * HD])
                        m.then_inc(job_done.sem, 1)
                    return turned

                def ret_scores(h):
                    if h == 0:
                        wait_read(pe, l, ("rqT", 0), ("rqT", 1), ("rkT", 0), ("rkT", 1))
                        stand_alone(pe)
                    causal_scores(take("ret_scores", h), rkT, rqT, h).then_inc(job_done.sem, 1)

                def ret_out(q):
                    wait_acc_read(pe, l, CI["rv"])
                    wait_read(pe, l, ("ret_scores", 2 * q), ("ret_scores", 2 * q + 1))
                    o = take("ret_out", q)
                    for h in (2 * q, 2 * q + 1):
                        pt, c, v = probT[:, h % 2, :], (h % 2) * 256, slice(h * HD, (h + 1) * HD)
                        pe.matmul(o[:, c:c + P], pt[:, 0:P], rv[:, 0, v], start=True, stop=True)
                        pe.matmul(o[:, c + P:c + 256], pt[:, P:2 * P], rv[:, 0, v], start=True, stop=False)
                        m = pe.matmul(o[:, c + P:c + 256], pt[:, 2 * P:3 * P], rv[:, 1, v], start=False, stop=True)
                    m.then_inc(job_done.sem, 1)

                def retT_(q):
                    wait_read(pe, l, ("ret_out", q))
                    o = take("retT", q)
                    for h in (2 * q, 2 * q + 1):
                        for i in range(NT):
                            m = turn(o[:, (h % 2) * 256 + i * P:(h % 2) * 256 + (i + 1) * P],
                                     retn[:, i, h * HD:(h + 1) * HD])
                    m.then_inc(job_done.sem, 1)

                steps = {"xT": xT, "mem_scores": mem_scores, "mem_pT": mem_pT, "mem_out": mem_out,
                         "ml_q": ml_proj("ml_q", 0), "ml_k": ml_proj("ml_k", 1), "gateT": gateT,
                         "gate_cols": gate_cols, "m_rows": m_rows, "cT": cT_, "kpeT": kpeT,
                         "ml_scores": ml_scores, "ml_out": ml_out, "mla_qr": mla_qr, "mla_kn": mla_kn,
                         "mla_qn": mla_qn, "mla_v": mla_v, "qrT": qrT_, "cellT": cellT,
                         "mla_scores": mla_scores, "mla_pT": mla_pT, "mla_out": mla_out,
                         "rqT": turn_heads("rqT", rqt), "rkT": turn_heads("rkT", rkt),
                         "ret_scores": ret_scores, "ret_out": ret_out, "retT": retT_}

                for t in range(SLOTS):
                    c, k = divmod(t, KT)
                    name, w, layout = CHUNKS[c]
                    s, p = t % RING, c % 2
                    ah, al = (mh, ml) if c < 2 else (xh, xl)
                    kk = OUT_ORDER[k] if c >= OUT0 else k
                    if k == 0:
                        pe.wait_ge(acc_read[p].sem, acc_read[p].at(l, (c // 2) * 2 - 1))
                    if c == 2 and k % 2 == 0:
                        wait_read(pe, l, ("xT", k // 2))
                    if c == OUT0 and k % 2 == 0:
                        pe.wait_ge(y_lo.sem, y_lo.at(l, k // 2))
                    pe.wait_ge(hi_done.sem, hi_done.at(l, t))
                    if layout == "tok":
                        for i in range(NT):
                            o, q = acc[:, p, i, 0:w], slice(i * P, (i + 1) * P)
                            pe.matmul(o, ah[:, kk, q], hi[:, s, 0:w], start=k == 0, stop=False)
                            pe.matmul(o, al[:, kk, q], hi[:, s, 0:w], start=False, stop=False)
                        pe.wait_ge(lo_done.sem, lo_done.at(l, t))
                        for i in range(NT):
                            m = pe.matmul(acc[:, p, i, 0:w], ah[:, kk, i * P:(i + 1) * P], lo[:, s, 0:w],
                                          start=False, stop=k == KT - 1)
                    else:
                        for j in range(4):
                            o, q = acc[:, p, j // 2, (j % 2) * 256:(j % 2 + 1) * 256], slice(j * P, (j + 1) * P)
                            pe.matmul(o, hi[:, s, q], ah[:, kk, :], start=k == 0 and j % 2 == 0, stop=False,
                                      skip_group_check=True)
                            pe.matmul(o, hi[:, s, q], al[:, kk, :], start=False, stop=False, skip_group_check=True)
                        pe.wait_ge(lo_done.sem, lo_done.at(l, t))
                        for j in range(4):
                            o, q = acc[:, p, j // 2, (j % 2) * 256:(j % 2 + 1) * 256], slice(j * P, (j + 1) * P)
                            m = pe.matmul(o, lo[:, s, q], ah[:, kk, :], start=False, stop=k == KT - 1,
                                          skip_group_check=True)
                    m.then_inc(tile_used.sem, 1)
                    for step, *args in PE_AT.get(t, ()):
                        steps[step](*args)

        @block.vector
        def _(dve):
            for p in range(2):
                dve.sem_inc(acc_read[p].sem, 2)
            for b in range(NBANK):
                dve.sem_inc(bank_read[b].sem, 1)
            dve.sem_inc(lo_done.sem, 2 * RAW)
            dve.memset(half[:, :], -0.5).then_inc(ready.sem, 1)
            dve.memset(ln_shift[:, :], 0.0)
            dve.memset(ln_rstd[:, :], 1.0).then_inc(ln_done.sem, 1)

            links = [0]

            def link0(ins):
                ins.then_inc(dve_own.sem, 1)
                links[0] += 1
                dve.wait_ge(dve_own.sem, links[0])

            ang = angle_views()
            dve.wait_ge(const_in.sem, 2 * 16)
            link0(dve.tensor_copy(rinv[:, 0, :], pos[:, :]))
            for i in range(NT):
                last = dve.tensor_scalar(ang["raw"][:, i, :], freq, rinv[:, 0, i:i + 1], None, ALU.mult)
            link0(last)
            turns, magic = 1.0 / (2.0 * np.pi), 12582912.0
            for n, (dst, quarter) in enumerate((("sin", 0.0), ("cos", 0.25))):
                d, r = ang[dst], ang["turns"]
                link0(dve.tensor_scalar(r, ang["raw"], turns, quarter, ALU.mult, ALU.add))
                link0(dve.tensor_scalar(r, r, magic, None, ALU.add))
                link0(dve.tensor_scalar(r, r, -magic, None, ALU.add))
                src = ang["raw"]
                for part in two_pi_parts():
                    link0(dve.scalar_tensor_tensor(d, r, -part, src, ALU.mult, ALU.add))
                    src = d
                link0(dve.tensor_scalar(d, d, quarter * 2.0 * np.pi, None, ALU.add))
                clamp = dve.tensor_scalar(d, d, PI_IN, -PI_IN, ALU.min, ALU.max)
                if n:
                    clamp.then_inc(angles.sem, 1)
                else:
                    link0(clamp)
            for q in range(4):
                dve.wait_ge(mem_hi.sem, q + 1)
                dve.tensor_tensor(ml[:, 4 * q:4 * q + 4, :], memT[q].rearrange("p (k t) -> p k t", k=4),
                                  mh[:, 4 * q:4 * q + 4, :].bitcast(F32), ALU.subtract).then_inc(mem_lo.sem, 1)
            dve.wait_ge(tables.sem, 2)
            for c_, s_, f0, f1 in ((cosr, sinr, 0, FR), (cosm, sinm, FR, FR + FM)):
                dve.tensor_copy(c_[:, :, :], ang["cos"][:, :, f0:f1])
                dve.tensor_scalar(s_[:, :, 0, :], ang["sin"][:, :, f0:f1], -1.0, None, ALU.mult)
                last = dve.tensor_copy(s_[:, :, 1, :], ang["sin"][:, :, f0:f1])
            link0(last)
            assert links[0] == DVE_LINKS_BEFORE, links

            with dve.Fori(0, DEPTH) as l:
                links = [0]

                def link(ins):
                    ins.then_inc(dve_own.sem, 1)
                    links[0] += 1
                    dve.wait_ge(dve_own.sem, dve_own.at(l, links[0] - 1))

                def x_lo(j):
                    dve.wait_ge(x_hi.sem, x_hi.at(l, j))
                    dve.tensor_tensor(xl[:, 2 * j:2 * j + 2, :], bank(("xT", j)).rearrange("p (k t) -> p k t", k=2),
                                      xh[:, 2 * j:2 * j + 2, :].bitcast(F32), ALU.subtract)\
                       .then_inc(free_bank("xT", j), 1)

                def y_lo_(j):
                    k = OUT_ORDER[2 * j]
                    dve.wait_ge(y_hi.sem, y_hi.at(l, j))
                    dve.tensor_tensor(xl[:, k:k + 2, :], yT[:, k:k + 2, :], xh[:, k:k + 2, :].bitcast(F32),
                                      ALU.subtract).then_inc(y_lo.sem, 1)

                def memv(i):
                    wait_chunk(dve, l, CI["memv"])
                    dve.tensor_copy(mV[:, i, :], A("memv", i)).then_inc(acc_sem("memv"), 1)

                def mem_max(h):
                    wait_job(dve, l, ("mem_scores", h))
                    link(dve.tensor_reduce(nmax[:, h % 2, :], bank(("mem_scores", h)).rearrange("p (i k) -> p i k", i=NT),
                                           AX.X, ALU.max, negate=True))
                    dve.tensor_scalar(nmax[:, h % 2, :], nmax[:, h % 2, :], HEAD_SCALE, None, ALU.mult)\
                       .then_inc(max_done.sem, 1)

                def mem_norm(h):
                    wait_read(dve, l, ("mem_scores", h))
                    link(dve.reciprocal(rinv[:, h % 2, :], rsum[:, h % 2, :]))
                    for i in range(NT):
                        pr = prob[:, h % 2, i * 256:(i + 1) * 256]
                        m = dve.tensor_scalar(pr, pr, rinv[:, h % 2, i:i + 1], None, ALU.mult)
                    m.then_inc(prob_done.sem, 1)

                def out_pair(name, dst):
                    def evacuate(q):
                        wait_job(dve, l, (name, q))
                        dve.tensor_copy(dst[:, 2 * q:2 * q + 2, :], bank((name, q)).rearrange("p (j t) -> p j t", j=2))\
                           .then_inc(free_bank(name, q), 1)
                    return evacuate

                def conv(s):
                    if s == 0:
                        dve.wait_ge(cols_in.sem, cols_in.at(l, 0))
                        dve.memset(LX[:, :, 0:PAD], 0.0).then_inc(lx_pad.sem, 1)
                        dve.wait_ge(lx_pad.sem, lx_pad.at(l, 0))
                        wait_acc_read(dve, l, CI["lx"])
                    j, tap0 = divmod(s, 2)
                    for tap in (2 * tap0, 2 * tap0 + 1):
                        wcol = cols[:, C_CONVW + tap * 4 + j:C_CONVW + tap * 4 + j + 1]
                        if tap == 0:
                            link(dve.tensor_scalar(xcT[:, j, :], LX[:, j, 0:SEQ], wcol, None, ALU.mult))
                        else:
                            m = dve.scalar_tensor_tensor(xcT[:, j, :], LX[:, j, tap:tap + SEQ], wcol, xcT[:, j, :],
                                                         ALU.mult, ALU.add)
                            if (j, tap) == (3, 3):
                                m.then_inc(conv_done.sem, 1)
                            else:
                                link(m)

                def rms_(r):
                    dve.wait_ge(sq_done.sem, sq_done.at(l, r))
                    dve.tensor_scalar(sumsq[:, r, :], sumsq[:, r, :], 1.0 / (KVRANK, QRANK)[r], RMS_EPS,
                                      ALU.mult, ALU.add).then_inc(var_done.sem, 1)

                def ckv(_):
                    dve.wait_ge(rms_done.sem, rms_done.at(l, 0))
                    for i in range(NT):
                        dve.tensor_scalar(cqn[:, i, QRANK:QRANK + KVRANK], A("akv", i)[:, 0:KVRANK], rms[:, 0, i:i + 1],
                                          None, ALU.mult).then_inc(acc_sem("akv"), 1)

                def cqn_(i):
                    dve.wait_ge(rms_done.sem, rms_done.at(l, 1))
                    dve.tensor_scalar(cqn[:, i, 0:QRANK], A("aq", i)[:, 0:QRANK], rms[:, 1, i:i + 1],
                                      None, ALU.mult).then_inc(acc_sem("aq"), 1)
                    if i:
                        wait_acc_read(dve, l, CI["aq"])
                        wait_acc_read(dve, l, CI["akv"])
                        dve.sem_inc(c_normed.sem, 2)

                def kpe_rope(_):
                    for i in range(NT):
                        src = small[:, i, 0:ROT].rearrange("p (a f) -> p a f", a=2)
                        t1 = tmp[:, i * P:i * P + ROT].rearrange("p (a f) -> p a f", a=2)
                        t2 = tmp[:, i * P + ROT:i * P + P].rearrange("p (a f) -> p a f", a=2)
                        dve.tensor_tensor(t1, src, cosm[:, i, :].unsqueeze(1).to_broadcast([P, 2, FM]), ALU.mult)
                        link(dve.tensor_tensor(t2, src[:, ::-1, :], sinm[:, i, :, :], ALU.mult))
                    for i in range(NT):
                        t1, t2 = tmp[:, i * P:i * P + ROT], tmp[:, i * P + ROT:i * P + P]
                        m = dve.tensor_tensor(krr[:, i, :].rearrange("p (d e) -> p d e", d=2),
                                              t1.unsqueeze(1).to_broadcast([P, 2, ROT]),
                                              t2.unsqueeze(1).to_broadcast([P, 2, ROT]), ALU.add)
                    m.then_inc(kpe_done.sem, 1)

                def gates(_):
                    wait_job(dve, l, ("gateT", 0), ("ml_k", 1))
                    dve.wait_ge(cols_in.sem, cols_in.at(l, 0))
                    o = bank(("gateT", 0))
                    dve.tensor_scalar(row[0], o[0:HEADS, 0:SEQ], cols[0:HEADS, C_IB:C_IB + 1], None, ALU.add)
                    link(dve.tensor_scalar(row[1], o[0:HEADS, SEQ:2 * SEQ], cols[0:HEADS, C_FB:C_FB + 1], None, ALU.add))
                    dve.sem_inc(free_bank("gateT", 0), 1)
                    dve.scalar_tensor_tensor(row[2], row[1], -1.0, row[1], ALU.mult, ALU.max).then_inc(gate_abs.sem, 1)

                def gate_scan(_):
                    link(dve.tensor_scalar(row[1], row[1], 0.0, None, ALU.min))
                    dve.wait_ge(softplus_done.sem, softplus_done.at(l, 0))
                    link(dve.tensor_tensor_scan(row[3], row[1], row[2], 0.0, ALU.add, ALU.subtract))
                    link(dve.tensor_tensor(row[0], row[0], row[3], ALU.subtract))
                    link(dve.tensor_tensor_scan(row[1], row[0], row[0], 0.0, ALU.max, ALU.max))
                    dve.tensor_tensor(row[3], row[3], row[1], ALU.add).then_inc(scan_done.sem, 1)

                def skip(_):
                    wait_job(dve, l, ("ml_k", 1))
                    for j in range(4):
                        m = dve.tensor_scalar(mls[:, j, :], xcT[:, j, :], cols[:, C_SKIP + j:C_SKIP + j + 1], None, ALU.mult)
                    m.then_inc(skip_done.sem, 1)

                def ones(_):
                    wait_job(dve, l, ("mem_scores", HEADS - 1))
                    dve.memset(lv1[:, :, :, HD:HD + 1], 1.0).then_inc(ones_done.sem, 1)

                def cT_(i):
                    wait_job(dve, l, ("cT", i))
                    dve.tensor_tensor(cT[:, :, i * P:(i + 1) * P], bank(("cT", i)).rearrange("p (j t) -> p j t", j=4),
                                      cols[:, C_CG:C_CG + 4].unsqueeze(2).to_broadcast([P, 4, P]), ALU.mult)\
                       .then_inc(free_bank("cT", i), 1)

                def gate_cols(_):
                    wait_job(dve, l, ("gate_cols", 0))
                    dve.tensor_copy(gcol[:, :, :], bank(("gate_cols", 0))[:, 0:4 * HEADS].rearrange("p (g h) -> p g h", g=4))\
                       .then_inc(free_bank("gate_cols", 0), 1)

                def ml_gap(h):
                    q = h // 2
                    wait_job(dve, l, ("m_rows", q))
                    if h == 0:
                        wait_read(dve, l, ("gate_cols", 0))
                    if h >= 2:
                        wait_read(dve, l, ("ml_scores", h - 2))
                    o = bank(("m_rows", q))[:, (h % 2) * 256:(h % 2 + 1) * 256]
                    dve.scalar_tensor_tensor(gap[:, h % 2, 0:256], o, gcol[:, 0, h:h + 1], big[:, 0:256],
                                             ALU.subtract, ALU.max)
                    dve.scalar_tensor_tensor(gap[:, h % 2, 256:TRI], o[:, P:256], gcol[:, 1, h:h + 1], big[:, 256:TRI],
                                             ALU.subtract, ALU.max).then_inc(gap_done.sem, 1)
                    if h % 2:
                        dve.wait_ge(gap_done.sem, gap_done.at(l, h))
                        dve.sem_inc(free_bank("m_rows", q), 1)

                def ml_weigh(h):
                    wait_job(dve, l, ("ml_scores", h), *([("ml_out", h - 2)] if h >= 2 else []))
                    dve.wait_ge(decay_done.sem, decay_done.at(l, h))
                    dve.scalar_tensor_tensor(probT[:, h % 2, 0:TRI], bank(("ml_scores", h))[:, 0:TRI], HEAD_SCALE,
                                             gap[:, h % 2, :], ALU.mult, ALU.mult).then_inc(free_bank("ml_scores", h), 1)

                def ml_out(h):
                    wait_job(dve, l, ("ml_out", h), ("ml_scores", HEADS - 1))
                    o = bank(("ml_out", h))[:, 0:NT * (HD + 1)].rearrange("p (i e) -> p i e", i=NT)
                    d = den[:, h % 2, :]
                    link(dve.scalar_tensor_tensor(d, o[:, :, HD], -1.0, gcol[:, 2:4, h], ALU.mult, ALU.max))
                    link(dve.tensor_tensor(d, o[:, :, HD], d, ALU.max))
                    link(dve.reciprocal(d, d))
                    for i in range(NT):
                        m = dve.tensor_scalar(cell[:, i, h * HD:(h + 1) * HD], o[:, i, 0:HD], den[:, h % 2, i:i + 1],
                                              None, ALU.mult)
                    m.then_inc(free_bank("ml_out", h), 1)

                def cell_gate(i):
                    wait_acc_read(dve, l, CI["lo"])
                    wait_read(dve, l, ("ml_out", HEADS - 1))
                    link(dve.tensor_tensor(cell[:, i, :], cell[:, i, :], sigo[:, i, :], ALU.mult))

                def cell_stats(i):
                    for h in range(HEADS):
                        m = dve.bn_stats(stats[:, i * HEADS + h, :], cell[:, i, h * HD:(h + 1) * HD])
                    link(m)
                    stand_alone(dve)
                    for h in range(HEADS):
                        m = dve.bn_aggr(mv[:, i * HEADS + h, :], stats[:, i * HEADS + h, :])
                    link(m)
                    if i:
                        dve.tensor_scalar(stats[:, :, 0], mv[:, :, 1], LN_EPS, None, ALU.add).then_inc(cell_var.sem, 1)

                def cell_norm(i):
                    dve.wait_ge(cell_pow.sem, cell_pow.at(l, 0))
                    for h in range(HEADS):
                        n, s = i * HEADS + h, cell[:, i, h * HD:(h + 1) * HD]
                        m = dve.tensor_scalar(s, s, mv[:, n, 0:1], rstd[:, n:n + 1], ALU.subtract, ALU.mult)
                    if i:
                        m.then_inc(cell_done.sem, 1)

                def cellT(q):
                    wait_job(dve, l, ("cellT", q))
                    dve.wait_ge(skip_done.sem, skip_done.at(l, 0))
                    for h in (2 * q, 2 * q + 1):
                        m = dve.scalar_tensor_tensor(mls[:, h, :], bank(("cellT", q))[:, (h % 2) * 256:(h % 2 + 1) * 256],
                                                     cols[:, C_MLG + h:C_MLG + h + 1], mls[:, h, :], ALU.mult, ALU.add)
                    m.then_inc(free_bank("cellT", q), 1)

                def rope(dst, src, cos, sin, halfw):
                    n = dst.shape[1] // (2 * halfw)
                    d = dst.rearrange("p (h a f) -> p h a f", h=n, a=2)
                    s = src.rearrange("p (h a f) -> p h a f", h=n, a=2)
                    t = tmp[:, 0:n * 2 * halfw].rearrange("p (h a f) -> p h a f", h=n, a=2)
                    dve.tensor_tensor(d, s, cos.unsqueeze(1).unsqueeze(1).to_broadcast([P, n, 2, halfw]), ALU.mult)
                    return dve.tensor_tensor(t, s[:, :, ::-1, :], sin.unsqueeze(1).to_broadcast([P, n, 2, halfw]), ALU.mult)

                def q_rope(i):
                    wait_job(dve, l, ("mla_qr", i))
                    link(rope(qr[:, i, :], bank(("mla_qr", i))[:, 0:HEADS * ROT], cosm[:, i, :], sinm[:, i, :, :], FM))
                    dve.sem_inc(free_bank("mla_qr", i), 1)
                    dve.tensor_tensor(qr[:, i, :], qr[:, i, :], tmp[:, 0:HEADS * ROT], ALU.add).then_inc(qr_done.sem, 1)
                    dve.wait_ge(qr_done.sem, qr_done.at(l, i))

                def rope_ret(name, dst, n):
                    def go(i):
                        wait_chunk(dve, l, CI[name])
                        if name == "rq" and i == 0:
                            wait_job(dve, l, ("mla_qn", 1))
                        rope(dst[:, i, :], A(name, i), cosr[:, i, :], sinr[:, i, :, :], FR).then_inc(acc_sem(name), 1)
                        wait_acc_read(dve, l, CI[name], halves=i + 1)
                        dve.tensor_tensor(dst[:, i, :], dst[:, i, :], tmp[:, :], ALU.add).then_inc(roped.sem, 1)
                        dve.wait_ge(roped.sem, roped.at(l, n + i))
                    return go

                def mla_max(h):
                    wait_job(dve, l, ("mla_scores", h), *([("mla_pT", h - 2)] if h >= 2 else []))
                    dve.tensor_tensor(prob[:, h % 2, 0:TRI], bank(("mla_scores", h))[:, 0:TRI], tri, ALU.add)\
                       .then_inc(free_bank("mla_scores", h), 1)
                    wait_read(dve, l, ("mla_scores", h))
                    dve.tensor_reduce(nmax[:, h % 2, 0:1], prob[:, h % 2, 0:P], AX.X, ALU.max, negate=True)
                    link(dve.tensor_reduce(nmax[:, h % 2, 1:2], prob[:, h % 2, P:TRI], AX.X, ALU.max, negate=True))
                    dve.tensor_scalar(nmax[:, h % 2, :], nmax[:, h % 2, :], MLA_SCALE, None, ALU.mult)\
                       .then_inc(max_done.sem, 1)

                def mla_norm(h):
                    dve.wait_ge(exp_done.sem, exp_done.at(l, h))
                    link(dve.reciprocal(rinv[:, h % 2, :], rsum[:, h % 2, :]))
                    for i, (c0, c1) in enumerate(((0, P), (P, TRI))):
                        pr = prob[:, h % 2, c0:c1]
                        m = dve.tensor_scalar(pr, pr, rinv[:, h % 2, i:i + 1], None, ALU.mult)
                    m.then_inc(prob_done.sem, 1)

                def ret_weigh(h):
                    wait_job(dve, l, ("ret_scores", h), ("ret_out", 0) if h >= 2 else ("mla_out", 1))
                    dve.tensor_tensor(probT[:, h % 2, 0:TRI], bank(("ret_scores", h))[:, 0:TRI], decay[:, h, :],
                                      ALU.mult).then_inc(free_bank("ret_scores", h), 1)

                def ret_block(q, n):
                    return bank(("ret_out", q))[:, n * HD:(n + 1) * HD]

                def ret_stats(q):
                    wait_job(dve, l, ("ret_out", q))
                    for n in range(4):
                        m = dve.bn_stats(stats[:, n, :], ret_block(q, n))
                    link(m)
                    stand_alone(dve)
                    for n in range(4):
                        m = dve.bn_aggr(mv[:, n, :], stats[:, n, :])
                    link(m)
                    dve.tensor_scalar(stats[:, 0:4, 0], mv[:, 0:4, 1], LN_EPS, None, ALU.add).then_inc(ret_var.sem, 1)

                def ret_norm(q):
                    dve.wait_ge(ret_pow.sem, ret_pow.at(l, q))
                    for n in range(4):
                        h, i = 2 * q + n // 2, n % 2
                        m = dve.tensor_scalar(retn[:, i, h * HD:(h + 1) * HD], ret_block(q, n), mv[:, n, 0:1],
                                              rstd[:, n:n + 1], ALU.subtract, ALU.mult)
                    m.then_inc(free_bank("ret_out", q), 1)

                def retT_(q):
                    wait_job(dve, l, ("retT", q))
                    for h in (2 * q, 2 * q + 1):
                        m = dve.tensor_scalar(retT[:, h, :], bank(("retT", q))[:, (h % 2) * 256:(h % 2 + 1) * 256],
                                              cols[:, C_RETG + h:C_RETG + h + 1], None, ALU.mult)
                    m.then_inc(free_bank("retT", q), 1)

                def gate(g, i):
                    src = {3: memo, 2: mls, 1: mlao, 0: retT}[g]
                    last = {3: "mem_out", 2: "cellT", 1: "mla_out", 0: "retT"}[g]
                    wait_acc_read(dve, l, CI[f"z{g}"], halves=i + 1)
                    wait_read(dve, l, (last, 1))
                    y = yT[:, 4 * g + 2 * i:4 * g + 2 * i + 2, :]
                    dve.tensor_tensor(y, y, src[:, 2 * i:2 * i + 2, :], ALU.mult).then_inc(gated.sem, 1)

                def residual(c):
                    name, w = CHUNKS[OUT0 + c][0], CHUNKS[OUT0 + c][1]
                    wait_chunk(dve, l, OUT0 + c)
                    for i in range(NT):
                        xc = X[:, i, OUTCOL[c]:OUTCOL[c] + w]
                        dve.scalar_tensor_tensor(xc, xc, ALPHA, A(name, i)[:, 0:w], ALU.mult, ALU.add)\
                           .then_inc(acc_sem(name), 1)
                        wait_acc_read(dve, l, OUT0 + c, halves=i + 1)
                        m = dve.bn_stats(ln_stats[:, i, c, :], xc)
                    return m

                steps = {"x_lo": x_lo, "y_lo": y_lo_, "memv": memv, "mem_max": mem_max, "mem_norm": mem_norm,
                         "mem_out": out_pair("mem_out", memo), "conv": conv, "rms": rms_, "ckv": ckv, "cqn": cqn_,
                         "kpe_rope": kpe_rope, "gates": gates, "gate_scan": gate_scan, "skip": skip, "ones": ones,
                         "cT": cT_, "gate_cols": gate_cols, "ml_gap": ml_gap, "ml_weigh": ml_weigh, "ml_out": ml_out,
                         "cell_gate": cell_gate, "cell_stats": cell_stats, "cell_norm": cell_norm, "cellT": cellT,
                         "q_rope": q_rope, "rope_rq": rope_ret("rq", rqt, 0), "rope_rk": rope_ret("rk", rkt, 2),
                         "mla_max": mla_max, "mla_norm": mla_norm, "mla_out": out_pair("mla_out", mlao),
                         "ret_weigh": ret_weigh, "ret_stats": ret_stats, "ret_norm": ret_norm, "retT": retT_,
                         "gate": gate, "residual": residual}
                for t in range(SLOTS):
                    c, k = divmod(t, KT)
                    w, s = CHUNKS[c][1], (t // 2) % RAW
                    dve.wait_ge(hi_done.sem, hi_done.at(l, t))
                    dve.wait_ge(tile_used.sem, tile_used.at(l, t - RING))
                    dve.tensor_tensor(lo[:, t % RING, 0:w], raw[:, s, (t % 2) * w:(t % 2 + 1) * w],
                                      hi[:, t % RING, 0:w].bitcast(F32), ALU.subtract).then_inc(lo_done.sem, 1)
                    for name, *args in DVE_AT.get(t, ()):
                        steps[name](*args)

                link(residual(NOUT - 1))
                stand_alone(dve)
                for i in range(NT):
                    m = dve.bn_aggr(ln_mv[:, i, :], ln_stats[:, i, :, :].rearrange("p c s -> p (c s)"))
                link(m)
                dve.tensor_scalar(ln_stats[:, :, 0, 0], ln_mv[:, :, 1], LN_EPS, None, ALU.add).then_inc(ln_var.sem, 1)
                dve.wait_ge(ln_pow.sem, ln_pow.at(l, 0))
                dve.scalar_tensor_tensor(ln_shift[:, :], ln_mv[:, :, 0], -1.0, ln_rstd[:, :], ALU.mult, ALU.mult)\
                   .then_inc(ln_done.sem, 1)
                assert links[0] == DVE_LINKS, links

            dve.wait_ge(gb_in.sem, gb_in.at(DEPTH - 1, 0))
            for b in range(8):
                cb, i = divmod(b, 2)
                blk = X[:, i, cb * 512:(cb + 1) * 512]
                dve.wait_ge(final_normed.sem, b + 1)
                dve.tensor_tensor(blk, blk, gb[:, 0, cb * 512:(cb + 1) * 512], ALU.mult).then_inc(final_scaled.sem, 1)


def stream_columns(name):
    r = lambda at, n: list(range(at, at + n))
    if name == "memk":
        return r(0, W)
    if name == "memv":
        return r(W, W)
    if name == "akv":
        return r(COL["akv"], KVRANK + ROT) + r(COL["li"], 2 * HEADS)
    if name == "aq":
        return r(COL["aq"], QRANK)
    if name[0] == "z":
        return r(COL["z"] + int(name[1:]) * W, W)
    if name[:3] == "out":
        c = int(name[3:])
        return r(OUTCOL[c], CHUNKS[OUT0 + c][1])
    return r(COL[name], W)


def constants():
    f = np.float64
    k, q = np.arange(P)[:, None], np.arange(SEQ)[None, :]
    rel = q - k
    rel = np.concatenate([rel, rel[:, :P]], 1)
    gamma = 1.0 - 2.0 ** (-5.0 - np.arange(HEADS, dtype=f))
    dec = np.where(rel[None] >= 0, gamma[:, None, None] ** np.maximum(rel, 0)[None], 0.0) * HEAD_SCALE
    dec = dec.transpose(1, 0, 2).reshape(P, HEADS * TRI)
    big = np.where(rel >= 0, 0.0, MASKED)
    above = np.where(np.arange(P)[None, :] <= np.arange(P)[:, None], 0.0, -MASKED)
    tri = np.concatenate([above, np.zeros((P, P)), above], 1)
    freqs = np.concatenate([THETA ** (-np.arange(n, dtype=f) / n) for n in (FR, FM)])
    return np.concatenate([np.eye(P), dec, tri, big, np.tile(freqs, (P, 1))], 1).astype(np.float32)


def kernel(**inputs):
    import concourse.bacc as _bacc
    from concourse.bass_utils import run_bass_kernel_spmd as _run

    g = {k: np.asarray(v) for k, v in inputs.items()}

    def stream(l):
        parts = []
        for name, w, _ in CHUNKS:
            m = g["w_mem_kv"] if name[:3] == "mem" else g["w_out"] if name[:3] == "out" else g["w_in"]
            order = OUT_ORDER if name[:3] == "out" else range(KT)
            t = m[l][:, stream_columns(name)].reshape(KT, P, w)[list(order)]
            parts.append(t.reshape(KT // 2, 2, P, w).transpose(0, 2, 1, 3).reshape(-1))
        return np.concatenate(parts)

    def columns(l):
        col = lambda v: v.reshape(-1, P).T
        bias = lambda v: np.concatenate([v, np.zeros(P - HEADS, v.dtype)])[:, None]
        return np.concatenate([col(g["ret_norm_g"][l]), col(g["mla_q_norm_g"][l]), col(g["mla_kv_norm_g"][l]),
                               col(g["ml_conv_w"][l].reshape(-1)), col(g["ml_conv_b"][l]), col(g["ml_skip"][l]),
                               col(g["ml_norm_g"][l]), bias(g["ml_i_bias"][l]), bias(g["ml_f_bias"][l])], 1).reshape(-1)

    none = np.concatenate([np.ones(D_MODEL, np.float32), np.zeros(D_MODEL, np.float32)])
    arrays = {
        "x": g["x"].reshape(SEQ, D_MODEL),
        "pos": np.ascontiguousarray(g["positions"].reshape(NT, P).T),
        "mem_t": np.ascontiguousarray(g["mem"][0].T.reshape(KT, P, MEM_LEN).transpose(1, 0, 2).reshape(P, -1)),
        "w": np.stack([stream(l) for l in range(DEPTH)]),
        "cols": np.stack([columns(l) for l in range(DEPTH)]),
        "lw": np.stack([np.stack([g["ml_w_q"][l], g["ml_w_k"][l]]).transpose(2, 0, 1, 3).reshape(-1) for l in range(DEPTH)]),
        "wuq": np.stack([g["mla_w_uq"][l].reshape(3, P, -1).transpose(1, 0, 2).reshape(-1) for l in range(DEPTH)]),
        "wukv": np.stack([g["mla_w_ukv"][l].reshape(-1) for l in range(DEPTH)]),
        "gb": np.stack([none] + [np.concatenate([g["ln_g"][l], g["ln_b"][l]]) for l in range(DEPTH)]),
        "const": constants(),
    }
    nc = _bacc.Bacc("TRN2", target_bir_lowering=False, num_devices=1)
    maps, args = {}, {}
    for name, v in arrays.items():
        v = np.ascontiguousarray(v)
        maps[f"in_{name}"] = v
        args[name] = nc.dram_tensor(f"in_{name}", v.shape, mybir.dt.from_np(v.dtype), kind="ExternalInput").ap()
    out = nc.dram_tensor("out_x", (SEQ, D_MODEL), F32, kind="ExternalOutput").ap()
    build_trunk(nc, args, out)
    r = _run(nc, [maps], core_ids=[0])
    return r.results[0]["out_x"].reshape(1, SEQ, D_MODEL)
```

```python
from contextlib import ExitStack

import numpy as np

import concourse.bass as bass
from concourse import mybir

F32 = mybir.dt.float32
F32R = mybir.dt.float32r
I32 = mybir.dt.int32
ALU = mybir.AluOpType
ACT = mybir.ActivationFunctionType
AX = mybir.AxisListType

P = 128
DEPTH = 2
D_MODEL = 2048
SEQ = 256
MEM_LEN = 256
HEADS = 4
HD = 128
NOPE, ROT = 128, 64
QRANK, KVRANK = 384, 128
TAPS = 4
NT = SEQ // P
KT = D_MODEL // P
GROUPS = 4
W = HEADS * HD
THETA = 10000.0
LN_EPS, RMS_EPS = 1e-5, 1e-6
ALPHA = (2 * DEPTH) ** 0.25
MLA_SCALE = float(NOPE + ROT) ** -0.5
HEAD_SCALE = float(HD) ** -0.5
PAD = TAPS - 1
TRI = 3 * P
MASKED = 1e30

_sizes = (W, W, W, QRANK, KVRANK, ROT, W, W, W, HEADS, HEADS, W, GROUPS * W)
_names = ("rq", "rk", "rv", "aq", "akv", "ape", "lx", "lv", "lo", "li", "lf", "cq", "z")
COL = dict(zip(_names, np.concatenate([[0], np.cumsum(_sizes)[:-1]]).tolist()))

AKV_W = KVRANK + ROT + 2 * HEADS
CHUNKS = [("memk", W, "feat"), ("memv", W, "tok"), ("lx", W, "feat"), ("cq", W, "feat"),
          ("akv", AKV_W, "tok"), ("aq", QRANK, "tok"), ("lv", W, "tok"), ("lo", W, "tok"),
          ("rq", W, "tok"), ("rk", W, "tok"), ("rv", W, "tok"),
          ("z3", W, "feat"), ("z2", W, "feat"), ("z1", W, "feat"), ("z0", W, "feat"),
          ("out0", 512, "tok"), ("out1", 512, "tok"), ("out2", 512, "tok"),
          ("out3", 256, "tok"), ("out4", 256, "tok")]
NCH = len(CHUNKS)
CI = {c[0]: i for i, c in enumerate(CHUNKS)}
OUT0 = CI["out0"]
OUTCOL = [0, 512, 1024, 1536, 1792]
NOUT = len(OUTCOL)
OUT_ORDER = [12, 13, 14, 15, 8, 9, 10, 11, 4, 5, 6, 7, 0, 1, 2, 3]
SLOTS = NCH * KT
PAIRS = SLOTS // 2
RAW = 5
RING = 5
AHEAD = 4
CHUNK_AT = np.concatenate([[0], np.cumsum([KT * P * w for _, w, _ in CHUNKS])]).tolist()

C_RETG, C_CG, C_CONVW, C_CONVB, C_SKIP, C_MLG, C_IB, C_FB = 0, 4, 8, 24, 28, 32, 36, 37
NCOLS = 38
K_DECAY = 0
K_TRI = K_DECAY + HEADS * TRI
K_BIG = K_TRI + TRI
NCONST = K_BIG + TRI
FR, FM = HD // 2, ROT // 2

PE_AT = {}


def _put(table, slot, *step):
    table.setdefault(slot, []).append(step)


for _j in range(8):
    _put(PE_AT, 16 + 2 * _j, "xT", _j)
for _h in range(HEADS):
    _put(PE_AT, 66 + 6 * _h, "mem_scores", _h)
    _put(PE_AT, 75 + 6 * _h, "mem_pT", _h)
    _put(PE_AT, 153 + 6 * _h, "mla_scores", _h)
    _put(PE_AT, 162 + 6 * _h, "mla_pT", _h)
for _s, *_step in [
        (87, "mem_out", 0), (99, "mem_out", 1),
        (83, "ml_q", 0), (85, "ml_q", 1), (87, "ml_k", 0), (89, "ml_k", 1),
        (90, "gateT", 0), (104, "gate_cols", 0), (106, "m_rows", 0), (114, "m_rows", 1),
        (105, "cT", 0), (107, "cT", 1), (108, "kpeT", 0),
        (110, "ml_scores", 0), (112, "ml_scores", 1), (119, "ml_scores", 2), (121, "ml_scores", 3),
        (119, "ml_out", 0), (121, "ml_out", 1), (127, "ml_out", 2), (129, "ml_out", 3),
        (131, "mla_qr", 0), (132, "mla_qr", 1), (133, "mla_kn", 0), (135, "mla_kn", 1),
        (136, "mla_qn", 0), (138, "mla_qn", 1), (140, "mla_v", 0), (142, "mla_v", 1), (143, "qrT", 0),
        (150, "cellT", 0), (151, "cellT", 1),
        (154, "rqT", 0), (155, "rqT", 1), (170, "rkT", 0), (172, "rkT", 1),
        (174, "mla_out", 0), (186, "mla_out", 1),
        (188, "ret_scores", 0), (190, "ret_scores", 1), (198, "ret_scores", 2), (200, "ret_scores", 3),
        (197, "ret_out", 0), (207, "ret_out", 1), (209, "retT", 0), (219, "retT", 1)]:
    _put(PE_AT, _s, *_step)
JOBS = [step for slot in sorted(PE_AT) for step in PE_AT[slot]]
NJOBS = len(JOBS)
NBANK = 4
JOB = {step: j for j, step in enumerate(JOBS)}

ACT_AT = {}
for _j in range(8):
    _put(ACT_AT, 8 + 3 * _j // 2, "normalise", _j)
    _put(ACT_AT, 21 + 2 * _j, "x_hi", _j)
for _h in range(HEADS):
    _put(ACT_AT, 71 + 6 * _h, "mem_exp", _h)
    _put(ACT_AT, 80 + 6 * _h, "mem_pT", _h)
    _put(ACT_AT, 158 + 6 * _h, "mla_exp", _h)
    _put(ACT_AT, 167 + 6 * _h, "mla_pT", _h)
for _s, *_step in [
        (20, "memk", 0), (22, "memk", 1), (44, "rotary", 0), (52, "lx", 0), (53, "lx", 1),
        (65, "silu_conv", 0), (66, "silu_conv", 1), (68, "cq", 0), (69, "cq", 1), (84, "akv", 0), (85, "akv", 1),
        (88, "ml_q", 0), (90, "ml_q", 1), (92, "ml_k", 0), (94, "ml_k", 1),
        (96, "softplus", 0), (99, "gate_floor", 0), (100, "aq", 0), (101, "aq", 1),
        (111, "ml_decay", 0), (112, "ml_decay", 1), (113, "kpeT", 0), (119, "ml_decay", 2), (120, "ml_decay", 3),
        (116, "lv", 0), (117, "lv", 1), (132, "lo", 0), (133, "lo", 1),
        (138, "mla_kn", 0), (140, "mla_kn", 1), (141, "mla_qn", 0), (143, "mla_qn", 1),
        (145, "mla_v", 0), (147, "mla_v", 1), (149, "qrT", 0),
        (160, "rqT", 0), (161, "rqT", 1), (176, "rkT", 0), (178, "rkT", 1),
        (180, "rv", 0), (181, "rv", 1),
        (196, "silu", 3, 0), (197, "silu", 3, 1), (212, "silu", 2, 0), (213, "silu", 2, 1),
        (228, "silu", 1, 0), (229, "silu", 1, 1), (246, "silu", 0, 0), (247, "silu", 0, 1),
        (205, "y_hi", 0), (207, "y_hi", 1), (221, "y_hi", 2), (223, "y_hi", 3),
        (244, "y_hi", 4), (245, "y_hi", 5), (251, "y_hi", 6), (252, "y_hi", 7)]:
    _put(ACT_AT, _s, *_step)

DVE_AT = {}
for _j in range(8):
    _put(DVE_AT, 21 + 2 * _j, "x_lo", _j)
    _put(DVE_AT, 54 + _j, "conv", _j)
    _put(DVE_AT, 22 + 2 * _j, "angles", _j)
for _h in range(HEADS):
    _put(DVE_AT, 71 + 6 * _h, "mem_max", _h)
    _put(DVE_AT, 73 + 6 * _h, "mem_norm", _h)
    _put(DVE_AT, 158 + 6 * _h, "mla_max", _h)
    _put(DVE_AT, 160 + 6 * _h, "mla_norm", _h)
for _s, *_step in [
        (36, "memv", 0), (38, "memv", 1), (92, "mem_out", 0), (105, "mem_out", 1),
        (86, "rms", 0), (88, "ckv", 0), (89, "kpe_rope", 0),
        (95, "gates", 0), (97, "gate_scan", 0), (98, "skip", 0), (100, "ones", 0),
        (102, "rms", 1), (103, "cqn", 0), (104, "cqn", 1), (110, "cT", 0), (113, "cT", 1), (109, "gate_cols", 0),
        (111, "ml_gap", 0), (112, "ml_gap", 1), (119, "ml_gap", 2), (120, "ml_gap", 3),
        (115, "ml_weigh", 0), (117, "ml_weigh", 1), (124, "ml_weigh", 2), (126, "ml_weigh", 3),
        (127, "ml_out", 0), (128, "ml_out", 1), (132, "ml_out", 2), (134, "ml_out", 3),
        (136, "cell_gate", 0), (137, "cell_gate", 1), (139, "cell_stats", 0), (140, "cell_stats", 1),
        (142, "cell_norm", 0), (144, "cell_norm", 1),
        (137, "q_rope", 0), (138, "q_rope", 1),
        (156, "cellT", 0), (157, "cellT", 1),
        (148, "rope_rq", 0), (150, "rope_rq", 1), (165, "rope_rk", 0), (167, "rope_rk", 1),
        (179, "mla_out", 0), (191, "mla_out", 1),
        (193, "ret_weigh", 0), (195, "ret_weigh", 1), (203, "ret_weigh", 2), (205, "ret_weigh", 3),
        (202, "ret_stats", 0), (204, "ret_norm", 0), (212, "ret_stats", 1), (214, "ret_norm", 1),
        (216, "retT", 0), (224, "retT", 1),
        (198, "gate", 3, 0), (199, "gate", 3, 1), (215, "gate", 2, 0), (216, "gate", 2, 1),
        (230, "gate", 1, 0), (231, "gate", 1, 1), (248, "gate", 0, 0), (249, "gate", 0, 1),
        (206, "y_lo", 0), (208, "y_lo", 1), (222, "y_lo", 2), (224, "y_lo", 3),
        (244, "y_lo", 4), (245, "y_lo", 5), (251, "y_lo", 6), (252, "y_lo", 7)]:
    _put(DVE_AT, _s, *_step)
for _c in range(NOUT - 1):
    _put(DVE_AT, (OUT0 + _c + 1) * KT + 4, "residual", _c)

DVE_LINKS, ACT_LINKS = 73, 3
DVE_LINKS_BEFORE = 4


POOL_BIAS, DVE_BIAS = [0, 1, 2, 4, 6], [3, 5, 7]


def pair_at(m):
    c, j = divmod(m, KT // 2)
    w = CHUNKS[c][1]
    return CHUNK_AT[c] + j * 2 * P * w, w


def two_pi_parts():
    first = 6.28125
    second = 253.0 / 2 ** 17
    return first, second, 2.0 * np.pi - first - second


PI_IN = 3.1415925


class Signal:

    def __init__(self, sem, per_layer, before=0, step=1):
        self.sem, self.per_layer, self.before, self.step = sem, per_layer, before, step

    def at(self, layer, i):
        return layer * (self.per_layer * self.step) + (self.before + i + 1) * self.step


def build_trunk(nc, a, out):
    ctx = ExitStack()
    with ctx:
        def sb(name, shape, dt=F32):
            return ctx.enter_context(nc.sbuf_tensor(name, shape, dt))

        def signal(name, per_layer, before=0, step=1):
            return Signal(ctx.enter_context(nc.semaphore(name)), per_layer, before, step)

        X = sb("X", [P, NT, D_MODEL])
        xh, xl = sb("xh", [P, KT, SEQ], F32R), sb("xl", [P, KT, SEQ], F32R)
        mh, ml = sb("mh", [P, KT, MEM_LEN], F32R), sb("ml", [P, KT, MEM_LEN], F32R)
        Y = sb("Y", [P, KT * SEQ])
        raw = sb("raw", [P, RAW, 2 * 512])
        hi, lo = sb("hi", [P, RING, 512], F32R), sb("lo", [P, RING, 512], F32R)
        const = sb("const", [P, NCONST])
        ident_buf = sb("ident", [P, P])
        cols = sb("cols", [P, NCOLS])
        early_buf, B = [], []
        for i in range(10):
            if i < 4:
                with nc.sbuf_tensor(f"early{i}", [P, 2, 2, SEQ], F32R) as same_place:
                    early_buf.append(same_place)
            B.append(sb(f"B{i}", [P, {0: NT * HEADS * (HD + 1), 3: 4 * (SEQ + PAD)}.get(i, 4 * SEQ)]))
        qr = sb("qr", [P, NT, HEADS * ROT])
        qrT = sb("qrT", [P, 2, SEQ])
        krr = sb("krr", [P, NT, P])
        krT = sb("krT", [P, SEQ])
        prob = sb("prob", [P, 2, 512])
        probT = sb("probT", [P, 2, 512])
        tmp = sb("tmp", [P, 512])
        freq = sb("freq", [P, FR + FM])
        cos, sin = sb("cos", [P, NT, FR + FM]), sb("sin", [P, 2, NT, FR + FM])
        small = sb("small", [P, NT, AKV_W - KVRANK])
        gcol = sb("gcol", [P, 4, HEADS])
        nmax, rsum, rinv = sb("nmax", [P, 2, 2]), sb("rsum", [P, 2, 2]), sb("rinv", [P, 2, 2])
        sumsq, rms = sb("sumsq", [P, 2, NT]), sb("rms", [P, 2, NT])
        den = sb("den", [P, 2, NT])
        stats, mv, rstd = sb("stats", [P, 8, 6]), sb("mv", [P, 8, 2]), sb("rstd", [P, 8])
        ln_stats, ln_mv = sb("ln_stats", [P, NT, NOUT, 6]), sb("ln_mv", [P, NT, 2])
        ln_rstd, ln_shift = sb("ln_rstd", [P, NT]), sb("ln_shift", [P, NT])
        half = sb("half", [P, 8])
        pos = sb("pos", [P, NT], I32)
        warm = sb("warm", [P, 1])

        memT = [B[i][:, 0:4 * SEQ] for i in range(4)]
        turn1 = B[4][:, 0:NT * (FR + FM)].rearrange("p (i f) -> p i f", i=NT)
        whole = B[4][:, 512:512 + 2 * NT * (FR + FM)].rearrange("p (a i f) -> p a i f", a=2, i=NT)
        angle = B[5][:, 0:2 * NT * (FR + FM)].rearrange("p (a i f) -> p a i f", a=2, i=NT)
        mKT, lv1, rqT = (B[0][:, 0:1024].rearrange("p (h t) -> p h t", h=HEADS),
                         B[0][:, 0:NT * HEADS * (HD + 1)].rearrange("p (i h e) -> p i h e", i=NT, h=HEADS),
                         B[0][:, 0:1024].rearrange("p (h t) -> p h t", h=HEADS))
        mV = mlaV = B[1][:, 0:1024].rearrange("p (i w) -> p i w", i=NT)
        cQT = memo = B[2][:, 0:1024].rearrange("p (h t) -> p h t", h=HEADS)
        LX = B[3][:, 0:4 * (SEQ + PAD)].rearrange("p (j t) -> p j t", j=4)
        lkT = rkT = B[3][:, 0:1024].rearrange("p (h t) -> p h t", h=HEADS)
        xcT = mls = B[4][:, 0:1024].rearrange("p (h t) -> p h t", h=HEADS)
        lqT = retT = B[5][:, 0:1024].rearrange("p (h t) -> p h t", h=HEADS)
        cell = B[5][:, 0:1024].rearrange("p (i w) -> p i w", i=NT)
        lw = B[6][:, 0:1024].rearrange("p (q h e) -> p q h e", q=2, h=HEADS)
        row = [B[6][0:HEADS, r * SEQ:(r + 1) * SEQ] for r in range(4)]
        sigo = rv = B[6][:, 0:1024].rearrange("p (i w) -> p i w", i=NT)
        cqn = B[7][:, 0:NT * 512].rearrange("p (i w) -> p i w", i=NT)
        knT = B[7][:, 0:1024].rearrange("p (h t) -> p h t", h=HEADS)
        cT = B[8][:, 0:1024].rearrange("p (j t) -> p j t", j=4)
        qnT = mlao = B[9][:, 0:1024].rearrange("p (h t) -> p h t", h=HEADS)
        gb = Y[:, :].rearrange("p (a n) -> p a n", a=2)
        wukv = Y[:, 0:1024].rearrange("p (h v e) -> p h v e", h=HEADS, v=2)
        wuq = Y[:, 1024:1024 + 3 * HEADS * (NOPE + ROT)].rearrange("p (k h e) -> p k h e", k=3, h=HEADS)
        gap = Y[:, 4096 - 2 * TRI:4096].rearrange("p (b c) -> p b c", b=2)
        rqt = Y[:, 1024:2048].rearrange("p (i w) -> p i w", i=NT)
        rkt = Y[:, 2048:3072].rearrange("p (i w) -> p i w", i=NT)
        retn = Y[:, 0:1024].rearrange("p (i w) -> p i w", i=NT)
        yT = Y[:, :].rearrange("p (k t) -> p k t", k=KT)
        junk = tmp

        early = [early_buf[i] for i in (1, 2, 3, 0)]

        def y_part(part, j):
            if j < len(early):
                return early[j][:, part, :, :]
            return (xh, xl)[part][:, OUT_ORDER[2 * j]:OUT_ORDER[2 * j] + 2, :]

        ident = ident_buf[:, :]
        decay = const[:, K_DECAY:K_DECAY + HEADS * TRI].rearrange("p (h c) -> p h c", h=HEADS)
        tri, big = const[:, K_TRI:K_TRI + TRI], const[:, K_BIG:K_BIG + TRI]

        acc = ctx.enter_context(nc.psum_tensor("acc", [P, 2, 2, 512], F32))
        work = ctx.enter_context(nc.psum_tensor("work", [P, NBANK, 512], F32))

        raw_full = [signal(f"raw_full{s}", PAIRS // RAW, step=16) for s in range(RAW)]
        hi_done = signal("hi_done", SLOTS)
        lo_done = signal("lo_done", SLOTS, before=2 * RAW)
        tile_used = signal("tile_used", SLOTS, before=RING)
        acc_read = [signal(f"acc_read{p}", NCH, before=2) for p in range(2)]
        job_done = signal("job_done", NJOBS)
        in_bank = [[j for j in range(NJOBS) if j % NBANK == b] for b in range(NBANK)]
        bank_read = [signal(f"bank_read{b}", len(in_bank[b]), before=1) for b in range(NBANK)]
        memb_in = [signal(f"mem_in{q}", 0, step=16) for q in range(4)]
        rotary_in, ident_in, const_in = (signal(n, 0, step=16) for n in ("rotary_in", "ident_in", "const_in"))
        x_in = [signal(f"x_in{cb}", 0, step=16) for cb in range(4)]
        mem_dve, mem_pool = signal("mem_dve", 0), signal("mem_pool", 0)
        angles, tables = signal("angles", 1), signal("tables", 1)
        pool_hi = signal("pool_hi", 0)
        ready = signal("ready", 0)
        cols_in = signal("cols_in", 1, step=16)
        lw_in = signal("lw_in", 1, step=16)
        mlaw_in = signal("mlaw_in", 2, step=16)
        gb_in = signal("gb_in", 1, before=1, step=16)
        normed = signal("normed", 8)
        x_done = signal("x_done", 8, before=0)
        x_hi = signal("x_hi", 8)
        y_hi, y_lo = signal("y_hi", 8), signal("y_lo", 8)
        conv_done, xc_done = signal("conv_done", 1), signal("xc_done", 2)
        lx_pad = signal("lx_pad", 1)
        sq_done, var_done, rms_done = signal("sq_done", 2), signal("var_done", 2), signal("rms_done", 2)
        c_normed = signal("c_normed", 2)
        kpe_done = signal("kpe_done", 1)
        gate_abs, softplus_done = signal("gate_abs", 1), signal("softplus_done", 1)
        scan_done, floor_done = signal("scan_done", 1), signal("floor_done", 1)
        skip_done, ones_done = signal("skip_done", 1), signal("ones_done", 1)
        gap_done, decay_done = signal("gap_done", 4), signal("decay_done", 4)
        max_done, exp_done, prob_done = signal("max_done", 8), signal("exp_done", 4), signal("prob_done", 8)
        qr_done = signal("qr_done", 2)
        cell_var, cell_pow, cell_done = signal("cell_var", 1), signal("cell_pow", 1), signal("cell_done", 1)
        ret_var, ret_pow = signal("ret_var", 2), signal("ret_pow", 2)
        ln_var, ln_pow, ln_done = signal("ln_var", 1), signal("ln_pow", 1), signal("ln_done", 1, before=1)
        gated = signal("gated", 8)
        roped = signal("roped", 4)
        pool_mul = signal("pool_mul", 8)
        alone = signal("alone", 0)
        final_scaled, stored = signal("final_scaled", 0), signal("stored", 0, step=16)
        pool_biased, dve_biased = signal("pool_biased", 0), signal("dve_biased", 0)
        final_normed = signal("final_normed", 0)
        dve_own = signal("dve_own", DVE_LINKS, before=DVE_LINKS_BEFORE)
        act_own = signal("act_own", ACT_LINKS)

        def stand_alone(eng):
            eng.sem_inc(alone.sem, 1)

        def bank_of(job):
            j = JOB[job]
            return j % NBANK, j // NBANK

        def bank(job):
            return work[:, bank_of(job)[0], :]

        def wait_job(eng, l, *jobs):
            eng.wait_ge(job_done.sem, job_done.at(l, max(JOB[job] for job in jobs)))

        def wait_read(eng, l, *jobs):
            last = {}
            for job in jobs:
                b, u = bank_of(job)
                last[b] = max(u, last.get(b, 0))
            for b, u in last.items():
                eng.wait_ge(bank_read[b].sem, bank_read[b].at(l, u))

        def free_bank(*job):
            return bank_read[bank_of(job)[0]].sem

        def wait_chunk(eng, l, c):
            eng.wait_ge(tile_used.sem, tile_used.at(l, (c + 1) * KT - 1))

        def wait_acc_read(eng, l, c, halves=2):
            eng.wait_ge(acc_read[c % 2].sem, acc_read[c % 2].at(l, (c // 2) * 2 + halves - 1))

        def acc_sem(name):
            return acc_read[CI[name] % 2].sem

        def A(name, i):
            return acc[:, CI[name] % 2, i, :]

        block = ctx.enter_context(nc.Block())

        @block.sync
        def _(sp):
            sp.dma_start(memT[0], a["mem_t"][:, 0:1024]).then_inc(memb_in[0].sem, 16)
            with sp.Fori(0, DEPTH) as l:
                for m in range(PAIRS):
                    sp.wait_ge(lo_done.sem, lo_done.at(l, 2 * m + 1 - 2 * RAW))
                    at, w = pair_at(m)
                    sp.dma_start(raw[:, m % RAW, 0:2 * w],
                                 a["w"][bass.ts(l, 1), at:at + 2 * P * w].rearrange("o (p n) -> p (o n)", p=P))\
                      .then_inc(raw_full[m % RAW].sem, 16)
                    if m == 4:
                        sp.dma_start(cols[:, :], a["cols"][bass.ts(l, 1), :].rearrange("o (p n) -> p (o n)", p=P))\
                          .then_inc(cols_in.sem, 16)
                    if m == 20:
                        sp.dma_start(B[6][:, 0:1024], a["lw"][bass.ts(l, 1), :].rearrange("o (p n) -> p (o n)", p=P))\
                          .then_inc(lw_in.sem, 16)
                    if m == 24:
                        sp.wait_ge(x_done.sem, x_done.at(l, 7))
                        sp.dma_start(Y[:, 0:1024], a["wukv"][bass.ts(l, 1), :].rearrange("o (p n) -> p (o n)", p=P))\
                          .then_inc(mlaw_in.sem, 16)
                        sp.dma_start(Y[:, 1024:3328], a["wuq"][bass.ts(l, 1), :].rearrange("o (p n) -> p (o n)", p=P))\
                          .then_inc(mlaw_in.sem, 16)
                    if m == 136:
                        sp.wait_ge(y_lo.sem, y_lo.at(l, 7))
                        sp.dma_start(Y[:, :], a["gb"][bass.ts(l, 1), :].partition_broadcast(P)
                                     .rearrange("p o n -> p (o n)")).then_inc(gb_in.sem, 16)
            for b in range(8):
                cb, i = divmod(b, 2)
                if b in POOL_BIAS:
                    sp.wait_ge(pool_biased.sem, POOL_BIAS.index(b) + 1)
                else:
                    sp.wait_ge(dve_biased.sem, DVE_BIAS.index(b) + 1)
                sp.dma_start(out[i * P:(i + 1) * P, cb * 512:(cb + 1) * 512],
                             X[:, i, cb * 512:(cb + 1) * 512]).then_inc(stored.sem, 16)
            sp.wait_ge(stored.sem, 8 * 16)

        @block.gpsimd
        def _(pool):
            pool.memset(gb[:, 0, :], 1.0)
            pool.memset(gb[:, 1, :], 0.0).then_inc(gb_in.sem, 16)

            def load_x(cb):
                pool.dma_start(X[:, :, cb * 512:(cb + 1) * 512],
                               a["x"][:, cb * 512:(cb + 1) * 512].rearrange("(i p) n -> p i n", p=P))\
                    .then_inc(x_in[cb].sem, 16)

            for q in (2, 3):
                m3 = memT[q].rearrange("p (k t) -> p k t", k=4)
                load_x(2 * q - 4)
                pool.wait_ge(memb_in[q].sem, 16)
                pool.tensor_copy(mh[:, 4 * q:4 * q + 4, :], m3).then_inc(pool_hi.sem, 1)
                load_x(2 * q - 3)
                pool.wait_ge(pool_hi.sem, q - 1)
                pool.tensor_tensor(ml[:, 4 * q:4 * q + 4, :], m3, mh[:, 4 * q:4 * q + 4, :].bitcast(F32), ALU.subtract)\
                    .then_inc(mem_pool.sem, 1)
            pool.dma_start(ident, a["ident"]).then_inc(ident_in.sem, 16)
            pool.dma_start(const[:, :], a["const"]).then_inc(const_in.sem, 16)
            pool.wait_ge(ready.sem, 1)

            def root(dst, src, n):
                return pool.tensor_tensor(dst, src, half[:, 0:n], ALU.pow)

            with pool.Fori(0, DEPTH) as l:
                pool.wait_ge(gb_in.sem, gb_in.at(l, -1))
                for b in range(8):
                    cb, i = divmod(b, 2)
                    blk = X[:, i, cb * 512:(cb + 1) * 512]
                    pool.wait_ge(normed.sem, normed.at(l, b))
                    pool.tensor_tensor(blk, blk, gb[:, 0, cb * 512:(cb + 1) * 512], ALU.mult)\
                        .then_inc(pool_mul.sem, 1)
                    pool.wait_ge(pool_mul.sem, pool_mul.at(l, b))
                    pool.tensor_tensor(blk, blk, gb[:, 1, cb * 512:(cb + 1) * 512], ALU.add)\
                        .then_inc(x_done.sem, 1)
                for r in range(2):
                    pool.wait_ge(var_done.sem, var_done.at(l, r))
                    root(rms[:, r, :], sumsq[:, r, :], NT).then_inc(rms_done.sem, 1)
                pool.wait_ge(cell_var.sem, cell_var.at(l, 0))
                root(rstd[:, :], stats[:, :, 0], 8).then_inc(cell_pow.sem, 1)
                for r in range(2):
                    pool.wait_ge(ret_var.sem, ret_var.at(l, r))
                    root(rstd[:, 0:4], stats[:, 0:4, 0], 4).then_inc(ret_pow.sem, 1)
                pool.wait_ge(ln_var.sem, ln_var.at(l, 0))
                root(ln_rstd[:, :], ln_stats[:, :, 0, 0], NT).then_inc(ln_pow.sem, 1)

            for b in POOL_BIAS:
                cb, i = divmod(b, 2)
                blk = X[:, i, cb * 512:(cb + 1) * 512]
                pool.wait_ge(final_scaled.sem, b + 1)
                pool.tensor_tensor(blk, blk, gb[:, 1, cb * 512:(cb + 1) * 512], ALU.add)\
                    .then_inc(pool_biased.sem, 1)

        @block.scalar
        def _(act):
            act.dma_start(pos[:, :], a["pos"]).then_inc(rotary_in.sem, 16)
            for q in range(1, 4):
                act.dma_start(memT[q], a["mem_t"][:, q * 1024:(q + 1) * 1024]).then_inc(memb_in[q].sem, 16)
            act.dma_start(freq[:, :], a["freq"]).then_inc(rotary_in.sem, 16)
            act.wait_ge(ready.sem, 1)

            with act.Fori(0, DEPTH) as l:
                act.activation(warm[:, :], half[:, 0:1], ACT.Copy)
                links = [0]

                def link(ins):
                    ins.then_inc(act_own.sem, 1)
                    links[0] += 1
                    act.wait_ge(act_own.sem, act_own.at(l, links[0] - 1))

                def normalise(b):
                    cb, i = divmod(b, 2)
                    blk = X[:, i, cb * 512:(cb + 1) * 512]
                    act.wait_ge(x_in[cb].sem, 16)
                    if b == 0:
                        act.wait_ge(ln_done.sem, ln_done.at(l, -1))
                    act.activation(blk, blk, ACT.Identity, scale=ln_rstd[:, i:i + 1], bias=ln_shift[:, i:i + 1])\
                       .then_inc(normed.sem, 1)

                def rotary(_):
                    act.wait_ge(angles.sem, angles.at(l, 0))
                    act.activation(cos[:, :, :], angle[:, 1, :, :], ACT.Sin)
                    act.activation(sin[:, 0, :, :], angle[:, 0, :, :], ACT.Sin, scale=-1.0)
                    act.activation(sin[:, 1, :, :], angle[:, 0, :, :], ACT.Sin).then_inc(tables.sem, 1)

                def x_hi_(j):
                    wait_job(act, l, ("xT", j))
                    act.activation(xh[:, 2 * j:2 * j + 2, :], bank(("xT", j)).rearrange("p (k t) -> p k t", k=2),
                                   ACT.Copy).then_inc(x_hi.sem, 1)

                def y_hi_(j):
                    k = OUT_ORDER[2 * j]
                    if j == 2:
                        wait_job(act, l, ("ret_scores", HEADS - 1))
                    if j == len(early):
                        wait_chunk(act, l, OUT0 - 1)
                    act.wait_ge(gated.sem, gated.at(l, j))
                    act.activation(y_part(0, j), yT[:, k:k + 2, :], ACT.Copy).then_inc(y_hi.sem, 1)

                def feat(name, dst):
                    def evacuate(i):
                        wait_chunk(act, l, CI[name])
                        act.activation(dst[:, 2 * i:2 * i + 2, :], A(name, i).rearrange("p (j t) -> p j t", j=2),
                                       ACT.Copy).then_inc(acc_sem(name), 1)
                    return evacuate

                def lx(i):
                    wait_chunk(act, l, CI["lx"])
                    act.activation(LX[:, 2 * i:2 * i + 2, PAD:PAD + SEQ],
                                   A("lx", i).rearrange("p (j t) -> p j t", j=2), ACT.Copy)\
                       .then_inc(acc_sem("lx"), 1)

                def mem_exp(h):
                    act.wait_ge(max_done.sem, max_done.at(l, h))
                    if h >= 2:
                        wait_job(act, l, ("mem_pT", h - 2))
                    for i in range(NT):
                        e = act.activation(prob[:, h % 2, i * 256:(i + 1) * 256], bank(("mem_scores", h))[:, i * 256:(i + 1) * 256],
                                           ACT.Exp, scale=HEAD_SCALE, bias=nmax[:, h % 2, i:i + 1],
                                           accum_out=rsum[:, h % 2, i:i + 1])
                    e.then_inc(free_bank("mem_scores", h), 1)

                def mem_pT(h):
                    wait_job(act, l, ("mem_pT", h), *([("mem_out", 0)] if h >= 2 else []))
                    act.activation(probT[:, h % 2, :], bank(("mem_pT", h)), ACT.Copy)\
                       .then_inc(free_bank("mem_pT", h), 1)

                def mla_exp(h):
                    act.wait_ge(max_done.sem, max_done.at(l, HEADS + h))
                    for i, (c0, c1) in enumerate(((0, P), (P, TRI))):
                        e = act.activation(prob[:, h % 2, c0:c1], prob[:, h % 2, c0:c1], ACT.Exp, scale=MLA_SCALE,
                                           bias=nmax[:, h % 2, i:i + 1], accum_out=rsum[:, h % 2, i:i + 1])
                    e.then_inc(exp_done.sem, 1)

                def mla_pT(h):
                    wait_job(act, l, ("mla_pT", h), *([("mla_out", 0)] if h >= 2 else []))
                    act.activation(probT[:, h % 2, 0:TRI], bank(("mla_pT", h))[:, 0:TRI], ACT.Copy)\
                       .then_inc(free_bank("mla_pT", h), 1)

                def silu_conv(q):
                    act.wait_ge(conv_done.sem, conv_done.at(l, 0))
                    for j in range(2 * q, 2 * q + 2):
                        s = act.activation(xcT[:, j, :], xcT[:, j, :], ACT.Silu, bias=cols[:, C_CONVB + j:C_CONVB + j + 1])
                    s.then_inc(xc_done.sem, 1)

                def akv(i):
                    wait_chunk(act, l, CI["akv"])
                    if i:
                        act.activation(small[:, i, :], A("akv", i)[:, KVRANK:AKV_W], ACT.Copy)
                        act.activation(junk[:, 0:KVRANK], A("akv", i)[:, 0:KVRANK], ACT.Square,
                                       accum_out=sumsq[:, 0, i:i + 1]).then_inc(sq_done.sem, 1)
                    else:
                        act.activation(small[:, i, :], A("akv", i)[:, KVRANK:AKV_W], ACT.Copy)
                        link(act.activation(junk[:, 0:KVRANK], A("akv", i)[:, 0:KVRANK], ACT.Square,
                                            accum_out=sumsq[:, 0, i:i + 1]))

                def aq(i):
                    wait_chunk(act, l, CI["aq"])
                    s = act.activation(junk[:, 0:QRANK], A("aq", i)[:, 0:QRANK], ACT.Square,
                                       accum_out=sumsq[:, 1, i:i + 1])
                    if i:
                        s.then_inc(sq_done.sem, 1)
                    else:
                        link(s)

                def pair(name, dst):
                    def evacuate(i):
                        wait_job(act, l, (name, i))
                        act.activation(dst[:, 2 * i:2 * i + 2, :], bank((name, i)).rearrange("p (j t) -> p j t", j=2),
                                       ACT.Copy).then_inc(free_bank(name, i), 1)
                    return evacuate

                def softplus(_):
                    act.wait_ge(gate_abs.sem, gate_abs.at(l, 0))
                    link(act.activation(row[2], row[2], ACT.Exp, scale=-1.0))
                    act.activation(row[2], row[2], ACT.Ln, bias=1.0).then_inc(softplus_done.sem, 1)

                def gate_floor(_):
                    act.wait_ge(scan_done.sem, scan_done.at(l, 0))
                    act.activation(row[3], row[3], ACT.Exp, scale=-1.0).then_inc(floor_done.sem, 1)

                def ml_decay(h):
                    act.wait_ge(gap_done.sem, gap_done.at(l, h))
                    act.activation(gap[:, h % 2, :], gap[:, h % 2, :], ACT.Exp, scale=-1.0).then_inc(decay_done.sem, 1)

                def lv(i):
                    wait_chunk(act, l, CI["lv"])
                    act.wait_ge(ones_done.sem, ones_done.at(l, 0))
                    act.activation(lv1[:, i, :, 0:HD], A("lv", i).rearrange("p (h e) -> p h e", h=HEADS), ACT.Copy)\
                       .then_inc(acc_sem("lv"), 1)

                def lo_(i):
                    wait_chunk(act, l, CI["lo"])
                    act.activation(sigo[:, i, :], A("lo", i), ACT.Sigmoid).then_inc(acc_sem("lo"), 1)

                def rv_(i):
                    wait_chunk(act, l, CI["rv"])
                    act.activation(rv[:, i, :], A("rv", i), ACT.Copy).then_inc(acc_sem("rv"), 1)

                def kpeT(_):
                    wait_job(act, l, ("kpeT", 0))
                    act.activation(krT[:, :], bank(("kpeT", 0))[:, 0:SEQ], ACT.Copy).then_inc(free_bank("kpeT", 0), 1)

                def mla_v(i):
                    wait_job(act, l, ("mla_v", i))
                    act.activation(mlaV[:, i, :], bank(("mla_v", i)), ACT.Copy).then_inc(free_bank("mla_v", i), 1)

                def qrT_(_):
                    wait_job(act, l, ("qrT", 0))
                    act.activation(qrT[:, :, :], bank(("qrT", 0)).rearrange("p (j t) -> p j t", j=2), ACT.Copy)\
                       .then_inc(free_bank("qrT", 0), 1)

                def turned(name, dst):
                    def evacuate(i):
                        wait_job(act, l, (name, i))
                        act.activation(dst[:, :, i * P:(i + 1) * P], bank((name, i)).rearrange("p (h t) -> p h t", h=HEADS),
                                       ACT.Copy).then_inc(free_bank(name, i), 1)
                    return evacuate

                def silu(g, i):
                    name = f"z{g}"
                    wait_chunk(act, l, CI[name])
                    if (g, i) == (3, 0):
                        wait_read(act, l, ("ml_scores", 3))
                    if (g, i) == (2, 0):
                        wait_job(act, l, ("rkT", 1))
                    if (g, i) == (0, 0):
                        wait_job(act, l, ("retT", 1))
                    act.activation(yT[:, 4 * g + 2 * i:4 * g + 2 * i + 2, :], A(name, i).rearrange("p (j t) -> p j t", j=2),
                                   ACT.Silu).then_inc(acc_sem(name), 1)

                steps = {"normalise": normalise, "rotary": rotary, "x_hi": x_hi_, "y_hi": y_hi_, "memk": feat("memk", mKT),
                         "cq": feat("cq", cQT), "lx": lx, "mem_exp": mem_exp, "mem_pT": mem_pT,
                         "mla_exp": mla_exp, "mla_pT": mla_pT, "silu_conv": silu_conv, "akv": akv, "aq": aq,
                         "ml_q": pair("ml_q", lqT), "ml_k": pair("ml_k", lkT), "softplus": softplus,
                         "gate_floor": gate_floor, "ml_decay": ml_decay, "lv": lv, "lo": lo_, "rv": rv_,
                         "kpeT": kpeT, "mla_kn": pair("mla_kn", knT), "mla_qn": pair("mla_qn", qnT),
                         "mla_v": mla_v, "qrT": qrT_, "rqT": turned("rqT", rqT), "rkT": turned("rkT", rkT),
                         "silu": silu}
                for t in range(SLOTS):
                    c, k = divmod(t, KT)
                    w, s = CHUNKS[c][1], (t // 2) % RAW
                    if t % 2 == 0:
                        act.wait_ge(raw_full[s].sem, raw_full[s].at(l, t // 2 // RAW))
                    act.wait_ge(tile_used.sem, tile_used.at(l, t - RING))
                    act.activation(hi[:, t % RING, 0:w], raw[:, s, (t % 2) * w:(t % 2 + 1) * w], ACT.Copy)\
                       .then_inc(hi_done.sem, 1)
                    for name, *args in ACT_AT.get(t, ()):
                        steps[name](*args)
                assert links[0] == ACT_LINKS, links
            act.wait_ge(lo_done.sem, lo_done.at(DEPTH - 1, SLOTS - 1))
            act.sem_inc(hi_done.sem, AHEAD)

            act.wait_ge(ln_done.sem, ln_done.at(DEPTH - 1, 0))
            for b in range(8):
                cb, i = divmod(b, 2)
                blk = X[:, i, cb * 512:(cb + 1) * 512]
                act.activation(blk, blk, ACT.Identity, scale=ln_rstd[:, i:i + 1], bias=ln_shift[:, i:i + 1])\
                   .then_inc(final_normed.sem, 1)

        @block.tensor
        def _(pe):
            pe.sem_inc(tile_used.sem, RING)

            with pe.Fori(0, DEPTH) as l:
                def take(*job):
                    b, u = bank_of(job)
                    stand_alone(pe)
                    pe.wait_ge(bank_read[b].sem, bank_read[b].at(l, u - 1))
                    return work[:, b, :]

                def turn(dst, src):
                    return pe.transpose(dst, src, ident[0:src.shape[0], 0:src.shape[0]])

                def xT(j):
                    pe.wait_ge(ident_in.sem, 16)
                    pe.wait_ge(x_done.sem, x_done.at(l, 2 * (j // 2) + 1))
                    o = take("xT", j)
                    for kk in range(2):
                        for i in range(NT):
                            m = turn(o[:, kk * 256 + i * P:kk * 256 + (i + 1) * P],
                                     X[:, i, (2 * j + kk) * P:(2 * j + kk + 1) * P])
                    m.then_inc(job_done.sem, 1)

                def mem_scores(h):
                    if h == 0:
                        wait_acc_read(pe, l, CI["memk"])
                        wait_acc_read(pe, l, CI["cq"])
                    o = take("mem_scores", h)
                    for i in range(NT):
                        m = pe.matmul(o[:, i * 256:(i + 1) * 256], cQT[:, h, i * P:(i + 1) * P], mKT[:, h, :],
                                      start=True, stop=True)
                    m.then_inc(job_done.sem, 1)

                def mem_pT(h):
                    pe.wait_ge(prob_done.sem, prob_done.at(l, h))
                    o = take("mem_pT", h)
                    for kt in range(2):
                        for i in range(NT):
                            m = turn(o[:, kt * 256 + i * P:kt * 256 + (i + 1) * P],
                                     prob[:, h % 2, i * 256 + kt * P:i * 256 + (kt + 1) * P])
                    m.then_inc(job_done.sem, 1)

                def mem_out(q):
                    wait_acc_read(pe, l, CI["memv"])
                    wait_read(pe, l, ("mem_pT", 2 * q), ("mem_pT", 2 * q + 1))
                    o = take("mem_out", q)
                    for h in (2 * q, 2 * q + 1):
                        for kt in range(2):
                            m = pe.matmul(o[:, (h % 2) * 256:(h % 2 + 1) * 256], mV[:, kt, h * HD:(h + 1) * HD],
                                          probT[:, h % 2, kt * 256:(kt + 1) * 256], start=kt == 0, stop=kt == 1)
                    m.then_inc(job_done.sem, 1)

                def ml_proj(name, which):
                    def project(q):
                        if q == 0:
                            pe.wait_ge(lw_in.sem, lw_in.at(l, 0))
                        pe.wait_ge(xc_done.sem, xc_done.at(l, q))
                        o = take(name, q)
                        for h in (2 * q, 2 * q + 1):
                            m = pe.matmul(o[:, (h % 2) * 256:(h % 2 + 1) * 256], lw[:, which, h, :], xcT[:, h, :],
                                          start=True, stop=True)
                        m.then_inc(job_done.sem, 1)
                    return project

                def gateT(_):
                    wait_acc_read(pe, l, CI["akv"])
                    o = take("gateT", 0)
                    for g in range(2):
                        for i in range(NT):
                            m = turn(o[0:HEADS, g * 256 + i * P:g * 256 + (i + 1) * P],
                                     small[:, i, ROT + g * HEADS:ROT + (g + 1) * HEADS])
                    m.then_inc(job_done.sem, 1)

                def gate_cols(_):
                    pe.wait_ge(scan_done.sem, scan_done.at(l, 0))
                    pe.wait_ge(floor_done.sem, floor_done.at(l, 0))
                    o = take("gate_cols", 0)
                    stand_alone(pe)
                    for g in range(2):
                        for i in range(NT):
                            m = turn(o[:, (2 * g + i) * HEADS:(2 * g + i + 1) * HEADS],
                                     row[3 * g][:, i * P:(i + 1) * P])
                    m.then_inc(job_done.sem, 1)

                def m_rows(q):
                    o = take("m_rows", q)
                    for h in (2 * q, 2 * q + 1):
                        m = pe.matmul(o[:, (h % 2) * 256:(h % 2 + 1) * 256],
                                      ident[0:HEADS, h:h + 1].to_broadcast([HEADS, P]), row[1], start=True, stop=True)
                    m.then_inc(job_done.sem, 1)

                def cT_(i):
                    pe.wait_ge(c_normed.sem, c_normed.at(l, 1))
                    o = take("cT", i)
                    for j in range(4):
                        m = turn(o[:, j * P:(j + 1) * P], cqn[:, i, j * P:(j + 1) * P])
                    m.then_inc(job_done.sem, 1)

                def kpeT(_):
                    pe.wait_ge(kpe_done.sem, kpe_done.at(l, 0))
                    o = take("kpeT", 0)
                    for i in range(NT):
                        m = turn(o[:, i * P:(i + 1) * P], krr[:, i, :])
                    m.then_inc(job_done.sem, 1)

                def causal_scores(o, kT_, qT_, h):
                    pe.matmul(o[:, 0:256], kT_[:, h, 0:P], qT_[:, h, :], start=True, stop=True)
                    return pe.matmul(o[:, 256:TRI], kT_[:, h, P:2 * P], qT_[:, h, P:2 * P], start=True, stop=True)

                def ml_scores(h):
                    if h == 0:
                        wait_read(pe, l, ("ml_q", 0), ("ml_q", 1), ("ml_k", 0), ("ml_k", 1))
                    causal_scores(take("ml_scores", h), lkT, lqT, h).then_inc(job_done.sem, 1)

                def ml_out(h):
                    if h == 0:
                        wait_acc_read(pe, l, CI["lv"])
                    wait_read(pe, l, ("ml_scores", h))
                    o = take("ml_out", h)
                    pt, e = probT[:, h % 2, :], HD + 1
                    pe.matmul(o[:, 0:e], pt[:, 0:P], lv1[:, 0, h, :], start=True, stop=True)
                    pe.matmul(o[:, e:2 * e], pt[:, P:2 * P], lv1[:, 0, h, :], start=True, stop=False)
                    pe.matmul(o[:, e:2 * e], pt[:, 2 * P:3 * P], lv1[:, 1, h, :], start=False, stop=True)\
                      .then_inc(job_done.sem, 1)

                def mla_qr(i):
                    pe.wait_ge(mlaw_in.sem, mlaw_in.at(l, 1))
                    wait_read(pe, l, ("cT", i))
                    o = take("mla_qr", i)
                    for k in range(3):
                        m = pe.matmul(o[:, 0:HEADS * ROT].rearrange("p (h e) -> p h e", h=HEADS),
                                      cT[:, k, i * P:(i + 1) * P], wuq[:, k, :, NOPE:], start=k == 0, stop=k == 2)
                    m.then_inc(job_done.sem, 1)

                def mla_kn(q):
                    o = take("mla_kn", q)
                    for h in (2 * q, 2 * q + 1):
                        m = pe.matmul(o[:, (h % 2) * 256:(h % 2 + 1) * 256], wukv[:, h, 0, :], cT[:, 3, :],
                                      start=True, stop=True)
                    m.then_inc(job_done.sem, 1)

                def mla_qn(q):
                    o = take("mla_qn", q)
                    for h in (2 * q, 2 * q + 1):
                        for k in range(3):
                            m = pe.matmul(o[:, (h % 2) * 256:(h % 2 + 1) * 256], wuq[:, k, h, 0:NOPE], cT[:, k, :],
                                          start=k == 0, stop=k == 2)
                    m.then_inc(job_done.sem, 1)

                def mla_v(i):
                    o = take("mla_v", i)
                    pe.matmul(o.rearrange("p (h e) -> p h e", h=HEADS), cT[:, 3, i * P:(i + 1) * P], wukv[:, :, 1, :],
                              start=True, stop=True).then_inc(job_done.sem, 1)

                def qrT_(_):
                    pe.wait_ge(qr_done.sem, qr_done.at(l, 1))
                    o = take("qrT", 0)
                    for g in range(2):
                        for i in range(NT):
                            m = turn(o[:, g * 256 + i * P:g * 256 + (i + 1) * P], qr[:, i, g * P:(g + 1) * P])
                    m.then_inc(job_done.sem, 1)

                def cellT(q):
                    pe.wait_ge(cell_done.sem, cell_done.at(l, 0))
                    o = take("cellT", q)
                    for h in (2 * q, 2 * q + 1):
                        for i in range(NT):
                            m = turn(o[:, (h % 2) * 256 + i * P:(h % 2) * 256 + (i + 1) * P],
                                     cell[:, i, h * HD:(h + 1) * HD])
                    m.then_inc(job_done.sem, 1)

                def mla_scores(h):
                    if h == 0:
                        wait_read(pe, l, ("mla_kn", 0), ("mla_kn", 1), ("mla_qn", 0), ("mla_qn", 1),
                                  ("kpeT", 0), ("qrT", 0))
                        stand_alone(pe)
                    o = take("mla_scores", h)
                    r = slice((h % 2) * ROT, (h % 2 + 1) * ROT)
                    for i, (c0, c1) in enumerate(((0, P), (P, TRI))):
                        q = slice(i * P, (i + 1) * P)
                        pe.matmul(o[:, c0:c1], qnT[:, h, q], knT[:, h, 0:c1 - c0], start=True, stop=False)
                        m = pe.matmul(o[:, c0:c1], qrT[r, h // 2, q], krT[r, 0:c1 - c0], start=False, stop=True)
                    m.then_inc(job_done.sem, 1)

                def mla_pT(h):
                    pe.wait_ge(prob_done.sem, prob_done.at(l, HEADS + h))
                    o = take("mla_pT", h)
                    for j in range(3):
                        m = turn(o[:, j * P:(j + 1) * P], prob[:, h % 2, j * P:(j + 1) * P])
                    m.then_inc(job_done.sem, 1)

                def mla_out(q):
                    wait_read(pe, l, ("mla_v", 0), ("mla_v", 1), ("mla_pT", 2 * q), ("mla_pT", 2 * q + 1))
                    stand_alone(pe)
                    o = take("mla_out", q)
                    for h in (2 * q, 2 * q + 1):
                        c = (h % 2) * 256
                        pe.matmul(o[:, c:c + 256], mlaV[:, 0, h * HD:(h + 1) * HD], probT[:, h % 2, 0:256],
                                  start=True, stop=False, skip_group_check=True)
                        m = pe.matmul(o[:, c + P:c + 256], mlaV[:, 1, h * HD:(h + 1) * HD], probT[:, h % 2, 256:TRI],
                                      start=False, stop=True, skip_group_check=True)
                    m.then_inc(job_done.sem, 1)

                def turn_heads(name, src):
                    def turned(i):
                        pe.wait_ge(roped.sem, roped.at(l, i + (2 if name == "rkT" else 0)))
                        o = take(name, i)
                        for h in range(HEADS):
                            m = turn(o[:, h * P:(h + 1) * P], src[:, i, h * HD:(h + 1) * HD])
                        m.then_inc(job_done.sem, 1)
                    return turned

                def ret_scores(h):
                    if h == 0:
                        wait_read(pe, l, ("rqT", 0), ("rqT", 1), ("rkT", 0), ("rkT", 1))
                        stand_alone(pe)
                    causal_scores(take("ret_scores", h), rkT, rqT, h).then_inc(job_done.sem, 1)

                def ret_out(q):
                    wait_acc_read(pe, l, CI["rv"])
                    wait_read(pe, l, ("ret_scores", 2 * q), ("ret_scores", 2 * q + 1))
                    o = take("ret_out", q)
                    for h in (2 * q, 2 * q + 1):
                        pt, c, v = probT[:, h % 2, :], (h % 2) * 256, slice(h * HD, (h + 1) * HD)
                        pe.matmul(o[:, c:c + P], pt[:, 0:P], rv[:, 0, v], start=True, stop=True)
                        pe.matmul(o[:, c + P:c + 256], pt[:, P:2 * P], rv[:, 0, v], start=True, stop=False)
                        m = pe.matmul(o[:, c + P:c + 256], pt[:, 2 * P:3 * P], rv[:, 1, v], start=False, stop=True)
                    m.then_inc(job_done.sem, 1)

                def retT_(q):
                    wait_read(pe, l, ("ret_out", q))
                    o = take("retT", q)
                    for h in (2 * q, 2 * q + 1):
                        for i in range(NT):
                            m = turn(o[:, (h % 2) * 256 + i * P:(h % 2) * 256 + (i + 1) * P],
                                     retn[:, i, h * HD:(h + 1) * HD])
                    m.then_inc(job_done.sem, 1)

                steps = {"xT": xT, "mem_scores": mem_scores, "mem_pT": mem_pT, "mem_out": mem_out,
                         "ml_q": ml_proj("ml_q", 0), "ml_k": ml_proj("ml_k", 1), "gateT": gateT,
                         "gate_cols": gate_cols, "m_rows": m_rows, "cT": cT_, "kpeT": kpeT,
                         "ml_scores": ml_scores, "ml_out": ml_out, "mla_qr": mla_qr, "mla_kn": mla_kn,
                         "mla_qn": mla_qn, "mla_v": mla_v, "qrT": qrT_, "cellT": cellT,
                         "mla_scores": mla_scores, "mla_pT": mla_pT, "mla_out": mla_out,
                         "rqT": turn_heads("rqT", rqt), "rkT": turn_heads("rkT", rkt),
                         "ret_scores": ret_scores, "ret_out": ret_out, "retT": retT_}

                for t in range(SLOTS):
                    c, k = divmod(t, KT)
                    name, w, layout = CHUNKS[c]
                    s, p = t % RING, c % 2
                    ah, al = ((mh, ml) if c < 2 else (xh, xl) if c < OUT0 else (y_part(0, k // 2), y_part(1, k // 2)))
                    kk = k % 2 if c >= OUT0 else k
                    if k == 0:
                        pe.wait_ge(acc_read[p].sem, acc_read[p].at(l, (c // 2) * 2 - 1))
                    if c == 0 and k < KT // 2 and k % 2 == 0:
                        pe.wait_ge(mem_dve.sem, k // 2 + 1)
                    if c == 0 and k >= KT // 2 and k % 4 == 0:
                        pe.wait_ge(mem_pool.sem, k // 4 - 1)
                    if c == 2 and k % 2 == 0:
                        wait_read(pe, l, ("xT", k // 2))
                    if c == OUT0 and k % 2 == 0:
                        pe.wait_ge(y_lo.sem, y_lo.at(l, k // 2))
                    pe.wait_ge(hi_done.sem, hi_done.at(l, t))
                    if layout == "tok":
                        for i in range(NT):
                            o, q = acc[:, p, i, 0:w], slice(i * P, (i + 1) * P)
                            pe.matmul(o, ah[:, kk, q], hi[:, s, 0:w], start=k == 0, stop=False)
                            pe.matmul(o, al[:, kk, q], hi[:, s, 0:w], start=False, stop=False)
                        pe.wait_ge(lo_done.sem, lo_done.at(l, t))
                        for i in range(NT):
                            m = pe.matmul(acc[:, p, i, 0:w], ah[:, kk, i * P:(i + 1) * P], lo[:, s, 0:w],
                                          start=False, stop=k == KT - 1)
                    else:
                        for j in range(4):
                            o, q = acc[:, p, j // 2, (j % 2) * 256:(j % 2 + 1) * 256], slice(j * P, (j + 1) * P)
                            pe.matmul(o, hi[:, s, q], ah[:, kk, :], start=k == 0 and j % 2 == 0, stop=False,
                                      skip_group_check=True)
                            pe.matmul(o, hi[:, s, q], al[:, kk, :], start=False, stop=False, skip_group_check=True)
                        pe.wait_ge(lo_done.sem, lo_done.at(l, t))
                        for j in range(4):
                            o, q = acc[:, p, j // 2, (j % 2) * 256:(j % 2 + 1) * 256], slice(j * P, (j + 1) * P)
                            m = pe.matmul(o, lo[:, s, q], ah[:, kk, :], start=False, stop=k == KT - 1,
                                          skip_group_check=True)
                    m.then_inc(tile_used.sem, 1)
                    for step, *args in PE_AT.get(t, ()):
                        steps[step](*args)

        @block.vector
        def _(dve):
            for p in range(2):
                dve.sem_inc(acc_read[p].sem, 2)
            for b in range(NBANK):
                dve.sem_inc(bank_read[b].sem, 1)
            dve.sem_inc(lo_done.sem, 2 * RAW)
            dve.memset(half[:, :], -0.5).then_inc(ready.sem, 1)
            dve.memset(ln_shift[:, :], 0.0)
            dve.memset(ln_rstd[:, :], 1.0).then_inc(ln_done.sem, 1)

            links = [0]

            def link0(ins):
                ins.then_inc(dve_own.sem, 1)
                links[0] += 1
                dve.wait_ge(dve_own.sem, links[0])

            def take_lo(l, t):
                w, s = CHUNKS[t % SLOTS // KT][1], (t // 2) % RAW
                dve.wait_ge(hi_done.sem, hi_done.at(l, t))
                dve.wait_ge(tile_used.sem, tile_used.at(l, t - RING))
                dve.tensor_tensor(lo[:, t % RING, 0:w], raw[:, s, (t % 2) * w:(t % 2 + 1) * w],
                                  hi[:, t % RING, 0:w].bitcast(F32), ALU.subtract).then_inc(lo_done.sem, 1)

            for j in range(4):
                k, m2 = 2 * j, memT[j // 2][:, (j % 2) * 512:(j % 2 + 1) * 512].rearrange("p (k t) -> p k t", k=2)
                dve.wait_ge(memb_in[j // 2].sem, 16)
                link0(dve.tensor_copy(mh[:, k:k + 2, :], m2))
                dve.tensor_tensor(ml[:, k:k + 2, :], m2, mh[:, k:k + 2, :].bitcast(F32), ALU.subtract)\
                   .then_inc(mem_dve.sem, 1)
                for t in {1: (0, 1), 2: (2,), 3: (3,)}.get(j, ()):
                    take_lo(0, t)
            assert links[0] == DVE_LINKS_BEFORE, links

            with dve.Fori(0, DEPTH) as l:
                links = [0]

                def link(ins):
                    ins.then_inc(dve_own.sem, 1)
                    links[0] += 1
                    dve.wait_ge(dve_own.sem, dve_own.at(l, links[0] - 1))

                def angles_(n):
                    turns, magic = 1.0 / (2.0 * np.pi), 12582912.0
                    if n == 0:
                        dve.wait_ge(rotary_in.sem, 2 * 16)
                        link(dve.tensor_copy(rinv[:, 0, :], pos[:, :]))
                        for i in range(NT):
                            last = dve.tensor_scalar(turn1[:, i, :], freq[:, :], rinv[:, 0, i:i + 1], None, ALU.mult)
                        link(last)
                    if n == 1:
                        dve.tensor_scalar(whole[:, 0, :, :], turn1, turns, None, ALU.mult)
                        link(dve.tensor_scalar(whole[:, 1, :, :], turn1, turns, 0.25, ALU.mult, ALU.add))
                    if n in (2, 3):
                        link(dve.tensor_scalar(whole, whole, (magic, -magic)[n - 2], None, ALU.add))
                    if n in (4, 5, 6):
                        src = turn1.unsqueeze(1).to_broadcast([P, 2, NT, FR + FM]) if n == 4 else angle
                        link(dve.scalar_tensor_tensor(angle, whole, -two_pi_parts()[n - 4], src, ALU.mult, ALU.add))
                    if n == 7:
                        link(dve.tensor_scalar(angle[:, 1, :, :], angle[:, 1, :, :], 0.5 * np.pi, None, ALU.add))
                        dve.tensor_scalar(angle, angle, PI_IN, -PI_IN, ALU.min, ALU.max).then_inc(angles.sem, 1)

                def x_lo(j):
                    dve.wait_ge(x_hi.sem, x_hi.at(l, j))
                    dve.tensor_tensor(xl[:, 2 * j:2 * j + 2, :], bank(("xT", j)).rearrange("p (k t) -> p k t", k=2),
                                      xh[:, 2 * j:2 * j + 2, :].bitcast(F32), ALU.subtract)\
                       .then_inc(free_bank("xT", j), 1)

                def y_lo_(j):
                    k = OUT_ORDER[2 * j]
                    dve.wait_ge(y_hi.sem, y_hi.at(l, j))
                    dve.tensor_tensor(y_part(1, j), yT[:, k:k + 2, :], y_part(0, j).bitcast(F32),
                                      ALU.subtract).then_inc(y_lo.sem, 1)

                def memv(i):
                    wait_chunk(dve, l, CI["memv"])
                    dve.tensor_copy(mV[:, i, :], A("memv", i)).then_inc(acc_sem("memv"), 1)

                def mem_max(h):
                    wait_job(dve, l, ("mem_scores", h))
                    link(dve.tensor_reduce(nmax[:, h % 2, :], bank(("mem_scores", h)).rearrange("p (i k) -> p i k", i=NT),
                                           AX.X, ALU.max, negate=True))
                    dve.tensor_scalar(nmax[:, h % 2, :], nmax[:, h % 2, :], HEAD_SCALE, None, ALU.mult)\
                       .then_inc(max_done.sem, 1)

                def mem_norm(h):
                    wait_read(dve, l, ("mem_scores", h))
                    link(dve.reciprocal(rinv[:, h % 2, :], rsum[:, h % 2, :]))
                    for i in range(NT):
                        pr = prob[:, h % 2, i * 256:(i + 1) * 256]
                        m = dve.tensor_scalar(pr, pr, rinv[:, h % 2, i:i + 1], None, ALU.mult)
                    m.then_inc(prob_done.sem, 1)

                def out_pair(name, dst):
                    def evacuate(q):
                        wait_job(dve, l, (name, q))
                        dve.tensor_copy(dst[:, 2 * q:2 * q + 2, :], bank((name, q)).rearrange("p (j t) -> p j t", j=2))\
                           .then_inc(free_bank(name, q), 1)
                    return evacuate

                def conv(s):
                    if s == 0:
                        dve.wait_ge(cols_in.sem, cols_in.at(l, 0))
                        dve.memset(LX[:, :, 0:PAD], 0.0).then_inc(lx_pad.sem, 1)
                        dve.wait_ge(lx_pad.sem, lx_pad.at(l, 0))
                        wait_acc_read(dve, l, CI["lx"])
                    j, tap0 = divmod(s, 2)
                    for tap in (2 * tap0, 2 * tap0 + 1):
                        wcol = cols[:, C_CONVW + tap * 4 + j:C_CONVW + tap * 4 + j + 1]
                        if tap == 0:
                            link(dve.tensor_scalar(xcT[:, j, :], LX[:, j, 0:SEQ], wcol, None, ALU.mult))
                        else:
                            m = dve.scalar_tensor_tensor(xcT[:, j, :], LX[:, j, tap:tap + SEQ], wcol, xcT[:, j, :],
                                                         ALU.mult, ALU.add)
                            if (j, tap) == (3, 3):
                                m.then_inc(conv_done.sem, 1)
                            else:
                                link(m)

                def rms_(r):
                    dve.wait_ge(sq_done.sem, sq_done.at(l, r))
                    dve.tensor_scalar(sumsq[:, r, :], sumsq[:, r, :], 1.0 / (KVRANK, QRANK)[r], RMS_EPS,
                                      ALU.mult, ALU.add).then_inc(var_done.sem, 1)

                def ckv(_):
                    dve.wait_ge(rms_done.sem, rms_done.at(l, 0))
                    for i in range(NT):
                        dve.tensor_scalar(cqn[:, i, QRANK:QRANK + KVRANK], A("akv", i)[:, 0:KVRANK], rms[:, 0, i:i + 1],
                                          None, ALU.mult).then_inc(acc_sem("akv"), 1)

                def cqn_(i):
                    dve.wait_ge(rms_done.sem, rms_done.at(l, 1))
                    dve.tensor_scalar(cqn[:, i, 0:QRANK], A("aq", i)[:, 0:QRANK], rms[:, 1, i:i + 1],
                                      None, ALU.mult).then_inc(acc_sem("aq"), 1)
                    if i:
                        wait_acc_read(dve, l, CI["aq"])
                        wait_acc_read(dve, l, CI["akv"])
                        dve.sem_inc(c_normed.sem, 2)

                def kpe_rope(_):
                    dve.wait_ge(tables.sem, tables.at(l, 0))
                    for i in range(NT):
                        src = small[:, i, 0:ROT].rearrange("p (a f) -> p a f", a=2)
                        t1 = tmp[:, i * P:i * P + ROT].rearrange("p (a f) -> p a f", a=2)
                        t2 = tmp[:, i * P + ROT:i * P + P].rearrange("p (a f) -> p a f", a=2)
                        dve.tensor_tensor(t1, src, cos[:, i, FR:].unsqueeze(1).to_broadcast([P, 2, FM]), ALU.mult)
                        link(dve.tensor_tensor(t2, src[:, ::-1, :], sin[:, :, i, FR:], ALU.mult))
                    for i in range(NT):
                        t1, t2 = tmp[:, i * P:i * P + ROT], tmp[:, i * P + ROT:i * P + P]
                        m = dve.tensor_tensor(krr[:, i, :].rearrange("p (d e) -> p d e", d=2),
                                              t1.unsqueeze(1).to_broadcast([P, 2, ROT]),
                                              t2.unsqueeze(1).to_broadcast([P, 2, ROT]), ALU.add)
                    m.then_inc(kpe_done.sem, 1)

                def gates(_):
                    wait_job(dve, l, ("gateT", 0), ("ml_k", 1))
                    dve.wait_ge(cols_in.sem, cols_in.at(l, 0))
                    o = bank(("gateT", 0))
                    dve.tensor_scalar(row[0], o[0:HEADS, 0:SEQ], cols[0:HEADS, C_IB:C_IB + 1], None, ALU.add)
                    link(dve.tensor_scalar(row[1], o[0:HEADS, SEQ:2 * SEQ], cols[0:HEADS, C_FB:C_FB + 1], None, ALU.add))
                    dve.sem_inc(free_bank("gateT", 0), 1)
                    dve.scalar_tensor_tensor(row[2], row[1], -1.0, row[1], ALU.mult, ALU.max).then_inc(gate_abs.sem, 1)

                def gate_scan(_):
                    link(dve.tensor_scalar(row[1], row[1], 0.0, None, ALU.min))
                    dve.wait_ge(softplus_done.sem, softplus_done.at(l, 0))
                    link(dve.tensor_tensor_scan(row[3], row[1], row[2], 0.0, ALU.add, ALU.subtract))
                    link(dve.tensor_tensor(row[0], row[0], row[3], ALU.subtract))
                    link(dve.tensor_tensor_scan(row[1], row[0], row[0], 0.0, ALU.max, ALU.max))
                    dve.tensor_tensor(row[3], row[3], row[1], ALU.add).then_inc(scan_done.sem, 1)

                def skip(_):
                    wait_job(dve, l, ("ml_k", 1))
                    for j in range(4):
                        m = dve.tensor_scalar(mls[:, j, :], xcT[:, j, :], cols[:, C_SKIP + j:C_SKIP + j + 1], None, ALU.mult)
                    m.then_inc(skip_done.sem, 1)

                def ones(_):
                    wait_job(dve, l, ("mem_scores", HEADS - 1))
                    dve.memset(lv1[:, :, :, HD:HD + 1], 1.0).then_inc(ones_done.sem, 1)

                def cT_(i):
                    wait_job(dve, l, ("cT", i))
                    dve.tensor_tensor(cT[:, :, i * P:(i + 1) * P], bank(("cT", i)).rearrange("p (j t) -> p j t", j=4),
                                      cols[:, C_CG:C_CG + 4].unsqueeze(2).to_broadcast([P, 4, P]), ALU.mult)\
                       .then_inc(free_bank("cT", i), 1)

                def gate_cols(_):
                    wait_job(dve, l, ("gate_cols", 0))
                    dve.tensor_copy(gcol[:, :, :], bank(("gate_cols", 0))[:, 0:4 * HEADS].rearrange("p (g h) -> p g h", g=4))\
                       .then_inc(free_bank("gate_cols", 0), 1)

                def ml_gap(h):
                    q = h // 2
                    wait_job(dve, l, ("m_rows", q))
                    dve.wait_ge(const_in.sem, 16)
                    if h == 0:
                        wait_read(dve, l, ("gate_cols", 0))
                    if h >= 2:
                        wait_read(dve, l, ("ml_scores", h - 2))
                    o = bank(("m_rows", q))[:, (h % 2) * 256:(h % 2 + 1) * 256]
                    dve.scalar_tensor_tensor(gap[:, h % 2, 0:256], o, gcol[:, 0, h:h + 1], big[:, 0:256],
                                             ALU.subtract, ALU.max)
                    dve.scalar_tensor_tensor(gap[:, h % 2, 256:TRI], o[:, P:256], gcol[:, 1, h:h + 1], big[:, 256:TRI],
                                             ALU.subtract, ALU.max).then_inc(gap_done.sem, 1)
                    if h % 2:
                        dve.wait_ge(gap_done.sem, gap_done.at(l, h))
                        dve.sem_inc(free_bank("m_rows", q), 1)

                def ml_weigh(h):
                    wait_job(dve, l, ("ml_scores", h), *([("ml_out", h - 2)] if h >= 2 else []))
                    dve.wait_ge(decay_done.sem, decay_done.at(l, h))
                    dve.scalar_tensor_tensor(probT[:, h % 2, 0:TRI], bank(("ml_scores", h))[:, 0:TRI], HEAD_SCALE,
                                             gap[:, h % 2, :], ALU.mult, ALU.mult).then_inc(free_bank("ml_scores", h), 1)

                def ml_out(h):
                    wait_job(dve, l, ("ml_out", h), ("ml_scores", HEADS - 1))
                    o = bank(("ml_out", h))[:, 0:NT * (HD + 1)].rearrange("p (i e) -> p i e", i=NT)
                    d = den[:, h % 2, :]
                    link(dve.scalar_tensor_tensor(d, o[:, :, HD], -1.0, gcol[:, 2:4, h], ALU.mult, ALU.max))
                    link(dve.tensor_tensor(d, o[:, :, HD], d, ALU.max))
                    link(dve.reciprocal(d, d))
                    for i in range(NT):
                        m = dve.tensor_scalar(cell[:, i, h * HD:(h + 1) * HD], o[:, i, 0:HD], den[:, h % 2, i:i + 1],
                                              None, ALU.mult)
                    m.then_inc(free_bank("ml_out", h), 1)

                def cell_gate(i):
                    wait_acc_read(dve, l, CI["lo"])
                    wait_read(dve, l, ("ml_out", HEADS - 1))
                    link(dve.tensor_tensor(cell[:, i, :], cell[:, i, :], sigo[:, i, :], ALU.mult))

                def cell_stats(i):
                    for h in range(HEADS):
                        m = dve.bn_stats(stats[:, i * HEADS + h, :], cell[:, i, h * HD:(h + 1) * HD])
                    link(m)
                    stand_alone(dve)
                    for h in range(HEADS):
                        m = dve.bn_aggr(mv[:, i * HEADS + h, :], stats[:, i * HEADS + h, :])
                    link(m)
                    if i:
                        dve.tensor_scalar(stats[:, :, 0], mv[:, :, 1], LN_EPS, None, ALU.add).then_inc(cell_var.sem, 1)

                def cell_norm(i):
                    dve.wait_ge(cell_pow.sem, cell_pow.at(l, 0))
                    for h in range(HEADS):
                        n, s = i * HEADS + h, cell[:, i, h * HD:(h + 1) * HD]
                        m = dve.tensor_scalar(s, s, mv[:, n, 0:1], rstd[:, n:n + 1], ALU.subtract, ALU.mult)
                    if i:
                        m.then_inc(cell_done.sem, 1)

                def cellT(q):
                    wait_job(dve, l, ("cellT", q))
                    dve.wait_ge(skip_done.sem, skip_done.at(l, 0))
                    for h in (2 * q, 2 * q + 1):
                        m = dve.scalar_tensor_tensor(mls[:, h, :], bank(("cellT", q))[:, (h % 2) * 256:(h % 2 + 1) * 256],
                                                     cols[:, C_MLG + h:C_MLG + h + 1], mls[:, h, :], ALU.mult, ALU.add)
                    m.then_inc(free_bank("cellT", q), 1)

                def rope(dst, src, cos, sin, halfw):
                    n = dst.shape[1] // (2 * halfw)
                    d = dst.rearrange("p (h a f) -> p h a f", h=n, a=2)
                    s = src.rearrange("p (h a f) -> p h a f", h=n, a=2)
                    t = tmp[:, 0:n * 2 * halfw].rearrange("p (h a f) -> p h a f", h=n, a=2)
                    dve.tensor_tensor(d, s, cos.unsqueeze(1).unsqueeze(1).to_broadcast([P, n, 2, halfw]), ALU.mult)
                    return dve.tensor_tensor(t, s[:, :, ::-1, :], sin.unsqueeze(1).to_broadcast([P, n, 2, halfw]), ALU.mult)

                def q_rope(i):
                    wait_job(dve, l, ("mla_qr", i))
                    link(rope(qr[:, i, :], bank(("mla_qr", i))[:, 0:HEADS * ROT], cos[:, i, FR:], sin[:, :, i, FR:], FM))
                    dve.sem_inc(free_bank("mla_qr", i), 1)
                    dve.tensor_tensor(qr[:, i, :], qr[:, i, :], tmp[:, 0:HEADS * ROT], ALU.add).then_inc(qr_done.sem, 1)
                    dve.wait_ge(qr_done.sem, qr_done.at(l, i))

                def rope_ret(name, dst, n):
                    def go(i):
                        wait_chunk(dve, l, CI[name])
                        if name == "rq" and i == 0:
                            wait_job(dve, l, ("mla_qn", 1))
                        rope(dst[:, i, :], A(name, i), cos[:, i, 0:FR], sin[:, :, i, 0:FR], FR).then_inc(acc_sem(name), 1)
                        wait_acc_read(dve, l, CI[name], halves=i + 1)
                        dve.tensor_tensor(dst[:, i, :], dst[:, i, :], tmp[:, :], ALU.add).then_inc(roped.sem, 1)
                        dve.wait_ge(roped.sem, roped.at(l, n + i))
                    return go

                def mla_max(h):
                    wait_job(dve, l, ("mla_scores", h), *([("mla_pT", h - 2)] if h >= 2 else []))
                    dve.tensor_tensor(prob[:, h % 2, 0:TRI], bank(("mla_scores", h))[:, 0:TRI], tri, ALU.add)\
                       .then_inc(free_bank("mla_scores", h), 1)
                    wait_read(dve, l, ("mla_scores", h))
                    dve.tensor_reduce(nmax[:, h % 2, 0:1], prob[:, h % 2, 0:P], AX.X, ALU.max, negate=True)
                    link(dve.tensor_reduce(nmax[:, h % 2, 1:2], prob[:, h % 2, P:TRI], AX.X, ALU.max, negate=True))
                    dve.tensor_scalar(nmax[:, h % 2, :], nmax[:, h % 2, :], MLA_SCALE, None, ALU.mult)\
                       .then_inc(max_done.sem, 1)

                def mla_norm(h):
                    dve.wait_ge(exp_done.sem, exp_done.at(l, h))
                    link(dve.reciprocal(rinv[:, h % 2, :], rsum[:, h % 2, :]))
                    for i, (c0, c1) in enumerate(((0, P), (P, TRI))):
                        pr = prob[:, h % 2, c0:c1]
                        m = dve.tensor_scalar(pr, pr, rinv[:, h % 2, i:i + 1], None, ALU.mult)
                    m.then_inc(prob_done.sem, 1)

                def ret_weigh(h):
                    wait_job(dve, l, ("ret_scores", h), ("ret_out", 0) if h >= 2 else ("mla_out", 1))
                    dve.tensor_tensor(probT[:, h % 2, 0:TRI], bank(("ret_scores", h))[:, 0:TRI], decay[:, h, :],
                                      ALU.mult).then_inc(free_bank("ret_scores", h), 1)

                def ret_block(q, n):
                    return bank(("ret_out", q))[:, n * HD:(n + 1) * HD]

                def ret_stats(q):
                    wait_job(dve, l, ("ret_out", q))
                    for n in range(4):
                        m = dve.bn_stats(stats[:, n, :], ret_block(q, n))
                    link(m)
                    stand_alone(dve)
                    for n in range(4):
                        m = dve.bn_aggr(mv[:, n, :], stats[:, n, :])
                    link(m)
                    dve.tensor_scalar(stats[:, 0:4, 0], mv[:, 0:4, 1], LN_EPS, None, ALU.add).then_inc(ret_var.sem, 1)

                def ret_norm(q):
                    dve.wait_ge(ret_pow.sem, ret_pow.at(l, q))
                    for n in range(4):
                        h, i = 2 * q + n // 2, n % 2
                        m = dve.tensor_scalar(retn[:, i, h * HD:(h + 1) * HD], ret_block(q, n), mv[:, n, 0:1],
                                              rstd[:, n:n + 1], ALU.subtract, ALU.mult)
                    m.then_inc(free_bank("ret_out", q), 1)

                def retT_(q):
                    wait_job(dve, l, ("retT", q))
                    for h in (2 * q, 2 * q + 1):
                        m = dve.tensor_scalar(retT[:, h, :], bank(("retT", q))[:, (h % 2) * 256:(h % 2 + 1) * 256],
                                              cols[:, C_RETG + h:C_RETG + h + 1], None, ALU.mult)
                    m.then_inc(free_bank("retT", q), 1)

                def gate(g, i):
                    src = {3: memo, 2: mls, 1: mlao, 0: retT}[g]
                    last = {3: "mem_out", 2: "cellT", 1: "mla_out", 0: "retT"}[g]
                    wait_acc_read(dve, l, CI[f"z{g}"], halves=i + 1)
                    wait_read(dve, l, (last, 1))
                    y = yT[:, 4 * g + 2 * i:4 * g + 2 * i + 2, :]
                    dve.tensor_tensor(y, y, src[:, 2 * i:2 * i + 2, :], ALU.mult).then_inc(gated.sem, 1)

                def residual(c):
                    name, w = CHUNKS[OUT0 + c][0], CHUNKS[OUT0 + c][1]
                    wait_chunk(dve, l, OUT0 + c)
                    for i in range(NT):
                        xc = X[:, i, OUTCOL[c]:OUTCOL[c] + w]
                        dve.scalar_tensor_tensor(xc, xc, ALPHA, A(name, i)[:, 0:w], ALU.mult, ALU.add)\
                           .then_inc(acc_sem(name), 1)
                    for i in range(NT):
                        wait_acc_read(dve, l, OUT0 + c, halves=i + 1)
                        m = dve.bn_stats(ln_stats[:, i, c, :], X[:, i, OUTCOL[c]:OUTCOL[c] + w])
                    return m

                steps = {"angles": angles_, "x_lo": x_lo, "y_lo": y_lo_, "memv": memv, "mem_max": mem_max, "mem_norm": mem_norm,
                         "mem_out": out_pair("mem_out", memo), "conv": conv, "rms": rms_, "ckv": ckv, "cqn": cqn_,
                         "kpe_rope": kpe_rope, "gates": gates, "gate_scan": gate_scan, "skip": skip, "ones": ones,
                         "cT": cT_, "gate_cols": gate_cols, "ml_gap": ml_gap, "ml_weigh": ml_weigh, "ml_out": ml_out,
                         "cell_gate": cell_gate, "cell_stats": cell_stats, "cell_norm": cell_norm, "cellT": cellT,
                         "q_rope": q_rope, "rope_rq": rope_ret("rq", rqt, 0), "rope_rk": rope_ret("rk", rkt, 2),
                         "mla_max": mla_max, "mla_norm": mla_norm, "mla_out": out_pair("mla_out", mlao),
                         "ret_weigh": ret_weigh, "ret_stats": ret_stats, "ret_norm": ret_norm, "retT": retT_,
                         "gate": gate, "residual": residual}
                for t in range(AHEAD, SLOTS + AHEAD):
                    take_lo(l, t)
                    for name, *args in DVE_AT.get(t, ()):
                        steps[name](*args)

                link(residual(NOUT - 1))
                stand_alone(dve)
                for i in range(NT):
                    m = dve.bn_aggr(ln_mv[:, i, :], ln_stats[:, i, :, :].rearrange("p c s -> p (c s)"))
                link(m)
                dve.tensor_scalar(ln_stats[:, :, 0, 0], ln_mv[:, :, 1], LN_EPS, None, ALU.add).then_inc(ln_var.sem, 1)
                dve.wait_ge(ln_pow.sem, ln_pow.at(l, 0))
                dve.scalar_tensor_tensor(ln_shift[:, :], ln_mv[:, :, 0], -1.0, ln_rstd[:, :], ALU.mult, ALU.mult)\
                   .then_inc(ln_done.sem, 1)
                assert links[0] == DVE_LINKS, links

            dve.wait_ge(gb_in.sem, gb_in.at(DEPTH - 1, 0))
            for b in range(8):
                cb, i = divmod(b, 2)
                blk = X[:, i, cb * 512:(cb + 1) * 512]
                dve.wait_ge(final_normed.sem, b + 1)
                dve.tensor_tensor(blk, blk, gb[:, 0, cb * 512:(cb + 1) * 512], ALU.mult).then_inc(final_scaled.sem, 1)
                if b in DVE_BIAS:
                    dve.wait_ge(final_scaled.sem, b + 1)
                    dve.tensor_tensor(blk, blk, gb[:, 1, cb * 512:(cb + 1) * 512], ALU.add).then_inc(dve_biased.sem, 1)


def stream_columns(name):
    r = lambda at, n: list(range(at, at + n))
    if name == "memk":
        return r(0, W)
    if name == "memv":
        return r(W, W)
    if name == "akv":
        return r(COL["akv"], KVRANK + ROT) + r(COL["li"], 2 * HEADS)
    if name == "aq":
        return r(COL["aq"], QRANK)
    if name[0] == "z":
        return r(COL["z"] + int(name[1:]) * W, W)
    if name[:3] == "out":
        c = int(name[3:])
        return r(OUTCOL[c], CHUNKS[OUT0 + c][1])
    return r(COL[name], W)


def constants():
    f = np.float64
    k, q = np.arange(P)[:, None], np.arange(SEQ)[None, :]
    rel = q - k
    rel = np.concatenate([rel, rel[:, :P]], 1)
    gamma = 1.0 - 2.0 ** (-5.0 - np.arange(HEADS, dtype=f))
    dec = np.where(rel[None] >= 0, gamma[:, None, None] ** np.maximum(rel, 0)[None], 0.0) * HEAD_SCALE
    dec = dec.transpose(1, 0, 2).reshape(P, HEADS * TRI)
    big = np.where(rel >= 0, 0.0, MASKED)
    above = np.where(np.arange(P)[None, :] <= np.arange(P)[:, None], 0.0, -MASKED)
    tri = np.concatenate([above, np.zeros((P, P)), above], 1)
    freqs = np.concatenate([THETA ** (-np.arange(n, dtype=f) / n) for n in (FR, FM)])
    blocks = {"ident": np.eye(P), "const": np.concatenate([dec, tri, big], 1), "freq": np.tile(freqs, (P, 1))}
    return {name: v.astype(np.float32) for name, v in blocks.items()}


def kernel(**inputs):
    import concourse.bacc as _bacc
    from concourse.bass_utils import run_bass_kernel_spmd as _run

    g = {k: np.asarray(v) for k, v in inputs.items()}

    def stream(l):
        parts = []
        for name, w, _ in CHUNKS:
            m = g["w_mem_kv"] if name[:3] == "mem" else g["w_out"] if name[:3] == "out" else g["w_in"]
            order = OUT_ORDER if name[:3] == "out" else range(KT)
            t = m[l][:, stream_columns(name)].reshape(KT, P, w)[list(order)]
            parts.append(t.reshape(KT // 2, 2, P, w).transpose(0, 2, 1, 3).reshape(-1))
        return np.concatenate(parts)

    def columns(l):
        col = lambda v: v.reshape(-1, P).T
        bias = lambda v: np.concatenate([v, np.zeros(P - HEADS, v.dtype)])[:, None]
        return np.concatenate([col(g["ret_norm_g"][l]), col(g["mla_q_norm_g"][l]), col(g["mla_kv_norm_g"][l]),
                               col(g["ml_conv_w"][l].reshape(-1)), col(g["ml_conv_b"][l]), col(g["ml_skip"][l]),
                               col(g["ml_norm_g"][l]), bias(g["ml_i_bias"][l]), bias(g["ml_f_bias"][l])], 1).reshape(-1)

    arrays = {
        "x": g["x"].reshape(SEQ, D_MODEL),
        "pos": np.ascontiguousarray(g["positions"].reshape(NT, P).T),
        "mem_t": np.ascontiguousarray(g["mem"][0].T.reshape(KT, P, MEM_LEN).transpose(1, 0, 2).reshape(P, -1)),
        "w": np.stack([stream(l) for l in range(DEPTH)]),
        "cols": np.stack([columns(l) for l in range(DEPTH)]),
        "lw": np.stack([np.stack([g["ml_w_q"][l], g["ml_w_k"][l]]).transpose(2, 0, 1, 3).reshape(-1) for l in range(DEPTH)]),
        "wuq": np.stack([g["mla_w_uq"][l].reshape(3, P, -1).transpose(1, 0, 2).reshape(-1) for l in range(DEPTH)]),
        "wukv": np.stack([g["mla_w_ukv"][l].reshape(-1) for l in range(DEPTH)]),
        "gb": np.concatenate([g["ln_g"], g["ln_b"]], 1),
        **constants(),
    }
    nc = _bacc.Bacc("TRN2", target_bir_lowering=False, num_devices=1)
    maps, args = {}, {}
    for name, v in arrays.items():
        v = np.ascontiguousarray(v)
        maps[f"in_{name}"] = v
        args[name] = nc.dram_tensor(f"in_{name}", v.shape, mybir.dt.from_np(v.dtype), kind="ExternalInput").ap()
    out = nc.dram_tensor("out_x", (SEQ, D_MODEL), F32, kind="ExternalOutput").ap()
    build_trunk(nc, args, out)
    r = _run(nc, [maps], core_ids=[0])
    return r.results[0]["out_x"].reshape(1, SEQ, D_MODEL)
```

```python
from contextlib import ExitStack

import numpy as np

import concourse.bass as bass
from concourse import mybir

F32 = mybir.dt.float32
F32R = mybir.dt.float32r
I32 = mybir.dt.int32
ALU = mybir.AluOpType
ACT = mybir.ActivationFunctionType
AX = mybir.AxisListType

P = 128
DEPTH = 2
D_MODEL = 2048
SEQ = 256
MEM_LEN = 256
HEADS = 4
HD = 128
NOPE, ROT = 128, 64
QRANK, KVRANK = 384, 128
TAPS = 4
NT = SEQ // P
KT = D_MODEL // P
GROUPS = 4
W = HEADS * HD
THETA = 10000.0
LN_EPS, RMS_EPS = 1e-5, 1e-6
ALPHA = (2 * DEPTH) ** 0.25
MLA_SCALE = float(NOPE + ROT) ** -0.5
HEAD_SCALE = float(HD) ** -0.5
PAD = TAPS - 1
TRI = 3 * P
MASKED = 1e30

_sizes = (W, W, W, QRANK, KVRANK, ROT, W, W, W, HEADS, HEADS, W, GROUPS * W)
_names = ("rq", "rk", "rv", "aq", "akv", "ape", "lx", "lv", "lo", "li", "lf", "cq", "z")
COL = dict(zip(_names, np.concatenate([[0], np.cumsum(_sizes)[:-1]]).tolist()))

AKV_W = 256
SMALL = AKV_W - KVRANK
C_GATE, C_CQ = ROT, ROT + 2 * HEADS
QHEAD = SMALL - C_CQ
CHUNKS = [("memk", W, "feat"), ("memv", W, "tok"), ("lx", W, "feat"), ("cq", W, "feat"),
          ("akv", AKV_W, "tok"), ("aq", QRANK - QHEAD, "tok"), ("lv", W, "tok"), ("lo", W, "tok"),
          ("rq", W, "tok"), ("rk", W, "tok"), ("rv", W, "tok"),
          ("z3", W, "feat"), ("z2", W, "feat"), ("z1", W, "feat"), ("z0", W, "feat"),
          ("out0", 512, "tok"), ("out1", 512, "tok"), ("out2", 512, "tok"),
          ("out3", 256, "tok"), ("out4", 256, "tok")]
NCH = len(CHUNKS)
CI = {c[0]: i for i, c in enumerate(CHUNKS)}
OUT0 = CI["out0"]
OUTCOL = [0, 512, 1024, 1536, 1792]
NOUT = len(OUTCOL)
OUT_ORDER = [12, 13, 14, 15, 8, 9, 10, 11, 4, 5, 6, 7, 0, 1, 2, 3]
SLOTS = NCH * KT
PAIRS = SLOTS // 2
RAW = 4
RING = 5
AHEAD = 4
CHUNK_AT = np.concatenate([[0], np.cumsum([KT * P * w for _, w, _ in CHUNKS])]).tolist()

C_RETG, C_CG, C_CONVW, C_CONVB, C_SKIP, C_MLG, C_IB, C_FB = 0, 4, 8, 24, 28, 32, 36, 37
NCOLS = 38
K_DECAY = 0
K_TRI = K_DECAY + HEADS * TRI
K_BIG = K_TRI + TRI
NCONST = K_BIG + TRI
FR, FM = HD // 2, ROT // 2

PE_AT = {}


def _put(table, slot, *step):
    table.setdefault(slot, []).append(step)


for _j in range(8):
    _put(PE_AT, 16 + 2 * _j, "xT", _j)
for _h in range(HEADS):
    _put(PE_AT, 69 + 6 * _h, "mem_scores", _h)
    _put(PE_AT, (78, 84, 91, 98)[_h], "mem_pT", _h)
    _put(PE_AT, 153 + 6 * _h, "mla_scores", _h)
    _put(PE_AT, 162 + 6 * _h, "mla_pT", _h)
for _s, *_step in [
        (92, "mem_out", 0), (105, "mem_out", 1),
        (88, "ml_q", 0), (88, "ml_q", 1), (89, "ml_k", 0), (91, "ml_k", 1),
        (91, "gateT", 0), (104, "gate_cols", 0),
        (105, "cT", 0), (107, "cT", 1), (108, "kpeT", 0),
        (110, "ml_scores", 0), (112, "ml_scores", 1), (119, "ml_scores", 2), (121, "ml_scores", 3),
        (119, "ml_out", 0), (121, "ml_out", 1), (127, "ml_out", 2), (129, "ml_out", 3),
        (131, "mla_qr", 0), (132, "mla_qr", 1), (133, "mla_kn", 0), (135, "mla_kn", 1),
        (136, "mla_qn", 0), (138, "mla_qn", 1), (140, "mla_v", 0), (142, "mla_v", 1), (143, "qrT", 0),
        (150, "cellT", 0), (151, "cellT", 1),
        (154, "rqT", 0), (155, "rqT", 1), (170, "rkT", 0), (172, "rkT", 1),
        (174, "mla_out", 0), (186, "mla_out", 1),
        (188, "ret_scores", 0), (190, "ret_scores", 1), (198, "ret_scores", 2), (200, "ret_scores", 3),
        (197, "ret_out", 0), (207, "ret_out", 1), (209, "retT", 0), (219, "retT", 1)]:
    _put(PE_AT, _s, *_step)
JOBS = [step for slot in sorted(PE_AT) for step in PE_AT[slot]]
NJOBS = len(JOBS)
NBANK = 4
JOB = {step: j for j, step in enumerate(JOBS)}

ACT_AT = {}
for _j in range(8):
    _put(ACT_AT, 8 + 3 * _j // 2, "normalise", _j)
    _put(ACT_AT, 21 + 2 * _j, "x_hi", _j)
for _h in range(HEADS):
    _put(ACT_AT, 74 + 6 * _h, "mem_exp", _h)
    _put(ACT_AT, 84 + 6 * _h + _h // 2, "mem_pT", _h)
    _put(ACT_AT, 158 + 6 * _h, "mla_exp", _h)
    _put(ACT_AT, 167 + 6 * _h, "mla_pT", _h)
for _s, *_step in [
        (20, "memk", 0), (22, "memk", 1), (44, "rotary", 0), (52, "lx", 0), (53, "lx", 1),
        (65, "silu_conv", 0), (66, "silu_conv", 1), (68, "cq", 0), (69, "cq", 1), (84, "akv", 0), (85, "akv", 1),
        (93, "ml_q", 0), (94, "ml_q", 1), (95, "ml_k", 0), (95, "ml_k", 1),
        (97, "softplus", 0), (100, "gate_floor", 0), (100, "aq", 0), (101, "aq", 1),
        (111, "ml_decay", 0), (112, "ml_decay", 1), (113, "kpeT", 0), (119, "ml_decay", 2), (120, "ml_decay", 3),
        (116, "lv", 0), (117, "lv", 1), (122, "wukv", 0), (124, "wukv", 1), (126, "ckvT", 0), (132, "lo", 0), (133, "lo", 1),
        (138, "mla_kn", 0), (140, "mla_kn", 1), (141, "mla_qn", 0), (143, "mla_qn", 1),
        (145, "mla_v", 0), (147, "mla_v", 1), (149, "qrT", 0),
        (160, "rqT", 0), (161, "rqT", 1), (176, "rkT", 0), (178, "rkT", 1),
        (180, "rv", 0), (181, "rv", 1),
        (196, "silu", 3, 0), (197, "silu", 3, 1), (212, "silu", 2, 0), (213, "silu", 2, 1),
        (228, "silu", 1, 0), (229, "silu", 1, 1), (246, "silu", 0, 0), (247, "silu", 0, 1),
        (205, "y_hi", 0), (207, "y_hi", 1), (221, "y_hi", 2), (223, "y_hi", 3),
        (244, "y_hi", 4), (245, "y_hi", 5), (251, "y_hi", 6), (252, "y_hi", 7)]:
    _put(ACT_AT, _s, *_step)

DVE_AT = {}
for _j in range(8):
    _put(DVE_AT, 21 + 2 * _j, "x_lo", _j)
    _put(DVE_AT, 54 + _j, "conv", _j)
    _put(DVE_AT, 22 + 2 * _j, "angles", _j)
for _h in range(HEADS):
    _put(DVE_AT, 74 + 6 * _h, "mem_max", _h)
    _put(DVE_AT, 76 + 6 * _h, "mem_norm", _h)
    _put(DVE_AT, 85 + 6 * _h + _h // 2, "lo", "mem_pT", _h)
    _put(DVE_AT, 158 + 6 * _h, "mla_max", _h)
    _put(DVE_AT, 160 + 6 * _h, "mla_norm", _h)
for _s, *_step in [
        (36, "memv", 0), (38, "memv", 1), (99, "mem_out", 0), (110, "mem_out", 1),
        (123, "lo", "wukv", 0), (125, "lo", "wukv", 1), (128, "lo", "ckvT", 0),
        (21, "lo", "memk", 0), (23, "lo", "memk", 1), (69, "lo", "cq", 0), (70, "lo", "cq", 1),
        (86, "rms", 0), (88, "ckv", 0), (89, "kpe_rope", 0),
        (96, "gates", 0), (98, "gate_scan", 0), (101, "skip", 0), (100, "ones", 0),
        (102, "rms", 1), (103, "cqn", 0), (104, "cqn", 1), (110, "cT", 0), (113, "cT", 1), (109, "gate_cols", 0),
        (111, "ml_gap", 0), (112, "ml_gap", 1), (119, "ml_gap", 2), (120, "ml_gap", 3),
        (115, "ml_weigh", 0), (117, "ml_weigh", 1), (124, "ml_weigh", 2), (126, "ml_weigh", 3),
        (127, "ml_out", 0), (128, "ml_out", 1), (132, "ml_out", 2), (134, "ml_out", 3),
        (136, "cell_gate", 0), (137, "cell_gate", 1), (139, "cell_stats", 0), (140, "cell_stats", 1),
        (142, "cell_norm", 0), (144, "cell_norm", 1),
        (137, "q_rope", 0), (138, "q_rope", 1),
        (156, "cellT", 0), (157, "cellT", 1),
        (148, "rope_rq", 0), (150, "rope_rq", 1), (165, "rope_rk", 0), (167, "rope_rk", 1),
        (179, "mla_out", 0), (191, "mla_out", 1),
        (193, "ret_weigh", 0), (195, "ret_weigh", 1), (203, "ret_weigh", 2), (205, "ret_weigh", 3),
        (202, "ret_stats", 0), (204, "ret_norm", 0), (212, "ret_stats", 1), (214, "ret_norm", 1),
        (216, "retT", 0), (224, "retT", 1),
        (198, "gate", 3, 0), (199, "gate", 3, 1), (215, "gate", 2, 0), (216, "gate", 2, 1),
        (230, "gate", 1, 0), (231, "gate", 1, 1), (248, "gate", 0, 0), (249, "gate", 0, 1),
        (206, "y_lo", 0), (208, "y_lo", 1), (222, "y_lo", 2), (224, "y_lo", 3),
        (244, "y_lo", 4), (245, "y_lo", 5), (251, "y_lo", 6), (252, "y_lo", 7)]:
    _put(DVE_AT, _s, *_step)
HI_STEPS = [step for slot in sorted(ACT_AT) for step in ACT_AT[slot] if step[0] in ("memk", "cq", "mem_pT", "wukv", "ckvT")]
for _c in range(NOUT - 1):
    _put(DVE_AT, (OUT0 + _c + 1) * KT + 4, "residual", _c)

DVE_LINKS, ACT_LINKS = 76, 5
DVE_LINKS_BEFORE = 4


POOL_BIAS, DVE_BIAS = [0, 1, 2, 3, 4], [5, 6, 7]
STORE_ORDER = [0, 1, 2, 5, 3, 6, 7, 4]


def pair_at(m):
    c, j = divmod(m, KT // 2)
    w = CHUNKS[c][1]
    return CHUNK_AT[c] + j * 2 * P * w, w


def two_pi_parts():
    first = 6.28125
    second = 253.0 / 2 ** 17
    return first, second, 2.0 * np.pi - first - second


PI_IN = 3.1415925


class Signal:

    def __init__(self, sem, per_layer, before=0, step=1):
        self.sem, self.per_layer, self.before, self.step = sem, per_layer, before, step

    def at(self, layer, i):
        return layer * (self.per_layer * self.step) + (self.before + i + 1) * self.step


def build_trunk(nc, a, out):
    ctx = ExitStack()
    with ctx:
        def sb(name, shape, dt=F32):
            return ctx.enter_context(nc.sbuf_tensor(name, shape, dt))

        def signal(name, per_layer, before=0, step=1):
            return Signal(ctx.enter_context(nc.semaphore(name)), per_layer, before, step)

        X = sb("X", [P, NT, D_MODEL])
        xh, xl = sb("xh", [P, KT, SEQ], F32R), sb("xl", [P, KT, SEQ], F32R)
        mh, ml = sb("mh", [P, KT, MEM_LEN], F32R), sb("ml", [P, KT, MEM_LEN], F32R)
        with nc.sbuf_tensor("Yr", [P, 1024], F32R) as Yr:
            pass
        Y = sb("Y", [P, KT * SEQ])
        raw = sb("raw", [P, RAW, 2 * 512])
        hi, lo = sb("hi", [P, RING, 512], F32R), sb("lo", [P, RING, 512], F32R)
        const = sb("const", [P, NCONST])
        ident_buf = sb("ident", [P, P])
        cols = sb("cols", [P, NCOLS])
        B, Br = [], []
        for i in range(10):
            size = {0: NT * HEADS * (HD + 1), 3: 4 * (SEQ + PAD)}.get(i, 4 * SEQ)
            with nc.sbuf_tensor(f"B{i}r", [P, 4 * SEQ], F32R) as same_place:
                Br.append(same_place)
            B.append(sb(f"B{i}", [P, size]))
        qr = sb("qr", [P, NT, HEADS * ROT])
        qrT = sb("qrT", [P, 2, SEQ])
        krr = sb("krr", [P, NT, P])
        krT = sb("krT", [P, SEQ])
        prob = sb("prob", [P, 2, 512])
        pTl = sb("pTl", [P, 2, 512], F32R)
        with nc.sbuf_tensor("pTh", [P, 2, 512], F32R) as pTh:
            pass
        probT = sb("probT", [P, 2, 512])
        tmp = sb("tmp", [P, 512])
        freq = sb("freq", [P, FR + FM])
        cos, sin = sb("cos", [P, NT, FR + FM]), sb("sin", [P, 2, NT, FR + FM])
        small = sb("small", [P, NT, SMALL])
        gcol = sb("gcol", [P, 4, HEADS])
        nmax, rsum, rinv = sb("nmax", [P, 2, 2]), sb("rsum", [P, 2, 2]), sb("rinv", [P, 2, 2])
        sumsq, rms = sb("sumsq", [P, 3, NT]), sb("rms", [P, 2, NT])
        den = sb("den", [P, 2, NT])
        stats, mv, rstd = sb("stats", [P, 8, 6]), sb("mv", [P, 8, 2]), sb("rstd", [P, 8])
        ln_stats, ln_mv = sb("ln_stats", [P, NT, NOUT, 6]), sb("ln_mv", [P, NT, 2])
        ln_nmu, ln_rstd, ln_shift = sb("ln_nmu", [P, NT]), sb("ln_rstd", [P, NT]), sb("ln_shift", [P, NT])
        half = sb("half", [P, 8])
        pos = sb("pos", [P, NT], I32)
        warm = sb("warm", [P, 1])

        memT = [B[i][:, 0:4 * SEQ] for i in range(4)]
        turn1 = B[4][:, 0:NT * (FR + FM)].rearrange("p (i f) -> p i f", i=NT)
        whole = B[4][:, 512:512 + 2 * NT * (FR + FM)].rearrange("p (a i f) -> p a i f", a=2, i=NT)
        angle = B[5][:, 0:2 * NT * (FR + FM)].rearrange("p (a i f) -> p a i f", a=2, i=NT)
        heads = lambda buf: buf[:, 0:1024].rearrange("p (h t) -> p h t", h=HEADS)
        tokens = lambda buf: buf[:, 0:1024].rearrange("p (i w) -> p i w", i=NT)
        mKT, cQT = (heads(Br[0]), heads(Br[8])), (heads(Br[2]), heads(Br[5]))
        mV = (tokens(Br[1]), tokens(Br[9]))
        lv1 = B[0][:, 0:NT * HEADS * (HD + 1)].rearrange("p (i h e) -> p i h e", i=NT, h=HEADS)
        rqT, mlaV, memo = heads(B[0]), tokens(B[1]), heads(B[2])
        LX = B[3][:, 0:4 * (SEQ + PAD)].rearrange("p (j t) -> p j t", j=4)
        lkT = rkT = B[3][:, 0:1024].rearrange("p (h t) -> p h t", h=HEADS)
        xcT = mls = B[4][:, 0:1024].rearrange("p (h t) -> p h t", h=HEADS)
        lqT = retT = B[5][:, 0:1024].rearrange("p (h t) -> p h t", h=HEADS)
        cell = B[5][:, 0:1024].rearrange("p (i w) -> p i w", i=NT)
        lw = B[6][:, 0:1024].rearrange("p (q h e) -> p q h e", q=2, h=HEADS)
        row = [B[6][0:HEADS, r * SEQ:(r + 1) * SEQ] for r in range(4)]
        sigo = rv = B[6][:, 0:1024].rearrange("p (i w) -> p i w", i=NT)
        cqn = B[7][:, 0:NT * 512].rearrange("p (i w) -> p i w", i=NT)
        knT = B[7][:, 0:1024].rearrange("p (h t) -> p h t", h=HEADS)
        cT = B[8][:, 0:1024].rearrange("p (j t) -> p j t", j=4)
        mrow = B[9][:, 0:1024].rearrange("p (h t) -> p h t", h=HEADS)
        qnT = mlao = B[9][:, 0:1024].rearrange("p (h t) -> p h t", h=HEADS)
        gb = Y[:, :].rearrange("p (a n) -> p a n", a=2)
        wukv = Y[:, 0:1024].rearrange("p (h v e) -> p h v e", h=HEADS, v=2)
        wuq = Y[:, 1024:1024 + 3 * HEADS * (NOPE + ROT)].rearrange("p (k h e) -> p k h e", k=3, h=HEADS)
        wukvp = tuple(b[:, :].rearrange("p (h v e) -> p h v e", h=HEADS, v=2) for b in (Br[1], Yr))
        ckvp = pTl[:, 0, 0:SEQ], pTl[:, 0, SEQ:2 * SEQ]
        gap = Y[:, 4096 - 2 * TRI:4096].rearrange("p (b c) -> p b c", b=2)
        rqt = Y[:, 1024:2048].rearrange("p (i w) -> p i w", i=NT)
        rkt = Y[:, 2048:3072].rearrange("p (i w) -> p i w", i=NT)
        retn = Y[:, 0:1024].rearrange("p (i w) -> p i w", i=NT)
        yT = Y[:, :].rearrange("p (k t) -> p k t", k=KT)
        junk = tmp

        early = [Br[i][:, :].rearrange("p (a k t) -> p a k t", a=2, k=2) for i in (1, 2, 3, 0)]

        def y_part(part, j):
            if j < len(early):
                return early[j][:, part, :, :]
            return (xh, xl)[part][:, OUT_ORDER[2 * j]:OUT_ORDER[2 * j] + 2, :]

        ident = ident_buf[:, :]
        decay = const[:, K_DECAY:K_DECAY + HEADS * TRI].rearrange("p (h c) -> p h c", h=HEADS)
        tri, big = const[:, K_TRI:K_TRI + TRI], const[:, K_BIG:K_BIG + TRI]

        acc = ctx.enter_context(nc.psum_tensor("acc", [P, 2, 2, 512], F32))
        work = ctx.enter_context(nc.psum_tensor("work", [P, NBANK, 512], F32))

        raw_full = [signal(f"raw_full{s}", PAIRS // RAW, step=16) for s in range(RAW)]
        hi_done = signal("hi_done", SLOTS)
        lo_done = signal("lo_done", SLOTS, before=2 * RAW)
        tile_used = signal("tile_used", SLOTS, before=RING)
        acc_read = [signal(f"acc_read{p}", NCH, before=2) for p in range(2)]
        job_done = signal("job_done", NJOBS)
        in_bank = [[j for j in range(NJOBS) if j % NBANK == b] for b in range(NBANK)]
        bank_read = [signal(f"bank_read{b}", len(in_bank[b]), before=1) for b in range(NBANK)]
        memb_in = [signal(f"mem_in{q}", 0, step=16) for q in range(4)]
        rotary_in, ident_in, const_in = (signal(n, 0, step=16) for n in ("rotary_in", "ident_in", "const_in"))
        x_in = [signal(f"x_in{cb}", 0, step=16) for cb in range(4)]
        mem_dve, mem_pool = signal("mem_dve", 0), signal("mem_pool", 0)
        pool_hi = signal("pool_hi", 0)
        angles, tables = signal("angles", 1), signal("tables", 1)
        ready = signal("ready", 0)
        cols_in = signal("cols_in", 1, step=16)
        lw_in = signal("lw_in", 1, step=16)
        mlaw_in = signal("mlaw_in", 2, step=16)
        gb_in = signal("gb_in", 1, before=1, step=16)
        normed = signal("normed", 8)
        x_done = signal("x_done", 8)
        x_hi = signal("x_hi", 8)
        y_hi, y_lo = signal("y_hi", 8), signal("y_lo", 8)
        kv_split = signal("kv_split", 3)
        hi_part = signal("hi_part", len(HI_STEPS))
        conv_done, xc_done = signal("conv_done", 1), signal("xc_done", 2)
        lx_pad = signal("lx_pad", 1)
        sq_done, var_done, rms_done = signal("sq_done", 2), signal("var_done", 2), signal("rms_done", 2)
        c_normed = signal("c_normed", 2)
        kpe_done = signal("kpe_done", 1)
        gate_abs, softplus_done = signal("gate_abs", 1), signal("softplus_done", 1)
        mrow_out, mrow_in = signal("mrow_out", 1, step=16), signal("mrow_in", 1, step=16)
        scan_done, floor_done = signal("scan_done", 1), signal("floor_done", 1)
        skip_done, ones_done = signal("skip_done", 1), signal("ones_done", 1)
        gap_done, decay_done = signal("gap_done", 4), signal("decay_done", 4)
        max_done, exp_done, prob_done = signal("max_done", 8), signal("exp_done", 4), signal("prob_done", 8)
        qr_done = signal("qr_done", 2)
        cell_var, cell_pow, cell_done = signal("cell_var", 1), signal("cell_pow", 1), signal("cell_done", 1)
        ret_var, ret_pow = signal("ret_var", 2), signal("ret_pow", 2)
        ln_var, ln_mean, ln_pow = signal("ln_var", 1), signal("ln_mean", 1), signal("ln_pow", 1)
        ln_done = signal("ln_done", 1, before=1)
        gated = signal("gated", 8)
        roped = signal("roped", 4)
        pool_mul = signal("pool_mul", 8)
        alone = signal("alone", 0)
        final_gained, final_scaled = signal("final_gained", 0), signal("final_scaled", 0)
        pool_biased, dve_biased = signal("pool_biased", 0), signal("dve_biased", 0)
        stored = signal("stored", 0, step=16)
        dve_own = signal("dve_own", DVE_LINKS, before=DVE_LINKS_BEFORE)
        act_own = signal("act_own", ACT_LINKS)

        def stand_alone(eng):
            eng.sem_inc(alone.sem, 1)

        def bank_of(job):
            j = JOB[job]
            return j % NBANK, j // NBANK

        def bank(job):
            return work[:, bank_of(job)[0], :]

        def wait_job(eng, l, *jobs):
            eng.wait_ge(job_done.sem, job_done.at(l, max(JOB[job] for job in jobs)))

        def wait_read(eng, l, *jobs):
            last = {}
            for job in jobs:
                b, u = bank_of(job)
                last[b] = max(u, last.get(b, 0))
            for b, u in last.items():
                eng.wait_ge(bank_read[b].sem, bank_read[b].at(l, u))

        def free_bank(*job):
            return bank_read[bank_of(job)[0]].sem

        def wait_chunk(eng, l, c):
            eng.wait_ge(tile_used.sem, tile_used.at(l, (c + 1) * KT - 1))

        def wait_acc_read(eng, l, c, halves=2):
            eng.wait_ge(acc_read[c % 2].sem, acc_read[c % 2].at(l, (c // 2) * 2 + halves - 1))

        def acc_sem(name):
            return acc_read[CI[name] % 2].sem

        def A(name, i):
            return acc[:, CI[name] % 2, i, :]

        def operand(name, i):
            if name == "wukv":
                return (wukv[:, 2 * i:2 * i + 2], wukvp[0][:, 2 * i:2 * i + 2], wukvp[1][:, 2 * i:2 * i + 2],
                        kv_split.sem)
            if name == "ckvT":
                return cT[:, 3, :], ckvp[0], ckvp[1], kv_split.sem
            if name in ("memk", "cq"):
                src, (h, l) = A(name, i).rearrange("p (j t) -> p j t", j=2), {"memk": mKT, "cq": cQT}[name]
                return src, h[:, 2 * i:2 * i + 2, :], l[:, 2 * i:2 * i + 2, :], acc_sem(name)
            if name == "mem_pT":
                return bank((name, i)), pTh[:, i % 2, :], pTl[:, i % 2, :], free_bank(name, i)
            return A("memv", i), mV[0][:, i, :], mV[1][:, i, :], acc_sem("memv")

        block = ctx.enter_context(nc.Block())

        def load_x(eng, cb):
            eng.dma_start(X[:, :, cb * 512:(cb + 1) * 512],
                          a["x"][:, cb * 512:(cb + 1) * 512].rearrange("(i p) n -> p i n", p=P))\
                .then_inc(x_in[cb].sem, 16)

        @block.sync
        def _(sp):
            sp.dma_start(memT[0], a["mem_t"][:, 0:1024]).then_inc(memb_in[0].sem, 16)
            with sp.Fori(0, DEPTH) as l:
                for m in range(PAIRS):
                    sp.wait_ge(lo_done.sem, lo_done.at(l, 2 * m + 1 - 2 * RAW))
                    at, w = pair_at(m)
                    sp.dma_start(raw[:, m % RAW, 0:2 * w],
                                 a["w"][bass.ts(l, 1), at:at + 2 * P * w].rearrange("o (p n) -> p (o n)", p=P))\
                      .then_inc(raw_full[m % RAW].sem, 16)
                    if m == 4:
                        sp.dma_start(cols[:, :], a["cols"][bass.ts(l, 1), :].rearrange("o (p n) -> p (o n)", p=P))\
                          .then_inc(cols_in.sem, 16)
                    if m == 20:
                        sp.dma_start(B[6][:, 0:1024], a["lw"][bass.ts(l, 1), :].rearrange("o (p n) -> p (o n)", p=P))\
                          .then_inc(lw_in.sem, 16)
                    if m == 24:
                        sp.wait_ge(x_done.sem, x_done.at(l, 7))
                        sp.dma_start(Y[:, 0:1024], a["wukv"][bass.ts(l, 1), :].rearrange("o (p n) -> p (o n)", p=P))\
                          .then_inc(mlaw_in.sem, 16)
                        sp.dma_start(Y[:, 1024:3328], a["wuq"][bass.ts(l, 1), :].rearrange("o (p n) -> p (o n)", p=P))\
                          .then_inc(mlaw_in.sem, 16)
                    if m == 54:
                        sp.wait_ge(scan_done.sem, scan_done.at(l, 0))
                        sp.dma_start(a["mrow"], row[1]).then_inc(mrow_out.sem, 16)
                    if m == 57:
                        sp.wait_ge(mrow_out.sem, mrow_out.at(l, 0))
                        wait_job(sp, l, ("mem_out", 1))
                        sp.dma_start(B[9][:, 0:1024], a["mrow"].rearrange("h t -> (h t)").partition_broadcast(P))\
                          .then_inc(mrow_in.sem, 16)
                    if m == 136:
                        sp.wait_ge(y_lo.sem, y_lo.at(l, 7))
                        sp.dma_start(Y[:, :], a["gb"][bass.ts(l, 1), :].partition_broadcast(P)
                                     .rearrange("p o n -> p (o n)")).then_inc(gb_in.sem, 16)
            for b in STORE_ORDER:
                cb, i = divmod(b, 2)
                if b in POOL_BIAS:
                    sp.wait_ge(pool_biased.sem, POOL_BIAS.index(b) + 1)
                else:
                    sp.wait_ge(dve_biased.sem, DVE_BIAS.index(b) + 1)
                sp.dma_start(out[i * P:(i + 1) * P, cb * 512:(cb + 1) * 512],
                             X[:, i, cb * 512:(cb + 1) * 512]).then_inc(stored.sem, 16)
            sp.wait_ge(stored.sem, 8 * 16)

        @block.gpsimd
        def _(pool):
            pool.memset(gb[:, 0, :], 1.0)
            for q in (2, 3):
                pool.dma_start(memT[q], a["mem_t"][:, q * 1024:(q + 1) * 1024]).then_inc(memb_in[q].sem, 16)
            pool.memset(gb[:, 1, :], 0.0).then_inc(gb_in.sem, 16)

            for q in (2, 3):
                m3 = memT[q].rearrange("p (k t) -> p k t", k=4)
                load_x(pool, q - 1)
                pool.wait_ge(memb_in[q].sem, 16)
                pool.tensor_copy(mh[:, 4 * q:4 * q + 4, :], m3).then_inc(pool_hi.sem, 1)
                if q == 2:
                    pool.dma_start(ident, a["ident"]).then_inc(ident_in.sem, 16)
                pool.wait_ge(pool_hi.sem, q - 1)
                pool.tensor_tensor(ml[:, 4 * q:4 * q + 4, :], m3, mh[:, 4 * q:4 * q + 4, :].bitcast(F32), ALU.subtract)\
                    .then_inc(mem_pool.sem, 1)
            load_x(pool, 3)
            pool.dma_start(const[:, :], a["const"]).then_inc(const_in.sem, 16)
            pool.wait_ge(ready.sem, 1)

            def root(dst, src, n):
                return pool.tensor_tensor(dst, src, half[:, 0:n], ALU.pow)

            with pool.Fori(0, DEPTH) as l:
                pool.wait_ge(gb_in.sem, gb_in.at(l, -1))
                for b in range(8):
                    cb, i = divmod(b, 2)
                    blk = X[:, i, cb * 512:(cb + 1) * 512]
                    pool.wait_ge(normed.sem, normed.at(l, b))
                    pool.tensor_tensor(blk, blk, gb[:, 0, cb * 512:(cb + 1) * 512], ALU.mult)\
                        .then_inc(pool_mul.sem, 1)
                    pool.wait_ge(pool_mul.sem, pool_mul.at(l, b))
                    pool.tensor_tensor(blk, blk, gb[:, 1, cb * 512:(cb + 1) * 512], ALU.add)\
                        .then_inc(x_done.sem, 1)
                for r in range(2):
                    pool.wait_ge(var_done.sem, var_done.at(l, r))
                    root(rms[:, r, :], sumsq[:, r, :], NT).then_inc(rms_done.sem, 1)
                pool.wait_ge(cell_var.sem, cell_var.at(l, 0))
                root(rstd[:, :], stats[:, :, 0], 8).then_inc(cell_pow.sem, 1)
                for r in range(2):
                    pool.wait_ge(ret_var.sem, ret_var.at(l, r))
                    root(rstd[:, 0:4], stats[:, 0:4, 0], 4).then_inc(ret_pow.sem, 1)
                pool.wait_ge(ln_var.sem, ln_var.at(l, 0))
                root(ln_rstd[:, :], ln_stats[:, :, 0, 0], NT).then_inc(ln_pow.sem, 1)
                pool.wait_ge(ln_mean.sem, ln_mean.at(l, 0))
                pool.wait_ge(ln_pow.sem, ln_pow.at(l, 0))
                pool.tensor_tensor(ln_shift[:, :], ln_nmu[:, :], ln_rstd[:, :], ALU.mult).then_inc(ln_done.sem, 1)

            for b in POOL_BIAS:
                cb, i = divmod(b, 2)
                blk = X[:, i, cb * 512:(cb + 1) * 512]
                pool.wait_ge(final_scaled.sem, POOL_BIAS.index(b) + 1)
                pool.tensor_tensor(blk, blk, gb[:, 1, cb * 512:(cb + 1) * 512], ALU.add)\
                    .then_inc(pool_biased.sem, 1)

        @block.scalar
        def _(act):
            act.dma_start(pos[:, :], a["pos"]).then_inc(rotary_in.sem, 16)
            act.dma_start(memT[1], a["mem_t"][:, 1024:2048]).then_inc(memb_in[1].sem, 16)
            act.dma_start(freq[:, :], a["freq"]).then_inc(rotary_in.sem, 16)
            load_x(act, 0)
            act.wait_ge(ready.sem, 1)

            with act.Fori(0, DEPTH) as l:
                act.activation(warm[:, :], half[:, 0:1], ACT.Copy)
                links = [0]

                def link(ins):
                    ins.then_inc(act_own.sem, 1)
                    links[0] += 1
                    act.wait_ge(act_own.sem, act_own.at(l, links[0] - 1))

                def normalise(b):
                    cb, i = divmod(b, 2)
                    blk = X[:, i, cb * 512:(cb + 1) * 512]
                    act.wait_ge(x_in[cb].sem, 16)
                    if b == 0:
                        act.wait_ge(ln_done.sem, ln_done.at(l, -1))
                    act.activation(blk, blk, ACT.Identity, scale=ln_rstd[:, i:i + 1], bias=ln_shift[:, i:i + 1])\
                       .then_inc(normed.sem, 1)

                def rotary(_):
                    act.wait_ge(angles.sem, angles.at(l, 0))
                    act.activation(cos[:, :, :], angle[:, 1, :, :], ACT.Sin)
                    act.activation(sin[:, 0, :, :], angle[:, 0, :, :], ACT.Sin, scale=-1.0)
                    act.activation(sin[:, 1, :, :], angle[:, 0, :, :], ACT.Sin).then_inc(tables.sem, 1)

                def x_hi_(j):
                    wait_job(act, l, ("xT", j))
                    act.activation(xh[:, 2 * j:2 * j + 2, :], bank(("xT", j)).rearrange("p (k t) -> p k t", k=2),
                                   ACT.Copy).then_inc(x_hi.sem, 1)

                def y_hi_(j):
                    k = OUT_ORDER[2 * j]
                    if j == 2:
                        wait_job(act, l, ("ret_scores", HEADS - 1))
                    if j == len(early):
                        wait_chunk(act, l, OUT0 - 1)
                    act.wait_ge(gated.sem, gated.at(l, j))
                    act.activation(y_part(0, j), yT[:, k:k + 2, :], ACT.Copy).then_inc(y_hi.sem, 1)

                def hi_of(name):
                    def go(i):
                        if name == "mem_pT":
                            wait_job(act, l, (name, i), *([("mem_out", 0)] if i >= 2 else []))
                        elif name == "wukv":
                            act.wait_ge(mlaw_in.sem, mlaw_in.at(l, 1))
                            wait_job(act, l, ("mem_out", 1))
                        elif name == "ckvT":
                            wait_read(act, l, ("cT", 0), ("cT", 1))
                        else:
                            wait_chunk(act, l, CI[name])
                        src, part, _, _ = operand(name, i)
                        act.activation(part, src, ACT.Copy).then_inc(hi_part.sem, 1)
                    return go

                def lx(i):
                    wait_chunk(act, l, CI["lx"])
                    act.activation(LX[:, 2 * i:2 * i + 2, PAD:PAD + SEQ],
                                   A("lx", i).rearrange("p (j t) -> p j t", j=2), ACT.Copy)\
                       .then_inc(acc_sem("lx"), 1)

                def mem_exp(h):
                    act.wait_ge(max_done.sem, max_done.at(l, h))
                    if h >= 2:
                        wait_job(act, l, ("mem_pT", h - 2))
                    for i in range(NT):
                        e = act.activation(prob[:, h % 2, i * 256:(i + 1) * 256], bank(("mem_scores", h))[:, i * 256:(i + 1) * 256],
                                           ACT.Exp, scale=HEAD_SCALE, bias=nmax[:, h % 2, i:i + 1],
                                           accum_out=rsum[:, h % 2, i:i + 1])
                    e.then_inc(free_bank("mem_scores", h), 1)

                def mla_exp(h):
                    act.wait_ge(max_done.sem, max_done.at(l, HEADS + h))
                    for i, (c0, c1) in enumerate(((0, P), (P, TRI))):
                        e = act.activation(prob[:, h % 2, c0:c1], prob[:, h % 2, c0:c1], ACT.Exp, scale=MLA_SCALE,
                                           bias=nmax[:, h % 2, i:i + 1], accum_out=rsum[:, h % 2, i:i + 1])
                    e.then_inc(exp_done.sem, 1)

                def mla_pT(h):
                    wait_job(act, l, ("mla_pT", h), *([("mla_out", 0)] if h >= 2 else []))
                    act.activation(probT[:, h % 2, 0:TRI], bank(("mla_pT", h))[:, 0:TRI], ACT.Copy)\
                       .then_inc(free_bank("mla_pT", h), 1)

                def silu_conv(q):
                    act.wait_ge(conv_done.sem, conv_done.at(l, 0))
                    for j in range(2 * q, 2 * q + 2):
                        s = act.activation(xcT[:, j, :], xcT[:, j, :], ACT.Silu, bias=cols[:, C_CONVB + j:C_CONVB + j + 1])
                    s.then_inc(xc_done.sem, 1)

                def akv(i):
                    wait_chunk(act, l, CI["akv"])
                    if i:
                        act.activation(small[:, i, :], A("akv", i)[:, KVRANK:AKV_W], ACT.Copy)
                        act.activation(junk[:, 0:KVRANK], A("akv", i)[:, 0:KVRANK], ACT.Square,
                                       accum_out=sumsq[:, 0, i:i + 1]).then_inc(sq_done.sem, 1)
                    else:
                        act.activation(small[:, i, :], A("akv", i)[:, KVRANK:AKV_W], ACT.Copy)
                        link(act.activation(junk[:, 0:KVRANK], A("akv", i)[:, 0:KVRANK], ACT.Square,
                                            accum_out=sumsq[:, 0, i:i + 1]))

                def aq(i):
                    wait_chunk(act, l, CI["aq"])
                    link(act.activation(junk[:, 0:QHEAD], small[:, i, C_CQ:SMALL], ACT.Square,
                                        accum_out=sumsq[:, 2, i:i + 1]))
                    s = act.activation(junk[:, 0:QRANK - QHEAD], A("aq", i)[:, 0:QRANK - QHEAD], ACT.Square,
                                       accum_out=sumsq[:, 1, i:i + 1])
                    if i:
                        s.then_inc(sq_done.sem, 1)
                    else:
                        link(s)

                def pair(name, dst):
                    def evacuate(i):
                        wait_job(act, l, (name, i))
                        act.activation(dst[:, 2 * i:2 * i + 2, :], bank((name, i)).rearrange("p (j t) -> p j t", j=2),
                                       ACT.Copy).then_inc(free_bank(name, i), 1)
                    return evacuate

                def softplus(_):
                    act.wait_ge(gate_abs.sem, gate_abs.at(l, 0))
                    link(act.activation(row[2], row[2], ACT.Exp, scale=-1.0))
                    act.activation(row[2], row[2], ACT.Ln, bias=1.0).then_inc(softplus_done.sem, 1)

                def gate_floor(_):
                    act.wait_ge(scan_done.sem, scan_done.at(l, 0))
                    act.activation(row[3], row[3], ACT.Exp, scale=-1.0).then_inc(floor_done.sem, 1)

                def ml_decay(h):
                    act.wait_ge(gap_done.sem, gap_done.at(l, h))
                    act.activation(gap[:, h % 2, :], gap[:, h % 2, :], ACT.Exp, scale=-1.0).then_inc(decay_done.sem, 1)

                def lv(i):
                    wait_chunk(act, l, CI["lv"])
                    act.wait_ge(ones_done.sem, ones_done.at(l, 0))
                    act.activation(lv1[:, i, :, 0:HD], A("lv", i).rearrange("p (h e) -> p h e", h=HEADS), ACT.Copy)\
                       .then_inc(acc_sem("lv"), 1)

                def lo_(i):
                    wait_chunk(act, l, CI["lo"])
                    act.activation(sigo[:, i, :], A("lo", i), ACT.Sigmoid).then_inc(acc_sem("lo"), 1)

                def rv_(i):
                    wait_chunk(act, l, CI["rv"])
                    act.activation(rv[:, i, :], A("rv", i), ACT.Copy).then_inc(acc_sem("rv"), 1)

                def kpeT(_):
                    wait_job(act, l, ("kpeT", 0))
                    act.activation(krT[:, :], bank(("kpeT", 0))[:, 0:SEQ], ACT.Copy).then_inc(free_bank("kpeT", 0), 1)

                def mla_v(i):
                    wait_job(act, l, ("mla_v", 1))
                    act.activation(mlaV[:, i, :], bank(("mla_v", i)), ACT.Copy).then_inc(free_bank("mla_v", i), 1)

                def qrT_(_):
                    wait_job(act, l, ("qrT", 0))
                    act.activation(qrT[:, :, :], bank(("qrT", 0)).rearrange("p (j t) -> p j t", j=2), ACT.Copy)\
                       .then_inc(free_bank("qrT", 0), 1)

                def turned(name, dst):
                    def evacuate(i):
                        wait_job(act, l, (name, i))
                        act.activation(dst[:, :, i * P:(i + 1) * P], bank((name, i)).rearrange("p (h t) -> p h t", h=HEADS),
                                       ACT.Copy).then_inc(free_bank(name, i), 1)
                    return evacuate

                def silu(g, i):
                    name = f"z{g}"
                    wait_chunk(act, l, CI[name])
                    if (g, i) == (3, 0):
                        wait_read(act, l, ("ml_scores", 3))
                    if (g, i) == (2, 0):
                        wait_job(act, l, ("rkT", 1))
                    if (g, i) == (0, 0):
                        wait_job(act, l, ("retT", 1))
                    act.activation(yT[:, 4 * g + 2 * i:4 * g + 2 * i + 2, :], A(name, i).rearrange("p (j t) -> p j t", j=2),
                                   ACT.Silu).then_inc(acc_sem(name), 1)

                steps = {"normalise": normalise, "rotary": rotary, "x_hi": x_hi_, "y_hi": y_hi_, "memk": hi_of("memk"), "wukv": hi_of("wukv"), "ckvT": hi_of("ckvT"),
                         "cq": hi_of("cq"), "lx": lx, "mem_exp": mem_exp, "mem_pT": hi_of("mem_pT"),
                         "mla_exp": mla_exp, "mla_pT": mla_pT, "silu_conv": silu_conv, "akv": akv, "aq": aq,
                         "ml_q": pair("ml_q", lqT), "ml_k": pair("ml_k", lkT), "softplus": softplus,
                         "gate_floor": gate_floor, "ml_decay": ml_decay, "lv": lv, "lo": lo_, "rv": rv_,
                         "kpeT": kpeT, "mla_kn": pair("mla_kn", knT), "mla_qn": pair("mla_qn", qnT),
                         "mla_v": mla_v, "qrT": qrT_, "rqT": turned("rqT", rqT), "rkT": turned("rkT", rkT),
                         "silu": silu}
                for t in range(SLOTS):
                    c, k = divmod(t, KT)
                    w, s = CHUNKS[c][1], (t // 2) % RAW
                    if t % 2 == 0:
                        act.wait_ge(raw_full[s].sem, raw_full[s].at(l, t // 2 // RAW))
                    act.wait_ge(tile_used.sem, tile_used.at(l, t - RING))
                    act.activation(hi[:, t % RING, 0:w], raw[:, s, (t % 2) * w:(t % 2 + 1) * w], ACT.Copy)\
                       .then_inc(hi_done.sem, 1)
                    for name, *args in ACT_AT.get(t, ()):
                        steps[name](*args)
                assert links[0] == ACT_LINKS, links
            act.wait_ge(lo_done.sem, lo_done.at(DEPTH - 1, SLOTS - 1))
            act.sem_inc(hi_done.sem, AHEAD)

            act.wait_ge(ln_pow.sem, ln_pow.at(DEPTH - 1, 0))
            for b in POOL_BIAS:
                cb, i = divmod(b, 2)
                blk = X[:, i, cb * 512:(cb + 1) * 512]
                act.wait_ge(final_gained.sem, b + 1)
                act.activation(blk, blk, ACT.Copy, scale=ln_rstd[:, i:i + 1]).then_inc(final_scaled.sem, 1)

        @block.tensor
        def _(pe):
            pe.sem_inc(tile_used.sem, RING)

            with pe.Fori(0, DEPTH) as l:
                def take(*job):
                    b, u = bank_of(job)
                    stand_alone(pe)
                    pe.wait_ge(bank_read[b].sem, bank_read[b].at(l, u - 1))
                    return work[:, b, :]

                def turn(dst, src):
                    return pe.transpose(dst, src, ident[0:src.shape[0], 0:src.shape[0]])

                def product(o, a_, b_, start=True, stop=True):
                    (ah, al), (bh, bl) = a_, b_
                    pe.matmul(o, ah, bh, start=start, stop=False)
                    pe.matmul(o, al, bh, start=False, stop=False)
                    return pe.matmul(o, ah, bl, start=False, stop=stop)

                def both(parts, at):
                    return tuple(at(x) for x in parts)

                def xT(j):
                    pe.wait_ge(ident_in.sem, 16)
                    pe.wait_ge(x_done.sem, x_done.at(l, 2 * (j // 2) + 1))
                    o = take("xT", j)
                    for kk in range(2):
                        for i in range(NT):
                            m = turn(o[:, kk * 256 + i * P:kk * 256 + (i + 1) * P],
                                     X[:, i, (2 * j + kk) * P:(2 * j + kk + 1) * P])
                    m.then_inc(job_done.sem, 1)

                def mem_scores(h):
                    if h == 0:
                        wait_acc_read(pe, l, CI["memk"])
                        wait_acc_read(pe, l, CI["cq"])
                    o = take("mem_scores", h)
                    for i in range(NT):
                        m = product(o[:, i * 256:(i + 1) * 256], both(cQT, lambda x: x[:, h, i * P:(i + 1) * P]),
                                    both(mKT, lambda x: x[:, h, :]))
                    m.then_inc(job_done.sem, 1)

                def mem_pT(h):
                    pe.wait_ge(prob_done.sem, prob_done.at(l, h))
                    o = take("mem_pT", h)
                    for kt in range(2):
                        for i in range(NT):
                            m = turn(o[:, kt * 256 + i * P:kt * 256 + (i + 1) * P],
                                     prob[:, h % 2, i * 256 + kt * P:i * 256 + (kt + 1) * P])
                    m.then_inc(job_done.sem, 1)

                def mem_out(q):
                    wait_acc_read(pe, l, CI["memv"])
                    wait_read(pe, l, ("mem_pT", 2 * q), ("mem_pT", 2 * q + 1))
                    o = take("mem_out", q)
                    for h in (2 * q, 2 * q + 1):
                        for kt in range(2):
                            m = product(o[:, (h % 2) * 256:(h % 2 + 1) * 256],
                                        both(mV, lambda x: x[:, kt, h * HD:(h + 1) * HD]),
                                        both((pTh, pTl), lambda x: x[:, h % 2, kt * 256:(kt + 1) * 256]),
                                        start=kt == 0, stop=kt == 1)
                    m.then_inc(job_done.sem, 1)

                def ml_proj(name, which):
                    def project(q):
                        if q == 0:
                            pe.wait_ge(lw_in.sem, lw_in.at(l, 0))
                        pe.wait_ge(xc_done.sem, xc_done.at(l, q))
                        o = take(name, q)
                        for h in (2 * q, 2 * q + 1):
                            m = pe.matmul(o[:, (h % 2) * 256:(h % 2 + 1) * 256], lw[:, which, h, :], xcT[:, h, :],
                                          start=True, stop=True)
                        m.then_inc(job_done.sem, 1)
                    return project

                def gateT(_):
                    wait_acc_read(pe, l, CI["akv"])
                    o = take("gateT", 0)
                    for g in range(2):
                        for i in range(NT):
                            m = turn(o[0:HEADS, g * 256 + i * P:g * 256 + (i + 1) * P],
                                     small[:, i, C_GATE + g * HEADS:C_GATE + (g + 1) * HEADS])
                    m.then_inc(job_done.sem, 1)

                def gate_cols(_):
                    pe.wait_ge(scan_done.sem, scan_done.at(l, 0))
                    pe.wait_ge(floor_done.sem, floor_done.at(l, 0))
                    o = take("gate_cols", 0)
                    stand_alone(pe)
                    for g in range(2):
                        for i in range(NT):
                            m = turn(o[:, (2 * g + i) * HEADS:(2 * g + i + 1) * HEADS],
                                     row[3 * g][:, i * P:(i + 1) * P])
                    m.then_inc(job_done.sem, 1)

                def cT_(i):
                    pe.wait_ge(c_normed.sem, c_normed.at(l, 1))
                    o = take("cT", i)
                    for j in range(4):
                        m = turn(o[:, j * P:(j + 1) * P], cqn[:, i, j * P:(j + 1) * P])
                    m.then_inc(job_done.sem, 1)

                def kpeT(_):
                    pe.wait_ge(kpe_done.sem, kpe_done.at(l, 0))
                    o = take("kpeT", 0)
                    for i in range(NT):
                        m = turn(o[:, i * P:(i + 1) * P], krr[:, i, :])
                    m.then_inc(job_done.sem, 1)

                def causal_scores(o, kT_, qT_, h):
                    pe.matmul(o[:, 0:256], kT_[:, h, 0:P], qT_[:, h, :], start=True, stop=True)
                    return pe.matmul(o[:, 256:TRI], kT_[:, h, P:2 * P], qT_[:, h, P:2 * P], start=True, stop=True)

                def ml_scores(h):
                    if h == 0:
                        wait_read(pe, l, ("ml_q", 0), ("ml_q", 1), ("ml_k", 0), ("ml_k", 1))
                    causal_scores(take("ml_scores", h), lkT, lqT, h).then_inc(job_done.sem, 1)

                def ml_out(h):
                    if h == 0:
                        wait_acc_read(pe, l, CI["lv"])
                    wait_read(pe, l, ("ml_scores", h))
                    o = take("ml_out", h)
                    pt, e = probT[:, h % 2, :], HD + 1
                    pe.matmul(o[:, 0:e], pt[:, 0:P], lv1[:, 0, h, :], start=True, stop=True)
                    pe.matmul(o[:, e:2 * e], pt[:, P:2 * P], lv1[:, 0, h, :], start=True, stop=False)
                    pe.matmul(o[:, e:2 * e], pt[:, 2 * P:3 * P], lv1[:, 1, h, :], start=False, stop=True)\
                      .then_inc(job_done.sem, 1)

                def mla_qr(i):
                    pe.wait_ge(mlaw_in.sem, mlaw_in.at(l, 1))
                    wait_read(pe, l, ("cT", i))
                    o = take("mla_qr", i)
                    for k in range(3):
                        m = pe.matmul(o[:, 0:HEADS * ROT].rearrange("p (h e) -> p h e", h=HEADS),
                                      cT[:, k, i * P:(i + 1) * P], wuq[:, k, :, NOPE:], start=k == 0, stop=k == 2)
                    m.then_inc(job_done.sem, 1)

                def mla_kn(q):
                    pe.wait_ge(kv_split.sem, kv_split.at(l, 2))
                    o = take("mla_kn", q)
                    for h in (2 * q, 2 * q + 1):
                        m = product(o[:, (h % 2) * 256:(h % 2 + 1) * 256], both(wukvp, lambda x: x[:, h, 0, :]), ckvp)
                    m.then_inc(job_done.sem, 1)

                def mla_qn(q):
                    o = take("mla_qn", q)
                    for h in (2 * q, 2 * q + 1):
                        for k in range(3):
                            m = pe.matmul(o[:, (h % 2) * 256:(h % 2 + 1) * 256], wuq[:, k, h, 0:NOPE], cT[:, k, :],
                                          start=k == 0, stop=k == 2)
                    m.then_inc(job_done.sem, 1)

                def mla_v(i):
                    o = take("mla_v", i)
                    product(o.rearrange("p (h e) -> p h e", h=HEADS), both(ckvp, lambda x: x[:, i * P:(i + 1) * P]),
                            both(wukvp, lambda x: x[:, :, 1, :])).then_inc(job_done.sem, 1)

                def qrT_(_):
                    pe.wait_ge(qr_done.sem, qr_done.at(l, 1))
                    o = take("qrT", 0)
                    for g in range(2):
                        for i in range(NT):
                            m = turn(o[:, g * 256 + i * P:g * 256 + (i + 1) * P], qr[:, i, g * P:(g + 1) * P])
                    m.then_inc(job_done.sem, 1)

                def cellT(q):
                    pe.wait_ge(cell_done.sem, cell_done.at(l, 0))
                    o = take("cellT", q)
                    for h in (2 * q, 2 * q + 1):
                        for i in range(NT):
                            m = turn(o[:, (h % 2) * 256 + i * P:(h % 2) * 256 + (i + 1) * P],
                                     cell[:, i, h * HD:(h + 1) * HD])
                    m.then_inc(job_done.sem, 1)

                def mla_scores(h):
                    if h == 0:
                        wait_read(pe, l, ("mla_kn", 0), ("mla_kn", 1), ("mla_qn", 0), ("mla_qn", 1),
                                  ("kpeT", 0), ("qrT", 0))
                        stand_alone(pe)
                    o = take("mla_scores", h)
                    r = slice((h % 2) * ROT, (h % 2 + 1) * ROT)
                    for i, (c0, c1) in enumerate(((0, P), (P, TRI))):
                        q = slice(i * P, (i + 1) * P)
                        pe.matmul(o[:, c0:c1], qnT[:, h, q], knT[:, h, 0:c1 - c0], start=True, stop=False)
                        m = pe.matmul(o[:, c0:c1], qrT[r, h // 2, q], krT[r, 0:c1 - c0], start=False, stop=True)
                    m.then_inc(job_done.sem, 1)

                def mla_pT(h):
                    pe.wait_ge(prob_done.sem, prob_done.at(l, HEADS + h))
                    o = take("mla_pT", h)
                    for j in range(3):
                        m = turn(o[:, j * P:(j + 1) * P], prob[:, h % 2, j * P:(j + 1) * P])
                    m.then_inc(job_done.sem, 1)

                def mla_out(q):
                    wait_read(pe, l, ("mla_v", 0), ("mla_v", 1), ("mla_pT", 2 * q), ("mla_pT", 2 * q + 1))
                    stand_alone(pe)
                    o = take("mla_out", q)
                    for h in (2 * q, 2 * q + 1):
                        c = (h % 2) * 256
                        pe.matmul(o[:, c:c + 256], mlaV[:, 0, h * HD:(h + 1) * HD], probT[:, h % 2, 0:256],
                                  start=True, stop=False, skip_group_check=True)
                        m = pe.matmul(o[:, c + P:c + 256], mlaV[:, 1, h * HD:(h + 1) * HD], probT[:, h % 2, 256:TRI],
                                      start=False, stop=True, skip_group_check=True)
                    m.then_inc(job_done.sem, 1)

                def turn_heads(name, src):
                    def turned(i):
                        pe.wait_ge(roped.sem, roped.at(l, i + (2 if name == "rkT" else 0)))
                        o = take(name, i)
                        for h in range(HEADS):
                            m = turn(o[:, h * P:(h + 1) * P], src[:, i, h * HD:(h + 1) * HD])
                        m.then_inc(job_done.sem, 1)
                    return turned

                def ret_scores(h):
                    if h == 0:
                        wait_read(pe, l, ("rqT", 0), ("rqT", 1), ("rkT", 0), ("rkT", 1))
                        stand_alone(pe)
                    causal_scores(take("ret_scores", h), rkT, rqT, h).then_inc(job_done.sem, 1)

                def ret_out(q):
                    wait_acc_read(pe, l, CI["rv"])
                    wait_read(pe, l, ("ret_scores", 2 * q), ("ret_scores", 2 * q + 1))
                    o = take("ret_out", q)
                    for h in (2 * q, 2 * q + 1):
                        pt, c, v = probT[:, h % 2, :], (h % 2) * 256, slice(h * HD, (h + 1) * HD)
                        pe.matmul(o[:, c:c + P], pt[:, 0:P], rv[:, 0, v], start=True, stop=True)
                        pe.matmul(o[:, c + P:c + 256], pt[:, P:2 * P], rv[:, 0, v], start=True, stop=False)
                        m = pe.matmul(o[:, c + P:c + 256], pt[:, 2 * P:3 * P], rv[:, 1, v], start=False, stop=True)
                    m.then_inc(job_done.sem, 1)

                def retT_(q):
                    wait_read(pe, l, ("ret_out", q))
                    o = take("retT", q)
                    for h in (2 * q, 2 * q + 1):
                        for i in range(NT):
                            m = turn(o[:, (h % 2) * 256 + i * P:(h % 2) * 256 + (i + 1) * P],
                                     retn[:, i, h * HD:(h + 1) * HD])
                    m.then_inc(job_done.sem, 1)

                steps = {"xT": xT, "mem_scores": mem_scores, "mem_pT": mem_pT, "mem_out": mem_out,
                         "ml_q": ml_proj("ml_q", 0), "ml_k": ml_proj("ml_k", 1), "gateT": gateT,
                         "gate_cols": gate_cols, "cT": cT_, "kpeT": kpeT,
                         "ml_scores": ml_scores, "ml_out": ml_out, "mla_qr": mla_qr, "mla_kn": mla_kn,
                         "mla_qn": mla_qn, "mla_v": mla_v, "qrT": qrT_, "cellT": cellT,
                         "mla_scores": mla_scores, "mla_pT": mla_pT, "mla_out": mla_out,
                         "rqT": turn_heads("rqT", rqt), "rkT": turn_heads("rkT", rkt),
                         "ret_scores": ret_scores, "ret_out": ret_out, "retT": retT_}

                for t in range(SLOTS):
                    c, k = divmod(t, KT)
                    name, w, layout = CHUNKS[c]
                    s, p = t % RING, c % 2
                    ah, al = ((mh, ml) if c < 2 else (xh, xl) if c < OUT0 else (y_part(0, k // 2), y_part(1, k // 2)))
                    kk = k % 2 if c >= OUT0 else k
                    if k == 0:
                        pe.wait_ge(acc_read[p].sem, acc_read[p].at(l, (c // 2) * 2 - 1))
                    if c == 0 and k < KT // 2 and k % 2 == 0:
                        pe.wait_ge(mem_dve.sem, k // 2 + 1)
                    if c == 0 and k >= KT // 2 and k % 4 == 0:
                        pe.wait_ge(mem_pool.sem, k // 4 - 1)
                    if c == 2 and k % 2 == 0:
                        wait_read(pe, l, ("xT", k // 2))
                    if c == OUT0 and k % 2 == 0:
                        pe.wait_ge(y_lo.sem, y_lo.at(l, k // 2))
                    pe.wait_ge(hi_done.sem, hi_done.at(l, t))
                    if layout == "tok":
                        for i in range(NT):
                            o, q = acc[:, p, i, 0:w], slice(i * P, (i + 1) * P)
                            pe.matmul(o, ah[:, kk, q], hi[:, s, 0:w], start=k == 0, stop=False)
                            pe.matmul(o, al[:, kk, q], hi[:, s, 0:w], start=False, stop=False)
                        pe.wait_ge(lo_done.sem, lo_done.at(l, t))
                        for i in range(NT):
                            m = pe.matmul(acc[:, p, i, 0:w], ah[:, kk, i * P:(i + 1) * P], lo[:, s, 0:w],
                                          start=False, stop=k == KT - 1)
                    else:
                        for j in range(4):
                            o, q = acc[:, p, j // 2, (j % 2) * 256:(j % 2 + 1) * 256], slice(j * P, (j + 1) * P)
                            pe.matmul(o, hi[:, s, q], ah[:, kk, :], start=k == 0 and j % 2 == 0, stop=False,
                                      skip_group_check=True)
                            pe.matmul(o, hi[:, s, q], al[:, kk, :], start=False, stop=False, skip_group_check=True)
                        pe.wait_ge(lo_done.sem, lo_done.at(l, t))
                        for j in range(4):
                            o, q = acc[:, p, j // 2, (j % 2) * 256:(j % 2 + 1) * 256], slice(j * P, (j + 1) * P)
                            m = pe.matmul(o, lo[:, s, q], ah[:, kk, :], start=False, stop=k == KT - 1,
                                          skip_group_check=True)
                    m.then_inc(tile_used.sem, 1)
                    for step, *args in PE_AT.get(t, ()):
                        steps[step](*args)

        @block.vector
        def _(dve):
            for p in range(2):
                dve.sem_inc(acc_read[p].sem, 2)
            for b in range(NBANK):
                dve.sem_inc(bank_read[b].sem, 1)
            dve.sem_inc(lo_done.sem, 2 * RAW)
            dve.memset(half[:, :], -0.5).then_inc(ready.sem, 1)
            dve.memset(ln_shift[:, :], 0.0)
            dve.memset(ln_rstd[:, :], 1.0).then_inc(ln_done.sem, 1)

            links = [0]

            def link0(ins):
                ins.then_inc(dve_own.sem, 1)
                links[0] += 1
                dve.wait_ge(dve_own.sem, links[0])

            def take_lo(l, t):
                w, s = CHUNKS[t % SLOTS // KT][1], (t // 2) % RAW
                dve.wait_ge(hi_done.sem, hi_done.at(l, t))
                dve.wait_ge(tile_used.sem, tile_used.at(l, t - RING))
                dve.tensor_tensor(lo[:, t % RING, 0:w], raw[:, s, (t % 2) * w:(t % 2 + 1) * w],
                                  hi[:, t % RING, 0:w].bitcast(F32), ALU.subtract).then_inc(lo_done.sem, 1)

            for j in range(4):
                k, m2 = 2 * j, memT[j // 2][:, (j % 2) * 512:(j % 2 + 1) * 512].rearrange("p (k t) -> p k t", k=2)
                dve.wait_ge(memb_in[j // 2].sem, 16)
                link0(dve.tensor_copy(mh[:, k:k + 2, :], m2))
                dve.tensor_tensor(ml[:, k:k + 2, :], m2, mh[:, k:k + 2, :].bitcast(F32), ALU.subtract)\
                   .then_inc(mem_dve.sem, 1)
                for t in {1: (0, 1), 2: (2,), 3: (3,)}.get(j, ()):
                    take_lo(0, t)
            assert links[0] == DVE_LINKS_BEFORE, links

            with dve.Fori(0, DEPTH) as l:
                links = [0]

                def link(ins):
                    ins.then_inc(dve_own.sem, 1)
                    links[0] += 1
                    dve.wait_ge(dve_own.sem, dve_own.at(l, links[0] - 1))

                def angles_(n):
                    turns, magic = 1.0 / (2.0 * np.pi), 12582912.0
                    if n == 0:
                        dve.wait_ge(rotary_in.sem, 2 * 16)
                        link(dve.tensor_copy(rinv[:, 0, :], pos[:, :]))
                        for i in range(NT):
                            last = dve.tensor_scalar(turn1[:, i, :], freq[:, :], rinv[:, 0, i:i + 1], None, ALU.mult)
                        link(last)
                    if n == 1:
                        dve.tensor_scalar(whole[:, 0, :, :], turn1, turns, None, ALU.mult)
                        link(dve.tensor_scalar(whole[:, 1, :, :], turn1, turns, 0.25, ALU.mult, ALU.add))
                    if n in (2, 3):
                        link(dve.tensor_scalar(whole, whole, (magic, -magic)[n - 2], None, ALU.add))
                    if n in (4, 5, 6):
                        src = turn1.unsqueeze(1).to_broadcast([P, 2, NT, FR + FM]) if n == 4 else angle
                        link(dve.scalar_tensor_tensor(angle, whole, -two_pi_parts()[n - 4], src, ALU.mult, ALU.add))
                    if n == 7:
                        link(dve.tensor_scalar(angle[:, 1, :, :], angle[:, 1, :, :], 0.5 * np.pi, None, ALU.add))
                        dve.tensor_scalar(angle, angle, PI_IN, -PI_IN, ALU.min, ALU.max).then_inc(angles.sem, 1)

                def x_lo(j):
                    dve.wait_ge(x_hi.sem, x_hi.at(l, j))
                    dve.tensor_tensor(xl[:, 2 * j:2 * j + 2, :], bank(("xT", j)).rearrange("p (k t) -> p k t", k=2),
                                      xh[:, 2 * j:2 * j + 2, :].bitcast(F32), ALU.subtract)\
                       .then_inc(free_bank("xT", j), 1)

                def y_lo_(j):
                    k = OUT_ORDER[2 * j]
                    dve.wait_ge(y_hi.sem, y_hi.at(l, j))
                    dve.tensor_tensor(y_part(1, j), yT[:, k:k + 2, :], y_part(0, j).bitcast(F32),
                                      ALU.subtract).then_inc(y_lo.sem, 1)

                def memv(i):
                    wait_chunk(dve, l, CI["memv"])
                    src, part, rest, free = operand("memv", i)
                    link(dve.tensor_copy(part, src))
                    dve.tensor_tensor(rest, src, part.bitcast(F32), ALU.subtract).then_inc(free, 1)

                def lo_of(name, i):
                    dve.wait_ge(hi_part.sem, hi_part.at(l, HI_STEPS.index((name, i))))
                    if (name, i) == ("cq", 0):
                        dve.wait_ge(tables.sem, tables.at(l, 0))
                    src, part, rest, free = operand(name, i)
                    dve.tensor_tensor(rest, src, part.bitcast(F32), ALU.subtract).then_inc(free, 1)

                def mem_max(h):
                    wait_job(dve, l, ("mem_scores", h))
                    link(dve.tensor_reduce(nmax[:, h % 2, :], bank(("mem_scores", h)).rearrange("p (i k) -> p i k", i=NT),
                                           AX.X, ALU.max, negate=True))
                    dve.tensor_scalar(nmax[:, h % 2, :], nmax[:, h % 2, :], HEAD_SCALE, None, ALU.mult)\
                       .then_inc(max_done.sem, 1)

                def mem_norm(h):
                    wait_read(dve, l, ("mem_scores", h))
                    link(dve.reciprocal(rinv[:, h % 2, :], rsum[:, h % 2, :]))
                    for i in range(NT):
                        pr = prob[:, h % 2, i * 256:(i + 1) * 256]
                        m = dve.tensor_scalar(pr, pr, rinv[:, h % 2, i:i + 1], None, ALU.mult)
                    m.then_inc(prob_done.sem, 1)

                def out_pair(name, dst):
                    def evacuate(q):
                        wait_job(dve, l, (name, q))
                        dve.tensor_copy(dst[:, 2 * q:2 * q + 2, :], bank((name, q)).rearrange("p (j t) -> p j t", j=2))\
                           .then_inc(free_bank(name, q), 1)
                    return evacuate

                def conv(s):
                    if s == 0:
                        dve.wait_ge(cols_in.sem, cols_in.at(l, 0))
                        dve.memset(LX[:, :, 0:PAD], 0.0).then_inc(lx_pad.sem, 1)
                        dve.wait_ge(lx_pad.sem, lx_pad.at(l, 0))
                        wait_acc_read(dve, l, CI["lx"])
                    j, tap0 = divmod(s, 2)
                    for tap in (2 * tap0, 2 * tap0 + 1):
                        wcol = cols[:, C_CONVW + tap * 4 + j:C_CONVW + tap * 4 + j + 1]
                        if tap == 0:
                            link(dve.tensor_scalar(xcT[:, j, :], LX[:, j, 0:SEQ], wcol, None, ALU.mult))
                        else:
                            m = dve.scalar_tensor_tensor(xcT[:, j, :], LX[:, j, tap:tap + SEQ], wcol, xcT[:, j, :],
                                                         ALU.mult, ALU.add)
                            if (j, tap) == (3, 3):
                                m.then_inc(conv_done.sem, 1)
                            else:
                                link(m)

                def rms_(r):
                    dve.wait_ge(sq_done.sem, sq_done.at(l, r))
                    if r:
                        link(dve.tensor_tensor(sumsq[:, 1, :], sumsq[:, 1, :], sumsq[:, 2, :], ALU.add))
                    dve.tensor_scalar(sumsq[:, r, :], sumsq[:, r, :], 1.0 / (KVRANK, QRANK)[r], RMS_EPS,
                                      ALU.mult, ALU.add).then_inc(var_done.sem, 1)

                def ckv(_):
                    dve.wait_ge(rms_done.sem, rms_done.at(l, 0))
                    for i in range(NT):
                        dve.tensor_scalar(cqn[:, i, QRANK:QRANK + KVRANK], A("akv", i)[:, 0:KVRANK], rms[:, 0, i:i + 1],
                                          None, ALU.mult).then_inc(acc_sem("akv"), 1)

                def cqn_(i):
                    dve.wait_ge(rms_done.sem, rms_done.at(l, 1))
                    dve.tensor_scalar(cqn[:, i, 0:QHEAD], small[:, i, C_CQ:SMALL], rms[:, 1, i:i + 1], None, ALU.mult)
                    dve.tensor_scalar(cqn[:, i, QHEAD:QRANK], A("aq", i)[:, 0:QRANK - QHEAD], rms[:, 1, i:i + 1],
                                      None, ALU.mult).then_inc(acc_sem("aq"), 1)
                    if i:
                        wait_acc_read(dve, l, CI["aq"])
                        wait_acc_read(dve, l, CI["akv"])
                        dve.sem_inc(c_normed.sem, 2)

                def kpe_rope(_):
                    dve.wait_ge(tables.sem, tables.at(l, 0))
                    for i in range(NT):
                        src = small[:, i, 0:ROT].rearrange("p (a f) -> p a f", a=2)
                        t1 = tmp[:, i * P:i * P + ROT].rearrange("p (a f) -> p a f", a=2)
                        t2 = tmp[:, i * P + ROT:i * P + P].rearrange("p (a f) -> p a f", a=2)
                        dve.tensor_tensor(t1, src, cos[:, i, FR:].unsqueeze(1).to_broadcast([P, 2, FM]), ALU.mult)
                        link(dve.tensor_tensor(t2, src[:, ::-1, :], sin[:, :, i, FR:], ALU.mult))
                    for i in range(NT):
                        t1, t2 = tmp[:, i * P:i * P + ROT], tmp[:, i * P + ROT:i * P + P]
                        m = dve.tensor_tensor(krr[:, i, :].rearrange("p (d e) -> p d e", d=2),
                                              t1.unsqueeze(1).to_broadcast([P, 2, ROT]),
                                              t2.unsqueeze(1).to_broadcast([P, 2, ROT]), ALU.add)
                    m.then_inc(kpe_done.sem, 1)

                def gates(_):
                    wait_job(dve, l, ("gateT", 0), ("ml_k", 1))
                    dve.wait_ge(cols_in.sem, cols_in.at(l, 0))
                    o = bank(("gateT", 0))
                    dve.tensor_scalar(row[0], o[0:HEADS, 0:SEQ], cols[0:HEADS, C_IB:C_IB + 1], None, ALU.add)
                    link(dve.tensor_scalar(row[1], o[0:HEADS, SEQ:2 * SEQ], cols[0:HEADS, C_FB:C_FB + 1], None, ALU.add))
                    dve.sem_inc(free_bank("gateT", 0), 1)
                    dve.scalar_tensor_tensor(row[2], row[1], -1.0, row[1], ALU.mult, ALU.max).then_inc(gate_abs.sem, 1)

                def gate_scan(_):
                    link(dve.tensor_scalar(row[1], row[1], 0.0, None, ALU.min))
                    dve.wait_ge(softplus_done.sem, softplus_done.at(l, 0))
                    link(dve.tensor_tensor_scan(row[3], row[1], row[2], 0.0, ALU.add, ALU.subtract))
                    link(dve.tensor_tensor(row[0], row[0], row[3], ALU.subtract))
                    link(dve.tensor_tensor_scan(row[1], row[0], row[0], 0.0, ALU.max, ALU.max))
                    dve.tensor_tensor(row[3], row[3], row[1], ALU.add).then_inc(scan_done.sem, 1)

                def skip(_):
                    wait_job(dve, l, ("ml_k", 1))
                    for j in range(4):
                        m = dve.tensor_scalar(mls[:, j, :], xcT[:, j, :], cols[:, C_SKIP + j:C_SKIP + j + 1], None, ALU.mult)
                    m.then_inc(skip_done.sem, 1)

                def ones(_):
                    wait_job(dve, l, ("mem_scores", HEADS - 1))
                    dve.memset(lv1[:, :, :, HD:HD + 1], 1.0).then_inc(ones_done.sem, 1)

                def cT_(i):
                    wait_job(dve, l, ("cT", i))
                    dve.tensor_tensor(cT[:, :, i * P:(i + 1) * P], bank(("cT", i)).rearrange("p (j t) -> p j t", j=4),
                                      cols[:, C_CG:C_CG + 4].unsqueeze(2).to_broadcast([P, 4, P]), ALU.mult)\
                       .then_inc(free_bank("cT", i), 1)

                def gate_cols(_):
                    wait_job(dve, l, ("gate_cols", 0))
                    dve.tensor_copy(gcol[:, :, :], bank(("gate_cols", 0))[:, 0:4 * HEADS].rearrange("p (g h) -> p g h", g=4))\
                       .then_inc(free_bank("gate_cols", 0), 1)

                def ml_gap(h):
                    dve.wait_ge(mrow_in.sem, mrow_in.at(l, 0))
                    dve.wait_ge(const_in.sem, 16)
                    if h == 0:
                        wait_read(dve, l, ("gate_cols", 0))
                    if h >= 2:
                        wait_read(dve, l, ("ml_scores", h - 2))
                    o = mrow[:, h, :]
                    dve.scalar_tensor_tensor(gap[:, h % 2, 0:256], o, gcol[:, 0, h:h + 1], big[:, 0:256],
                                             ALU.subtract, ALU.max)
                    dve.scalar_tensor_tensor(gap[:, h % 2, 256:TRI], o[:, P:256], gcol[:, 1, h:h + 1], big[:, 256:TRI],
                                             ALU.subtract, ALU.max).then_inc(gap_done.sem, 1)

                def ml_weigh(h):
                    wait_job(dve, l, ("ml_scores", h), *([("ml_out", h - 2)] if h >= 2 else []))
                    dve.wait_ge(decay_done.sem, decay_done.at(l, h))
                    dve.scalar_tensor_tensor(probT[:, h % 2, 0:TRI], bank(("ml_scores", h))[:, 0:TRI], HEAD_SCALE,
                                             gap[:, h % 2, :], ALU.mult, ALU.mult).then_inc(free_bank("ml_scores", h), 1)

                def ml_out(h):
                    wait_job(dve, l, ("ml_out", h), ("ml_scores", HEADS - 1))
                    o = bank(("ml_out", h))[:, 0:NT * (HD + 1)].rearrange("p (i e) -> p i e", i=NT)
                    d = den[:, h % 2, :]
                    link(dve.scalar_tensor_tensor(d, o[:, :, HD], -1.0, gcol[:, 2:4, h], ALU.mult, ALU.max))
                    link(dve.tensor_tensor(d, o[:, :, HD], d, ALU.max))
                    link(dve.reciprocal(d, d))
                    for i in range(NT):
                        m = dve.tensor_scalar(cell[:, i, h * HD:(h + 1) * HD], o[:, i, 0:HD], den[:, h % 2, i:i + 1],
                                              None, ALU.mult)
                    m.then_inc(free_bank("ml_out", h), 1)

                def cell_gate(i):
                    wait_acc_read(dve, l, CI["lo"])
                    wait_read(dve, l, ("ml_out", HEADS - 1))
                    link(dve.tensor_tensor(cell[:, i, :], cell[:, i, :], sigo[:, i, :], ALU.mult))

                def cell_stats(i):
                    for h in range(HEADS):
                        m = dve.bn_stats(stats[:, i * HEADS + h, :], cell[:, i, h * HD:(h + 1) * HD])
                    link(m)
                    stand_alone(dve)
                    for h in range(HEADS):
                        m = dve.bn_aggr(mv[:, i * HEADS + h, :], stats[:, i * HEADS + h, :])
                    link(m)
                    if i:
                        dve.tensor_scalar(stats[:, :, 0], mv[:, :, 1], LN_EPS, None, ALU.add).then_inc(cell_var.sem, 1)

                def cell_norm(i):
                    dve.wait_ge(cell_pow.sem, cell_pow.at(l, 0))
                    for h in range(HEADS):
                        n, s = i * HEADS + h, cell[:, i, h * HD:(h + 1) * HD]
                        m = dve.tensor_scalar(s, s, mv[:, n, 0:1], rstd[:, n:n + 1], ALU.subtract, ALU.mult)
                    if i:
                        m.then_inc(cell_done.sem, 1)

                def cellT(q):
                    wait_job(dve, l, ("cellT", q))
                    dve.wait_ge(skip_done.sem, skip_done.at(l, 0))
                    for h in (2 * q, 2 * q + 1):
                        m = dve.scalar_tensor_tensor(mls[:, h, :], bank(("cellT", q))[:, (h % 2) * 256:(h % 2 + 1) * 256],
                                                     cols[:, C_MLG + h:C_MLG + h + 1], mls[:, h, :], ALU.mult, ALU.add)
                    m.then_inc(free_bank("cellT", q), 1)

                def rope(dst, src, cos, sin, halfw):
                    n = dst.shape[1] // (2 * halfw)
                    d = dst.rearrange("p (h a f) -> p h a f", h=n, a=2)
                    s = src.rearrange("p (h a f) -> p h a f", h=n, a=2)
                    t = tmp[:, 0:n * 2 * halfw].rearrange("p (h a f) -> p h a f", h=n, a=2)
                    dve.tensor_tensor(d, s, cos.unsqueeze(1).unsqueeze(1).to_broadcast([P, n, 2, halfw]), ALU.mult)
                    return dve.tensor_tensor(t, s[:, :, ::-1, :], sin.unsqueeze(1).to_broadcast([P, n, 2, halfw]), ALU.mult)

                def q_rope(i):
                    wait_job(dve, l, ("mla_qr", i))
                    link(rope(qr[:, i, :], bank(("mla_qr", i))[:, 0:HEADS * ROT], cos[:, i, FR:], sin[:, :, i, FR:], FM))
                    dve.sem_inc(free_bank("mla_qr", i), 1)
                    dve.tensor_tensor(qr[:, i, :], qr[:, i, :], tmp[:, 0:HEADS * ROT], ALU.add).then_inc(qr_done.sem, 1)
                    dve.wait_ge(qr_done.sem, qr_done.at(l, i))

                def rope_ret(name, dst, n):
                    def go(i):
                        wait_chunk(dve, l, CI[name])
                        if name == "rq" and i == 0:
                            wait_job(dve, l, ("mla_qn", 1))
                        rope(dst[:, i, :], A(name, i), cos[:, i, 0:FR], sin[:, :, i, 0:FR], FR).then_inc(acc_sem(name), 1)
                        wait_acc_read(dve, l, CI[name], halves=i + 1)
                        dve.tensor_tensor(dst[:, i, :], dst[:, i, :], tmp[:, :], ALU.add).then_inc(roped.sem, 1)
                        dve.wait_ge(roped.sem, roped.at(l, n + i))
                    return go

                def mla_max(h):
                    wait_job(dve, l, ("mla_scores", h), *([("mla_pT", h - 2)] if h >= 2 else []))
                    dve.tensor_tensor(prob[:, h % 2, 0:TRI], bank(("mla_scores", h))[:, 0:TRI], tri, ALU.add)\
                       .then_inc(free_bank("mla_scores", h), 1)
                    wait_read(dve, l, ("mla_scores", h))
                    dve.tensor_reduce(nmax[:, h % 2, 0:1], prob[:, h % 2, 0:P], AX.X, ALU.max, negate=True)
                    link(dve.tensor_reduce(nmax[:, h % 2, 1:2], prob[:, h % 2, P:TRI], AX.X, ALU.max, negate=True))
                    dve.tensor_scalar(nmax[:, h % 2, :], nmax[:, h % 2, :], MLA_SCALE, None, ALU.mult)\
                       .then_inc(max_done.sem, 1)

                def mla_norm(h):
                    dve.wait_ge(exp_done.sem, exp_done.at(l, h))
                    link(dve.reciprocal(rinv[:, h % 2, :], rsum[:, h % 2, :]))
                    for i, (c0, c1) in enumerate(((0, P), (P, TRI))):
                        pr = prob[:, h % 2, c0:c1]
                        m = dve.tensor_scalar(pr, pr, rinv[:, h % 2, i:i + 1], None, ALU.mult)
                    m.then_inc(prob_done.sem, 1)

                def ret_weigh(h):
                    wait_job(dve, l, ("ret_scores", h), ("ret_out", 0) if h >= 2 else ("mla_out", 1))
                    dve.tensor_tensor(probT[:, h % 2, 0:TRI], bank(("ret_scores", h))[:, 0:TRI], decay[:, h, :],
                                      ALU.mult).then_inc(free_bank("ret_scores", h), 1)

                def ret_block(q, n):
                    return bank(("ret_out", q))[:, n * HD:(n + 1) * HD]

                def ret_stats(q):
                    wait_job(dve, l, ("ret_out", q))
                    for n in range(4):
                        m = dve.bn_stats(stats[:, n, :], ret_block(q, n))
                    link(m)
                    stand_alone(dve)
                    for n in range(4):
                        m = dve.bn_aggr(mv[:, n, :], stats[:, n, :])
                    link(m)
                    dve.tensor_scalar(stats[:, 0:4, 0], mv[:, 0:4, 1], LN_EPS, None, ALU.add).then_inc(ret_var.sem, 1)

                def ret_norm(q):
                    dve.wait_ge(ret_pow.sem, ret_pow.at(l, q))
                    for n in range(4):
                        h, i = 2 * q + n // 2, n % 2
                        m = dve.tensor_scalar(retn[:, i, h * HD:(h + 1) * HD], ret_block(q, n), mv[:, n, 0:1],
                                              rstd[:, n:n + 1], ALU.subtract, ALU.mult)
                    m.then_inc(free_bank("ret_out", q), 1)

                def retT_(q):
                    wait_job(dve, l, ("retT", q))
                    for h in (2 * q, 2 * q + 1):
                        m = dve.tensor_scalar(retT[:, h, :], bank(("retT", q))[:, (h % 2) * 256:(h % 2 + 1) * 256],
                                              cols[:, C_RETG + h:C_RETG + h + 1], None, ALU.mult)
                    m.then_inc(free_bank("retT", q), 1)

                def gate(g, i):
                    src = {3: memo, 2: mls, 1: mlao, 0: retT}[g]
                    last = {3: "mem_out", 2: "cellT", 1: "mla_out", 0: "retT"}[g]
                    wait_acc_read(dve, l, CI[f"z{g}"], halves=i + 1)
                    wait_read(dve, l, (last, 1))
                    y = yT[:, 4 * g + 2 * i:4 * g + 2 * i + 2, :]
                    dve.tensor_tensor(y, y, src[:, 2 * i:2 * i + 2, :], ALU.mult).then_inc(gated.sem, 1)

                def residual(c):
                    name, w = CHUNKS[OUT0 + c][0], CHUNKS[OUT0 + c][1]
                    wait_chunk(dve, l, OUT0 + c)
                    for i in range(NT):
                        xc = X[:, i, OUTCOL[c]:OUTCOL[c] + w]
                        dve.scalar_tensor_tensor(xc, xc, ALPHA, A(name, i)[:, 0:w], ALU.mult, ALU.add)\
                           .then_inc(acc_sem(name), 1)
                    for i in range(NT):
                        wait_acc_read(dve, l, OUT0 + c, halves=i + 1)
                        m = dve.bn_stats(ln_stats[:, i, c, :], X[:, i, OUTCOL[c]:OUTCOL[c] + w])
                    return m

                steps = {"angles": angles_, "lo": lo_of, "x_lo": x_lo, "y_lo": y_lo_, "memv": memv, "mem_max": mem_max, "mem_norm": mem_norm,
                         "mem_out": out_pair("mem_out", memo), "conv": conv, "rms": rms_, "ckv": ckv, "cqn": cqn_,
                         "kpe_rope": kpe_rope, "gates": gates, "gate_scan": gate_scan, "skip": skip, "ones": ones,
                         "cT": cT_, "gate_cols": gate_cols, "ml_gap": ml_gap, "ml_weigh": ml_weigh, "ml_out": ml_out,
                         "cell_gate": cell_gate, "cell_stats": cell_stats, "cell_norm": cell_norm, "cellT": cellT,
                         "q_rope": q_rope, "rope_rq": rope_ret("rq", rqt, 0), "rope_rk": rope_ret("rk", rkt, 2),
                         "mla_max": mla_max, "mla_norm": mla_norm, "mla_out": out_pair("mla_out", mlao),
                         "ret_weigh": ret_weigh, "ret_stats": ret_stats, "ret_norm": ret_norm, "retT": retT_,
                         "gate": gate, "residual": residual}
                for t in range(AHEAD, SLOTS + AHEAD):
                    take_lo(l, t)
                    for name, *args in DVE_AT.get(t, ()):
                        steps[name](*args)

                link(residual(NOUT - 1))
                stand_alone(dve)
                for i in range(NT):
                    m = dve.bn_aggr(ln_mv[:, i, :], ln_stats[:, i, :, :].rearrange("p c s -> p (c s)"))
                link(m)
                dve.tensor_scalar(ln_stats[:, :, 0, 0], ln_mv[:, :, 1], LN_EPS, None, ALU.add).then_inc(ln_var.sem, 1)
                dve.tensor_scalar(ln_nmu[:, :], ln_mv[:, :, 0], -1.0, None, ALU.mult).then_inc(ln_mean.sem, 1)
                assert links[0] == DVE_LINKS, links

            dve.wait_ge(gb_in.sem, gb_in.at(DEPTH - 1, 0))
            dve.wait_ge(ln_mean.sem, ln_mean.at(DEPTH - 1, 0))
            for b in range(8):
                cb, i = divmod(b, 2)
                blk = X[:, i, cb * 512:(cb + 1) * 512]
                dve.scalar_tensor_tensor(blk, blk, ln_nmu[:, i:i + 1], gb[:, 0, cb * 512:(cb + 1) * 512],
                                         ALU.add, ALU.mult).then_inc(final_gained.sem, 1)
            dve.wait_ge(ln_pow.sem, ln_pow.at(DEPTH - 1, 0))
            for b in DVE_BIAS:
                cb, i = divmod(b, 2)
                blk = X[:, i, cb * 512:(cb + 1) * 512]
                dve.wait_ge(final_gained.sem, b + 1)
                dve.scalar_tensor_tensor(blk, blk, ln_rstd[:, i:i + 1], gb[:, 1, cb * 512:(cb + 1) * 512],
                                         ALU.mult, ALU.add).then_inc(dve_biased.sem, 1)


def stream_columns(name):
    r = lambda at, n: list(range(at, at + n))
    if name == "memk":
        return r(0, W)
    if name == "memv":
        return r(W, W)
    if name == "akv":
        return r(COL["akv"], KVRANK + ROT) + r(COL["li"], 2 * HEADS) + r(COL["aq"], QHEAD)
    if name == "aq":
        return r(COL["aq"] + QHEAD, QRANK - QHEAD)
    if name[0] == "z":
        return r(COL["z"] + int(name[1:]) * W, W)
    if name[:3] == "out":
        c = int(name[3:])
        return r(OUTCOL[c], CHUNKS[OUT0 + c][1])
    return r(COL[name], W)


def constants():
    f = np.float64
    k, q = np.arange(P)[:, None], np.arange(SEQ)[None, :]
    rel = q - k
    rel = np.concatenate([rel, rel[:, :P]], 1)
    gamma = 1.0 - 2.0 ** (-5.0 - np.arange(HEADS, dtype=f))
    dec = np.where(rel[None] >= 0, gamma[:, None, None] ** np.maximum(rel, 0)[None], 0.0) * HEAD_SCALE
    dec = dec.transpose(1, 0, 2).reshape(P, HEADS * TRI)
    big = np.where(rel >= 0, 0.0, MASKED)
    above = np.where(np.arange(P)[None, :] <= np.arange(P)[:, None], 0.0, -MASKED)
    tri = np.concatenate([above, np.zeros((P, P)), above], 1)
    freqs = np.concatenate([THETA ** (-np.arange(n, dtype=f) / n) for n in (FR, FM)])
    blocks = {"ident": np.eye(P), "const": np.concatenate([dec, tri, big], 1), "freq": np.tile(freqs, (P, 1))}
    return {name: v.astype(np.float32) for name, v in blocks.items()}


def kernel(**inputs):
    import concourse.bacc as _bacc
    from concourse.bass_utils import run_bass_kernel_spmd as _run

    g = {k: np.asarray(v) for k, v in inputs.items()}

    def stream(l):
        parts = []
        for name, w, _ in CHUNKS:
            m = g["w_mem_kv"] if name[:3] == "mem" else g["w_out"] if name[:3] == "out" else g["w_in"]
            order = OUT_ORDER if name[:3] == "out" else range(KT)
            t = m[l][:, stream_columns(name)].reshape(KT, P, w)[list(order)]
            parts.append(t.reshape(KT // 2, 2, P, w).transpose(0, 2, 1, 3).reshape(-1))
        return np.concatenate(parts)

    def columns(l):
        col = lambda v: v.reshape(-1, P).T
        bias = lambda v: np.concatenate([v, np.zeros(P - HEADS, v.dtype)])[:, None]
        return np.concatenate([col(g["ret_norm_g"][l]), col(g["mla_q_norm_g"][l]), col(g["mla_kv_norm_g"][l]),
                               col(g["ml_conv_w"][l].reshape(-1)), col(g["ml_conv_b"][l]), col(g["ml_skip"][l]),
                               col(g["ml_norm_g"][l]), bias(g["ml_i_bias"][l]), bias(g["ml_f_bias"][l])], 1).reshape(-1)

    arrays = {
        "x": g["x"].reshape(SEQ, D_MODEL),
        "pos": np.ascontiguousarray(g["positions"].reshape(NT, P).T),
        "mem_t": np.ascontiguousarray(g["mem"][0].T.reshape(KT, P, MEM_LEN).transpose(1, 0, 2).reshape(P, -1)),
        "w": np.stack([stream(l) for l in range(DEPTH)]),
        "cols": np.stack([columns(l) for l in range(DEPTH)]),
        "lw": np.stack([np.stack([g["ml_w_q"][l], g["ml_w_k"][l]]).transpose(2, 0, 1, 3).reshape(-1) for l in range(DEPTH)]),
        "wuq": np.stack([g["mla_w_uq"][l].reshape(3, P, -1).transpose(1, 0, 2).reshape(-1) for l in range(DEPTH)]),
        "wukv": np.stack([g["mla_w_ukv"][l].reshape(-1) for l in range(DEPTH)]),
        "gb": np.concatenate([g["ln_g"], g["ln_b"]], 1),
        **constants(),
    }
    nc = _bacc.Bacc("TRN2", target_bir_lowering=False, num_devices=1)
    maps, args = {}, {}
    for name, v in arrays.items():
        v = np.ascontiguousarray(v)
        maps[f"in_{name}"] = v
        args[name] = nc.dram_tensor(f"in_{name}", v.shape, mybir.dt.from_np(v.dtype), kind="ExternalInput").ap()
    args["mrow"] = nc.dram_tensor("mrow", (HEADS, SEQ), F32, kind="Internal").ap()
    out = nc.dram_tensor("out_x", (SEQ, D_MODEL), F32, kind="ExternalOutput").ap()
    build_trunk(nc, args, out)
    r = _run(nc, [maps], core_ids=[0])
    return r.results[0]["out_x"].reshape(1, SEQ, D_MODEL)
```
